# Optimizing a Trainium2 kernel written in Bass

```python
import math
import jax, jax.numpy as jnp
from jax import lax
import numpy as np

D_MODEL = 1024
BATCH = 1
SEQ = 256
DEPTH = 2

D_MIX = D_MODEL
GROUP = D_MIX // 4
HEAD_DIM = 64
N_HEADS_GROUP = GROUP // HEAD_DIM
CHUNK = 64
CONV_K = 4
LRU_BLOCKS = 4
LRU_BLOCK = GROUP // LRU_BLOCKS
LRU_C = 8.0
RWKV_W_LORA = 64
RWKV_A_LORA = 64
RWKV_G_LORA = 128
RWKV_V_LORA = 32
RWKV_GN_EPS = 64e-5
MEM_LEN = 256
XATTN_HEADS = 4
XATTN_HEAD_DIM = D_MODEL // XATTN_HEADS
D_FF = 2816
N_EXPERTS = 8
TOP_K = 2
D_FF_EXPERT = 3584
EPS = 1e-6

HG_COLS = 4 * GROUP
GDN_COLS = 4 * GROUP + 2 * N_HEADS_GROUP
LRU_COLS = 2 * GROUP
RWKV_COLS = 3 * GROUP + RWKV_W_LORA + RWKV_A_LORA + RWKV_G_LORA
N_IN = HG_COLS + GDN_COLS + LRU_COLS + RWKV_COLS

kernel_name = "hybrid_parallel_heads_trunk"

def rmsnorm(x, g):
    xf = x.astype(jnp.float32)
    y = xf * lax.rsqrt(jnp.mean(xf * xf, axis=-1, keepdims=True) + EPS)
    return (y * g.astype(jnp.float32)).astype(x.dtype)

def l2norm(x):
    xf = x.astype(jnp.float32)
    return xf * lax.rsqrt(jnp.sum(xf * xf, axis=-1, keepdims=True) + EPS)

def split_cols(t, sizes):
    return jnp.split(t, [int(o) for o in np.cumsum(sizes)[:-1]], axis=-1)

def causal_dwconv(x, w, b=None):
    y = lax.conv_general_dilated(x, w[:, None, :], window_strides=(1,), padding=[(w.shape[0] - 1, 0)],
                                 dimension_numbers=("NWC", "WIO", "NWC"), feature_group_count=x.shape[-1])
    return y if b is None else y + b

def to_heads(t):
    return t.reshape(t.shape[0], t.shape[1], -1, HEAD_DIM).transpose(0, 2, 1, 3)

def chunk_gla(q, k, v, log_f):
    B, H, S, dk = q.shape
    dv = v.shape[-1]
    n = S // CHUNK

    def chunks(t):
        return jnp.moveaxis(t.reshape(B, H, n, CHUNK, t.shape[-1]), 2, 0)

    qc, kc, vc = chunks(q), chunks(k), chunks(v)
    bc = jnp.cumsum(chunks(log_f), axis=3)
    causal = jnp.tril(jnp.ones((CHUNK, CHUNK), bool))

    def step(state, inp):
        qi, ki, vi, bi = inp
        o_inter = jnp.einsum("bhtd,bhde->bhte", qi * jnp.exp(bi), state)
        rel = jnp.exp(jnp.where(causal[:, :, None], bi[:, :, :, None, :] - bi[:, :, None, :, :], -jnp.inf))
        scores = jnp.einsum("bhtd,bhsd,bhtsd->bhts", qi, ki, rel)
        o = o_inter + jnp.einsum("bhts,bhse->bhte", scores, vi)
        b_last = bi[:, :, -1:, :]
        state = jnp.exp(b_last[:, :, 0, :, None]) * state + jnp.einsum("bhsd,bhse->bhde", ki * jnp.exp(b_last - bi), vi)
        return state, o

    state0 = jnp.zeros((B, H, dk, dv), jnp.float32)
    _, o = lax.scan(step, state0, (qc, kc, vc, bc))
    return jnp.moveaxis(o, 0, 2).reshape(B, H, S, dv)

def hgrn2_mixer(q, f_logit, i, g, lb, norm_g):
    B, S, _ = q.shape
    f32 = jnp.float32
    fl = f_logit.astype(f32)
    lb = lb.astype(f32)
    log_f = jnp.logaddexp(jnp.log(lb), jnp.log1p(-lb) + jax.nn.log_sigmoid(fl))
    k = (1.0 - lb) * jax.nn.sigmoid(-fl)
    o = chunk_gla(to_heads(q.astype(f32)), to_heads(k), to_heads(i.astype(f32)), to_heads(log_f))
    o = rmsnorm(o.transpose(0, 2, 1, 3), norm_g.reshape(N_HEADS_GROUP, HEAD_DIM))
    return (o.reshape(B, S, GROUP) * jax.nn.silu(g.astype(f32))).astype(q.dtype)

def chunk_gated_delta(q, k, v, g, beta):
    B, H, S, dk = q.shape
    dv = v.shape[-1]
    n = S // CHUNK
    f32 = jnp.float32

    def chunks(t):
        return t.reshape(B, H, n, CHUNK, *t.shape[3:])

    qc, kc, vc, bc = chunks(q), chunks(k), chunks(v), chunks(beta)
    gc = jnp.cumsum(chunks(g), axis=-1)
    causal = jnp.tril(jnp.ones((CHUNK, CHUNK), bool))
    strict = jnp.tril(jnp.ones((CHUNK, CHUNK), f32), -1)
    rel = jnp.exp(jnp.where(causal, gc[..., :, None] - gc[..., None, :], -jnp.inf))
    kb = kc * bc[..., None]
    lower = jnp.einsum("bhntd,bhnsd->bhnts", kb, kc) * rel * strict
    rhs = jnp.concatenate([vc * bc[..., None], kb * jnp.exp(gc)[..., None]], axis=-1)
    uw = lax.linalg.triangular_solve(jnp.eye(CHUNK, dtype=f32) + lower, rhs,
                                     left_side=True, lower=True, unit_diagonal=True)
    u, w = uw[..., :dv], uw[..., dv:]
    scores = jnp.einsum("bhntd,bhnsd->bhnts", qc, kc) * rel

    def step(state, inp):
        qi, ki, ui, wi, gi, si = inp
        v_new = ui - jnp.einsum("bhtd,bhde->bhte", wi, state)
        o = (jnp.einsum("bhtd,bhde->bhte", qi * jnp.exp(gi)[..., None], state)
             + jnp.einsum("bhts,bhse->bhte", si, v_new))
        g_last = gi[..., -1:]
        state = (jnp.exp(g_last)[..., None] * state
                 + jnp.einsum("bhsd,bhse->bhde", ki * jnp.exp(g_last - gi)[..., None], v_new))
        return state, o

    xs = tuple(jnp.moveaxis(t, 2, 0) for t in (qc, kc, u, w, gc, scores))
    _, o = lax.scan(step, jnp.zeros((B, H, dk, dv), f32), xs)
    return jnp.moveaxis(o, 0, 2).reshape(B, H, S, dv)

def gated_deltanet_mixer(qkv, z, alpha, beta_logit, conv_w, A_log, dt_bias, norm_g):
    B, S, _ = qkv.shape
    f32 = jnp.float32
    qkv = jax.nn.silu(causal_dwconv(qkv, conv_w)).astype(f32)
    q, k, v = jnp.split(qkv, 3, axis=-1)
    q = l2norm(to_heads(q)) * HEAD_DIM ** -0.5
    k = l2norm(to_heads(k))
    v = to_heads(v)
    g = -jnp.exp(A_log.astype(f32)) * jax.nn.softplus(alpha.astype(f32) + dt_bias.astype(f32))
    beta = jax.nn.sigmoid(beta_logit.astype(f32))
    o = chunk_gated_delta(q, k, v, g.transpose(0, 2, 1), beta.transpose(0, 2, 1))
    o = rmsnorm(o.transpose(0, 2, 1, 3), norm_g)
    return (o.reshape(B, S, GROUP) * jax.nn.silu(z.astype(f32))).astype(z.dtype)

def rglru_mixer(xb, gate, conv_w, conv_b, wa, ba, wx, bx, lam):
    B, S, _ = xb.shape
    f32 = jnp.float32
    xc = causal_dwconv(xb, conv_w, conv_b).astype(f32)
    xblk = xc.reshape(B, S, LRU_BLOCKS, LRU_BLOCK)
    r = jax.nn.sigmoid(jnp.einsum("bsni,nij->bsnj", xblk, wa.astype(f32)).reshape(B, S, GROUP) + ba)
    i = jax.nn.sigmoid(jnp.einsum("bsni,nij->bsnj", xblk, wx.astype(f32)).reshape(B, S, GROUP) + bx)
    log_a = -LRU_C * r * jax.nn.softplus(-lam.astype(f32))
    a = jnp.exp(log_a)
    u = jnp.sqrt(-jnp.expm1(2.0 * log_a)) * (i * xc)

    def combine(left, right):
        a_l, h_l = left
        a_r, h_r = right
        return a_l * a_r, a_r * h_l + h_r

    _, h = lax.associative_scan(combine, (a, u), axis=1)
    return (h * jax.nn.gelu(gate.astype(f32))).astype(xb.dtype)

def rwkv7_scan(r, w, k, v, kk, a):
    B, S, H, d = r.shape

    def step(state, inp):
        r_t, w_t, k_t, v_t, kk_t, a_t = inp
        sa = jnp.einsum("bhvk,bhk->bhv", state, kk_t)
        state = (state * w_t[:, :, None, :] - sa[..., None] * (kk_t * a_t)[:, :, None, :]
                 + v_t[..., None] * k_t[:, :, None, :])
        return state, jnp.einsum("bhvk,bhk->bhv", state, r_t)

    xs = tuple(jnp.moveaxis(t, 1, 0) for t in (r, w, k, v, kk, a))
    _, y = lax.scan(step, jnp.zeros((B, H, d, d), jnp.float32), xs)
    return jnp.moveaxis(y, 0, 1)

def rwkv7_mixer(cols, mu, w0, w2, a0, a2, g2, k_k, k_a, r_k, ln_w, ln_b, v_first, v_mix):
    B, S, _ = cols.shape
    f32 = jnp.float32
    c = cols.astype(f32)
    prev = jnp.pad(c, ((0, 0), (1, 0), (0, 0)))[:, :-1]
    c = c + mu * (prev - c)
    r, k, v, w_lo, a_lo, g_lo = split_cols(c, (GROUP, GROUP, GROUP, RWKV_W_LORA, RWKV_A_LORA, RWKV_G_LORA))
    w = jnp.exp(-math.exp(-0.5) * jax.nn.sigmoid(w0 + jnp.tanh(w_lo) @ w2))
    a = jax.nn.sigmoid(a0 + a_lo @ a2)
    g = jax.nn.sigmoid(g_lo) @ g2
    if v_mix is None:
        v_first = v
    else:
        v0, v1, v2 = v_mix
        v = v + (v_first - v) * jax.nn.sigmoid(v0 + (v @ v1) @ v2)
    heads = lambda t: t.reshape(B, S, N_HEADS_GROUP, HEAD_DIM)
    kk = l2norm(heads(k * k_k))
    k = k * (1.0 + (a - 1.0) * k_a)
    y = rwkv7_scan(heads(r), heads(w), heads(k), heads(v), kk, heads(a))
    mean = jnp.mean(y, axis=-1, keepdims=True)
    var = jnp.mean(jnp.square(y - mean), axis=-1, keepdims=True)
    y = ((y - mean) * lax.rsqrt(var + RWKV_GN_EPS)).reshape(B, S, GROUP) * ln_w + ln_b
    r_k_h = r_k.astype(f32).reshape(N_HEADS_GROUP, HEAD_DIM)
    bonus = jnp.sum(heads(r) * heads(k) * r_k_h, axis=-1, keepdims=True) * heads(v)
    y = (y + bonus.reshape(B, S, GROUP)) * g
    return y.astype(cols.dtype), v_first

def memory_cross_attention(h, mem_n, wq, wk, wv, wo):
    B, S, _ = h.shape
    M = mem_n.shape[1]
    q = (h @ wq).reshape(B, S, XATTN_HEADS, XATTN_HEAD_DIM)
    k = (mem_n @ wk).reshape(B, M, XATTN_HEADS, XATTN_HEAD_DIM)
    v = (mem_n @ wv).reshape(B, M, XATTN_HEADS, XATTN_HEAD_DIM)
    s = jnp.einsum("bshd,bmhd->bhsm", q, k).astype(jnp.float32) * XATTN_HEAD_DIM ** -0.5
    p = jax.nn.softmax(s, axis=-1).astype(h.dtype)
    o = jnp.einsum("bhsm,bmhd->bshd", p, v).reshape(B, S, D_MODEL)
    return o @ wo

def swiglu(h, wg, wu, wd):
    return (jax.nn.silu(h @ wg) * (h @ wu)) @ wd

def moe_swiglu(h, router, wg, wu, wd):
    logits = (h @ router).astype(jnp.float32)
    top_v, top_i = lax.top_k(logits, TOP_K)
    gates = jax.nn.softmax(top_v, axis=-1)
    combine = jnp.sum(jax.nn.one_hot(top_i, N_EXPERTS, dtype=jnp.float32) * gates[..., None], axis=-2)
    out = jnp.zeros_like(h)
    for e in range(N_EXPERTS):
        out = out + combine[..., e:e + 1].astype(h.dtype) * swiglu(h, wg[e], wu[e], wd[e])
    return out

def setup_inputs(seed: int = 0) -> dict:
    key = jax.random.key(seed)
    ks = iter(jax.random.split(key, 64))
    f32 = jnp.float32

    def nrm(shape, scale):
        return scale * jax.random.normal(next(ks), shape, f32)

    def gain(shape):
        return 1.0 + 0.02 * jax.random.normal(next(ks), shape, f32)

    def unif(shape, lo, hi):
        return jax.random.uniform(next(ks), shape, f32, minval=lo, maxval=hi)

    H = N_HEADS_GROUP
    n_dense = (DEPTH + 1) // 2
    n_moe = DEPTH // 2
    n_vres = DEPTH - 1
    dt = jnp.exp(unif((DEPTH, H), math.log(1e-3), math.log(1e-1)))
    lru_a = unif((DEPTH, GROUP), 0.9, 0.999)
    return {
        "x": nrm((BATCH, SEQ, D_MODEL), 1.0),
        "mem": nrm((BATCH, MEM_LEN, D_MODEL), 1.0),
        "norm_mix": gain((DEPTH, D_MODEL)),
        "w_in": nrm((DEPTH, D_MODEL, N_IN), D_MODEL ** -0.5),
        "w_out": nrm((DEPTH, D_MIX, D_MODEL), D_MIX ** -0.5),
        "hgrn_lb_logits": nrm((DEPTH, GROUP), 0.5),
        "hgrn_norm": gain((DEPTH, GROUP)),
        "gdn_conv_w": nrm((DEPTH, CONV_K, 3 * GROUP), CONV_K ** -0.5),
        "gdn_A_log": jnp.log(unif((DEPTH, H), 1.0, 16.0)),
        "gdn_dt_bias": dt + jnp.log(-jnp.expm1(-dt)),
        "gdn_norm": gain((DEPTH, HEAD_DIM)),
        "lru_conv_w": nrm((DEPTH, CONV_K, GROUP), CONV_K ** -0.5),
        "lru_conv_b": nrm((DEPTH, GROUP), 0.02),
        "lru_wa": nrm((DEPTH, LRU_BLOCKS, LRU_BLOCK, LRU_BLOCK), LRU_BLOCK ** -0.5),
        "lru_ba": nrm((DEPTH, GROUP), 0.02),
        "lru_wx": nrm((DEPTH, LRU_BLOCKS, LRU_BLOCK, LRU_BLOCK), LRU_BLOCK ** -0.5),
        "lru_bx": nrm((DEPTH, GROUP), 0.02),
        "lru_lambda": jnp.log(lru_a) - jnp.log1p(-lru_a),
        "rwkv_mu": unif((DEPTH, RWKV_COLS), 0.0, 1.0),
        "rwkv_w0": nrm((DEPTH, GROUP), 0.5),
        "rwkv_w2": nrm((DEPTH, RWKV_W_LORA, GROUP), RWKV_W_LORA ** -0.5),
        "rwkv_a0": nrm((DEPTH, GROUP), 0.1),
        "rwkv_a2": nrm((DEPTH, RWKV_A_LORA, GROUP), RWKV_A_LORA ** -0.5),
        "rwkv_g2": nrm((DEPTH, RWKV_G_LORA, GROUP), RWKV_G_LORA ** -0.5),
        "rwkv_k_k": 0.85 + 0.05 * jax.random.normal(next(ks), (DEPTH, GROUP), f32),
        "rwkv_k_a": gain((DEPTH, GROUP)),
        "rwkv_r_k": nrm((DEPTH, GROUP), 0.1),
        "rwkv_ln_w": gain((DEPTH, GROUP)),
        "rwkv_ln_b": nrm((DEPTH, GROUP), 0.02),
        "rwkv_v0": nrm((n_vres, GROUP), 0.1),
        "rwkv_v1": nrm((n_vres, GROUP, RWKV_V_LORA), GROUP ** -0.5),
        "rwkv_v2": nrm((n_vres, RWKV_V_LORA, GROUP), RWKV_V_LORA ** -0.5),
        "mem_norm": gain((D_MODEL,)),
        "norm_xattn": gain((DEPTH, D_MODEL)),
        "xattn_wq": nrm((DEPTH, D_MODEL, D_MODEL), D_MODEL ** -0.5),
        "xattn_wk": nrm((DEPTH, D_MODEL, D_MODEL), D_MODEL ** -0.5),
        "xattn_wv": nrm((DEPTH, D_MODEL, D_MODEL), D_MODEL ** -0.5),
        "xattn_wo": nrm((DEPTH, D_MODEL, D_MODEL), D_MODEL ** -0.5),
        "norm_ffn": gain((DEPTH, D_MODEL)),
        "ffn_w_gate": nrm((n_dense, D_MODEL, D_FF), D_MODEL ** -0.5),
        "ffn_w_up": nrm((n_dense, D_MODEL, D_FF), D_MODEL ** -0.5),
        "ffn_w_down": nrm((n_dense, D_FF, D_MODEL), D_FF ** -0.5),
        "moe_router": nrm((n_moe, D_MODEL, N_EXPERTS), D_MODEL ** -0.5),
        "moe_w_gate": nrm((n_moe, N_EXPERTS, D_MODEL, D_FF_EXPERT), D_MODEL ** -0.5),
        "moe_w_up": nrm((n_moe, N_EXPERTS, D_MODEL, D_FF_EXPERT), D_MODEL ** -0.5),
        "moe_w_down": nrm((n_moe, N_EXPERTS, D_FF_EXPERT, D_MODEL), D_FF_EXPERT ** -0.5),
        "norm_final": gain((D_MODEL,)),
    }

def reference(x, mem, norm_mix, w_in, w_out, hgrn_lb_logits, hgrn_norm, gdn_conv_w, gdn_A_log, gdn_dt_bias,
              gdn_norm, lru_conv_w, lru_conv_b, lru_wa, lru_ba, lru_wx, lru_bx, lru_lambda, rwkv_mu, rwkv_w0,
              rwkv_w2, rwkv_a0, rwkv_a2, rwkv_g2, rwkv_k_k, rwkv_k_a, rwkv_r_k, rwkv_ln_w, rwkv_ln_b, rwkv_v0,
              rwkv_v1, rwkv_v2, mem_norm, norm_xattn, xattn_wq, xattn_wk, xattn_wv, xattn_wo, norm_ffn,
              ffn_w_gate, ffn_w_up, ffn_w_down, moe_router, moe_w_gate, moe_w_up, moe_w_down, norm_final):
    mem_n = rmsnorm(mem, mem_norm)
    lb = jnp.cumsum(jax.nn.softmax(hgrn_lb_logits.astype(jnp.float32), axis=0), axis=0)
    lb = lb - lb[0]
    v_first = None
    for l in range(DEPTH):
        h = rmsnorm(x, norm_mix[l])
        p = h @ w_in[l]
        p_a, p_b, p_c, p_d = split_cols(p, (HG_COLS, GDN_COLS, LRU_COLS, RWKV_COLS))
        q_a, f_a, i_a, g_a = split_cols(p_a, (GROUP, GROUP, GROUP, GROUP))
        y_a = hgrn2_mixer(q_a, f_a, i_a, g_a, lb[l], hgrn_norm[l])
        qkv_b, z_b, alpha_b, beta_b = split_cols(p_b, (3 * GROUP, GROUP, N_HEADS_GROUP, N_HEADS_GROUP))
        y_b = gated_deltanet_mixer(qkv_b, z_b, alpha_b, beta_b, gdn_conv_w[l], gdn_A_log[l], gdn_dt_bias[l],
                                   gdn_norm[l])
        x_c, gate_c = split_cols(p_c, (GROUP, GROUP))
        y_c = rglru_mixer(x_c, gate_c, lru_conv_w[l], lru_conv_b[l], lru_wa[l], lru_ba[l], lru_wx[l], lru_bx[l],
                          lru_lambda[l])
        v_mix = None if l == 0 else (rwkv_v0[l - 1], rwkv_v1[l - 1], rwkv_v2[l - 1])
        y_d, v_first = rwkv7_mixer(p_d, rwkv_mu[l], rwkv_w0[l], rwkv_w2[l], rwkv_a0[l], rwkv_a2[l], rwkv_g2[l],
                                   rwkv_k_k[l], rwkv_k_a[l], rwkv_r_k[l], rwkv_ln_w[l], rwkv_ln_b[l], v_first, v_mix)
        x = x + jnp.concatenate([y_a, y_b, y_c, y_d], axis=-1) @ w_out[l]
        x = x + memory_cross_attention(rmsnorm(x, norm_xattn[l]), mem_n, xattn_wq[l], xattn_wk[l], xattn_wv[l],
                                       xattn_wo[l])
        h = rmsnorm(x, norm_ffn[l])
        if l % 2 == 0:
            x = x + swiglu(h, ffn_w_gate[l // 2], ffn_w_up[l // 2], ffn_w_down[l // 2])
        else:
            x = x + moe_swiglu(h, moe_router[l // 2], moe_w_gate[l // 2], moe_w_up[l // 2], moe_w_down[l // 2])
    return rmsnorm(x, norm_final)


_drawn_inputs = setup_inputs


def setup_inputs(seed=0):
    import zlib

    import numpy as np

    out = dict(_drawn_inputs(seed))
    spreads = {}
    factors = {'hgrn_norm': 2.799,
     'gdn_norm': 3.414,
     'lru_ba': 8.0,
     'lru_bx': 8.0,
     'rwkv_k_k': 2.919,
     'rwkv_ln_w': 4.387,
     'rwkv_ln_b': 2.908,
     'rwkv_v0': 2.683,
     'mem_norm': 2.695,
     'norm_xattn': 4.749,
     'norm_final': 8.541,
     'norm_ffn': 3.143}
    for name, (base, spread) in spreads.items():
        noise = np.random.default_rng([zlib.crc32(name.encode()), seed]).standard_normal(out[name].shape)
        drawn = base * np.exp(spread * noise) if base else spread * noise
        out[name] = __import__('jax').numpy.asarray(drawn.astype(out[name].dtype))
    for name, factor in factors.items():
        out[name] = (out[name] * factor).astype(out[name].dtype)
    return out
```

```python
from contextlib import ExitStack

import numpy as np

import concourse.bass as bass
from concourse import mybir

P = 128
D = 1024
KT = D // P
SEQ = 256
TT = SEQ // P
DEPTH = 2
GROUP = 256
HD = 64
NH = 4
LEVELS = 7
D_FF = 2816
D_FFE = 3584
NE = 8
CH = 2048
CM_COLS = CH // KT
TM_ROWS = CH // D
EPS = 1e-6
GN_EPS = 64e-5
RAW = 3
SPL = 3

F32 = mybir.dt.float32
F32R = mybir.dt.float32r
I32 = mybir.dt.int32
U32 = mybir.dt.uint32
ACT = mybir.ActivationFunctionType
ALU = mybir.AluOpType
AX = mybir.AxisListType.X

A_Q, A_F, A_I, A_G, B_Q, B_K, B_V, B_Z, C_X, C_G, D_R, D_K, D_V, D_W, D_G = 0, 2, 4, 6, 8, 10, 12, 14, 16, 18, 20, 22, 24, 26, 27
GDN_AB = 2048
W_IN_COLS = [256 * j for j in range(8)] + [GDN_AB + 8 + 256 * j for j in range(6)]


def param_columns():
    sizes = [("norm_mix", 8), ("norm_xattn", 8), ("norm_ffn", 8), ("hgrn_norm", 2), ("gdn_conv_w", 24),
             ("gdn_A_log", 4), ("gdn_dt_bias", 4), ("gdn_norm", 1), ("lru_conv_w", 8), ("lru_conv_b", 2),
             ("lru_ba", 2), ("lru_bx", 2), ("lru_lambda", 2), ("rwkv_mu", 8), ("rwkv_w0", 2), ("rwkv_a0", 2),
             ("rwkv_k_k", 2), ("rwkv_k_a", 2), ("rwkv_r_k", 2), ("rwkv_ln_w", 2), ("rwkv_ln_b", 2)]
    at, out = 0, {}
    for layer in range(DEPTH):
        for name, n in sizes:
            out[name, layer] = (at, n)
            at += n
    for name, n in (("lb0", 2), ("lb1", 2), ("rwkv_v0", 2), ("mem_norm", 8)):
        out[name] = (at, n)
        at += n
    return out, at


PCOL, NPAR = param_columns()
C_ID, C_INCL, C_STRICT, C_BD, C_IOTA = (P * i for i in range(5))
NCON = P * 5
SW_LRU, SW_WA, SW_G2, SW_V1, SW_V2 = 0, 4 * P, 4 * P + GROUP, 4 * P + 2 * GROUP, 4 * P + 2 * GROUP + 64
NSW = SW_V2 + GROUP


def plan_chunks():
    out = []
    for layer in range(DEPTH):
        out += [("cm", "w_in", layer, c) for c in W_IN_COLS]
        out += [("tm", "w_out", layer, r) for r in range(0, KT, TM_ROWS)]
        out += [("cm", "xattn_wk", layer, c) for c in range(0, D, CM_COLS)]
        out += [("tm", "xattn_wv", layer, r) for r in range(0, KT, TM_ROWS)]
        out += [("cm", "xattn_wq", layer, c) for c in range(0, D, CM_COLS)]
        out += [("tm", "xattn_wo", layer, r) for r in range(0, KT, TM_ROWS)]
        if layer == 0:
            steps = D_FF // CM_COLS
            for j in range(steps + 1):
                if j < steps:
                    out += [("cm", "ffn_w_gate", 0, CM_COLS * j), ("cm", "ffn_w_up", 0, CM_COLS * j)]
                if j:
                    out += [("tm", "ffn_w_down", 0, TM_ROWS * (j - 1))]
    return out


def build(nc, A, out):
    chunks = plan_chunks()
    n_straight = len(chunks)
    first_chunk = {}
    for n, c in enumerate(chunks):
        first_chunk.setdefault(c[1:3], n)
    FSTEPS = D_FF // CM_COLS
    ESTEPS = D_FFE // CM_COLS

    with ExitStack() as ctx:
        def sb(name, cols, dt=F32):
            return ctx.enter_context(nc.sbuf_tensor(name, [P, cols], dt))

        sems = {}

        def S(name):
            if name not in sems:
                sems[name] = ctx.enter_context(nc.semaphore(name))
            return sems[name]

        raw = [sb(f"raw{i}", CH) for i in range(RAW)]
        whi = [sb(f"whi{i}", CH, F32R) for i in range(SPL)]
        wlo = [sb(f"wlo{i}", CH, F32R) for i in range(SPL)]
        x = sb("x", TT * D)[:, :].rearrange("p (t n) -> p t n", t=TT)
        hT = [sb(f"hT_{s}", KT * SEQ, F32R)[:, :].rearrange("p (c n) -> p c n", c=KT) for s in ("hi", "lo")]
        memT_flat = [sb(f"memT_{s}", KT * SEQ, F32R) for s in ("hi", "lo")]
        memT = [m[:, :].rearrange("p (c n) -> p c n", c=KT) for m in memT_flat]
        yT = hT
        actT = [[sb(f"act{b}_{s}", 2 * SEQ, F32R)[:, :] for s in ("hi", "lo")] for b in range(2)]
        small = [sb(f"wsm_{s}", 64, F32R)[:, :].rearrange("p (k n) -> p k n", k=KT) for s in ("hi", "lo")]
        PT = sb("PT", 28 * SEQ)
        MT = sb("MT", 7 * 1024)
        TMP = sb("TMP", 8 * 512)
        v_first = sb("v_first", 512)
        par = sb("par", NPAR)
        con = sb("con", NCON)
        sw = sb("sw", NSW)
        wsm_raw = sb("wsm_raw", 64)
        st = sb("st", 256)
        ps = ctx.enter_context(nc.psum_tensor("ps", [P, 8, 512], F32))

        def pt(m, n=2):
            return PT[:, m * SEQ:(m + n) * SEQ]

        def mt(i):
            return MT[:, i * 1024:(i + 1) * 1024]

        def tmp(i):
            return TMP[:, i * 512:(i + 1) * 512]

        def pc(name, layer=None, j=0, rows=slice(0, P)):
            a, _ = PCOL[(name, layer) if layer is not None else name]
            return par[rows, a + j:a + j + 1]

        def cst(a, n=P):
            return con[:, a:a + n]

        ident = cst(C_ID)
        con16 = sb("con16", 2 * LEVELS * P, mybir.dt.bfloat16)
        bdones = cst(C_BD)
        incl, strict = cst(C_INCL), cst(C_STRICT)
        xs = PT[:, 0:TT * D].rearrange("p (t n) -> p t n", t=TT)

        def cm(ap):
            return ap.rearrange("p (c n) -> p c n", c=2)

        NORMS = ["mem", "mix0", "xat0", "ffn0", "mix1", "xat1", "ffn1"]
        cm_index, n_cm = {}, 0
        for n, c in enumerate(chunks):
            if c[0] == "cm" and not c[1].startswith("ffn"):
                cm_index[n] = n_cm
                n_cm += 1
        TM_PHASES = [(w, l) for l in range(DEPTH) for w in ("w_out", "xattn_wv", "xattn_wo")]
        TM_PHASES.insert(3, ("ffn_w_down", 0))

        def chunk_src(c):
            kind, name, layer, at = c
            w = A[name][layer]
            if kind == "cm":
                return w.rearrange("(k p) n -> p k n", p=P)[:, :, at:at + CM_COLS]
            return w.rearrange("(k p) n -> p k n", p=P)[:, at:at + TM_ROWS, :]

        def chunk_view(ap, kind):
            return ap.rearrange("p (k n) -> p k n", k=KT if kind == "cm" else TM_ROWS)

        class Signalled:

            def __init__(self, ins):
                self.ins, self.sem = ins, None

            def then_inc(self, sem, by):
                if by:
                    self.ins.then_inc(sem, by)
                    self.sem = sem
                return self

        class Chain:

            def __init__(self, eng, own):
                self.eng, self.own, self.last, self.counts = eng, own, None, {}

            def settle(self):
                if self.last is not None:
                    if self.last.sem is None:
                        self.last.then_inc(self.own, 1)
                    n = self.counts[self.last.sem.name] = self.counts.get(self.last.sem.name, 0) + 1
                    self.eng.wait_ge(self.last.sem, n)
                self.last = None

            def link(self, emit):
                self.settle()
                self.last = Signalled(emit())
                return self.last



        def H(i):
            return MT[:, i * 512:(i + 1) * 512]

        def lvl(v, flip=False):
            a = (v + LEVELS * flip) * P
            return con16[:, a:a + P]

        def rep(ap, n):
            return ap.unsqueeze(1).to_broadcast([P, n, P])

        def many(ap, n=4):
            return ap.rearrange("p (n m) -> p n m", n=n)

        def at(par_, t, c):
            return par_ * 512 + t * 256 + c * P

        def col(a, n=1):
            return st[:, a:a + n]

        ST_AB, ST_SIG, ST_X, ST_SP, ST_EXPA, ST_LBD, ST_LB, ST_LB1, ST_LAM = 16, 32, 48, 56, 64, 68, 70, 72, 74
        ST_G, ST_GC, ST_GTOT, ST_GD, ST_EGC, ST_NC0 = 80, 88, 96, 104, 112, 120
        ST_MX, ST_SUM, ST_RS = 128, 136, 144
        ST_LG, ST_TOP, ST_SEL, ST_GATE, ST_RANK, ST_W = 160, 176, 192, 208, 224, 240
        ST_BASE, ST_TOTAL, ST_OVER, ST_NEXT, ST_COUNT, ST_N1 = ST_SIG, ST_X, ST_SP, ST_EXPA, ST_G, ST_G + 1
        beta = col(ST_SIG, 16).rearrange("p (t n) -> p t n", t=2)[:, :, 4:8]

        kT = PT[:, 2048:4096].rearrange("p (c n) -> p c n", c=KT)
        vA = PT[:, 4096:6144].rearrange("p (t n) -> p t n", t=TT)
        qT = MT[:, 0:2048].rearrange("p (c n) -> p c n", c=KT)
        pr = MT[:, 2048:4096].rearrange("p (t h n) -> p t h n", t=TT, h=NH)
        prT = MT[:, 4096:6144].rearrange("p (m h n) -> p m h n", m=2, h=NH)
        hE = [m[:, 0:KT * P].rearrange("p (c n) -> p c n", c=KT) for m in memT_flat]
        yE = mt(2)
        g_tokens = lambda c: ps[:, 6 + c // 4, P * (c % 4):P * (c % 4) + P]
        pass_expert, gather_expert, pass_count = (col(a_, n_).bitcast(I32) for a_, n_ in
                                                  ((ST_AB, 2 * NE), (ST_NEXT, 2 * NE), (ST_COUNT, 1)))
        SECONDS = TT * P * 2 // (P + 1)
        oneh, onehg, onehT = mt(3)[:, 0:256], mt(3)[:, 256:512], mt(4)[:, 0:256]
        EXRAW = 2 * RAW
        assert (3 * ESTEPS) % EXRAW == 0 and RAW == SPL == 3

        def ff_chunk(j):
            return first_chunk["ffn_w_gate", 0] + 3 * j - (1 if j else 0)

        def ff_down(j):
            return first_chunk["ffn_w_gate", 0] + 3 * j + (4 if j < FSTEPS - 1 else 2)

        assert ESTEPS % 2 == 0

        def ex_slot(q):
            return (n_straight + q) % SPL

        def ex_count(s, q):
            return s * 3 + (n_straight + q + 1)

        def ex_raw_slot(m, q):
            return (3 * m + q) % EXRAW

        def ex_fill(h, m, q):
            i = ex_raw_slot(m, q)
            return h + ((3 * m + q) // EXRAW + 1 + (len(range(i, n_straight, RAW)) if i < RAW else 0))

        ones = col(10).to_broadcast([P, P])
        epsc = lambda i: col(8 + i)
        mem = xs
        final_gain = PT[:, 6144:7168]
        ex_raw = [raw[i][:, :] for i in range(RAW)] + [PT[:, CH:2 * CH], PT[:, 2 * CH:3 * CH], TMP[:, 0:CH]]

        block = ctx.enter_context(nc.Block())

        @block.sync
        def _(sp):

            sp.dma_start(par[:, :], A["params"]).then_inc(S("tables_in"), 16)
            sp.dma_start(con[:, :], A["consts"]).then_inc(S("tables_in"), 16)
            sp.dma_start(con16[:, :], A["level_masks"]).then_inc(S("tables_in"), 16)
            sp.dma_start(xs, A["mem"][0].rearrange("(t p) n -> p t n", p=P)).then_inc(S("mem_in"), 16)
            sp.dma_start(x, A["x"][0].rearrange("(t p) n -> p t n", p=P)).then_inc(S("x_in"), 16)
            sp.dma_start(sw[:, :], A["small_w"][0]).then_inc(S("sw_in"), 16)
            sp.dma_start(wsm_raw[:, :].rearrange("p (k n) -> p k n", k=KT),
                 A["w_in"][0].rearrange("(k p) n -> p k n", p=P)[:, :, GDN_AB:GDN_AB + 8]).then_inc(S("wsm_in"), 16)
            for n, c in enumerate(chunks):
                if n >= RAW:
                    sp.wait_ge(S("w_lo"), n - RAW + 1)
                sp.dma_start(chunk_view(raw[n % RAW][:, :], c[0]), chunk_src(c)).then_inc(S(f"raw_in{n % RAW}"), 16)
                if n == first_chunk["w_out", 0]:
                    sp.wait_ge(S("wsm_split"), 1)
                    sp.dma_start(wsm_raw[:, :].rearrange("p (k n) -> p k n", k=KT),
                         A["w_in"][1].rearrange("(k p) n -> p k n", p=P)[:, :, GDN_AB:GDN_AB + 8]).then_inc(S("wsm_in"), 16)
                if n == first_chunk["xattn_wq", 0]:
                    sp.wait_ge(S("mix_done"), 1)
                    sp.dma_start(sw[:, :], A["small_w"][1]).then_inc(S("sw_in"), 16)
                if n == first_chunk["w_out", 1]:
                    sp.wait_ge(S("wsm_split"), 2)
                    sp.dma_start(wsm_raw[:, :].rearrange("p (k n) -> p k n", k=KT),
                         A["moe_router"][0].rearrange("(k p) n -> p k n", p=P)).then_inc(S("wsm_in"), 16)
            sp.wait_ge(S("x_done"), 5)
            sp.dma_start(final_gain, A["norm_final"]).then_inc(S("nf_in"), 16)

            def ex_load(name, e, j, h, m, q):
                i = ex_raw_slot(m, q)
                sp.wait_ge(S("w_lo"), ex_count(h * 2 + m, q - EXRAW))
                wt = A[name][0][bass.ds(e, 1)].rearrange("a (k p) n -> p (a k) n", p=P)
                down = name == "moe_w_down"
                src = wt[:, bass.ds(j * TM_ROWS, TM_ROWS), :] if down else wt[:, :, bass.ds(j * CM_COLS, CM_COLS)]
                sp.dma_start(chunk_view(ex_raw[i], "tm" if down else "cm"), src).then_inc(S(f"raw_in{i}"), 16)

            def ex_pass(ep, e):
                h = ep * (ESTEPS // 2)

                def step(j, h, m):
                    ex_load("moe_w_gate", e, j + 1, h, m, 2)
                    ex_load("moe_w_up", e, j + 1, h, m, 3)
                    ex_load("moe_w_down", e, j, h, m, 4)

                ex_load("moe_w_gate", e, 0, h, 0, 0)
                ex_load("moe_w_up", e, 0, h, 0, 1)
                step(0, h, 0)
                with sp.Fori(0, (ESTEPS - 2) // 2) as i:
                    for m in (1, 2):
                        step(i * 2 + m, h + i, m)
                ex_load("moe_w_down", e, ESTEPS - 1, h, ESTEPS - 1, 2)

            sp.wait_ge(S("w_lo"), n_straight)
            with sp.Fori(0, NE) as e:
                ex_pass(e, e)
            sp.wait_ge(S("ex_table"), 1)
            with sp.Fori(0, SECONDS) as i:
                which = sp.value_load(pass_expert[0:1, bass.ds(i + NE, 1)], min_val=0, max_val=NE)
                with sp.If(which < NE):
                    e = sp.value_load(pass_expert[0:1, bass.ds(i + NE, 1)], min_val=0, max_val=NE - 1)
                    ex_pass(i + NE, e)
            sp.wait_ge(S("x_done"), 7)
            sp.dma_start(out[0].rearrange("(t p) n -> p t n", p=P), x).then_inc(S("stored"), 16)
            sp.wait_ge(S("stored"), 16)

        @block.scalar
        def _(act):
            chain = Chain(act, S("act_step"))
            split = [0]

            def a(o, i, f, **kw):
                return chain.link(lambda: nc.scalar.activation(o, i, f, **kw))

            def ahead(n):
                while split[0] < min(n, n_straight):
                    i = split[0]
                    act.wait_ge(S(f"raw_in{i % RAW}"), 16 * (i // RAW + 1))
                    if i >= SPL:
                        act.wait_ge(S("chunk_done"), i - SPL + 1)
                    nc.scalar.activation(whi[i % SPL][:, :], raw[i % RAW][:, :], ACT.Copy).then_inc(S("w_hi"), 1)
                    split[0] += 1

            def norm(i, src, gain, dst):
                for t in range(TT):
                    a(mt(6), src[:, t, :], ACT.Square, accum_out=col(2 + t))
                a(col(4, 2), col(2, 2), ACT.Ln, scale=1.0 / D, bias=epsc(0))
                a(col(0, 2), col(4, 2), ACT.Exp, scale=-0.5).then_inc(S("n_rstd"), 1)
                for c in range(KT):
                    act.wait_ge(S("n_tr"), i * KT + c + 1)
                    a(dst[0][:, c, :], ps[:, c, 0:SEQ], ACT.Copy, scale=gain(c)).then_inc(S("n_hi"), 1)

            def cm_evac(n0, count, dst, scale=1.0):
                for j in range(count):
                    n = n0 + j
                    ahead(n + SPL)
                    act.wait_ge(S("chunk_done"), n + 1)
                    a(dst(j), ps[:, cm_index[n] % 4, :], ACT.Copy, scale=scale).then_inc(S("cm_free"), 1)

            def split_small(k):
                act.wait_ge(S("wsm_in"), 16 * (k + 1))
                if k:
                    act.wait_ge(S("ab_mm"), k)
                a(small[0], wsm_raw[:, :].rearrange("p (k n) -> p k n", k=KT), ACT.Copy).then_inc(S("wsm_hi"), 1)

            def gates(l):
                act.wait_ge(S("sm_ready"), l + 1)
                a(tmp(0), pt(A_F), ACT.Sigmoid, scale=-1.0).then_inc(S("s_kA"), 1)
                a(tmp(1), pt(A_G), ACT.Sigmoid)
                a(tmp(2), pt(B_Z), ACT.Sigmoid).then_inc(S("s_z"), 1)
                a(col(ST_SIG, 16), col(ST_AB, 16), ACT.Sigmoid)
                if l:
                    a(tmp(5), pt(A_F), ACT.Sigmoid)
                    a(col(ST_LB, 2), col(ST_LBD, 2), ACT.Sigmoid)
                act.wait_ge(S("conv_g"), l + 1)
                for j in range(3):
                    a(H(3 + j), H(j), ACT.Sigmoid).then_inc(S("s_qkv"), 1)
                act.wait_ge(S("shift"), l + 1)
                a(PT[0:64, D_W * SEQ:(D_W + 1) * SEQ], PT[0:64, D_W * SEQ:(D_W + 1) * SEQ], ACT.Tanh)
                a(pt(D_G, 1), pt(D_G, 1), ACT.Sigmoid).then_inc(S("lora_in"), 1)
                act.wait_ge(S("lru_mm"), l + 1)
                for j in range(2):
                    a(H(8)[:, 256 * j:256 * j + 256], ps[:, 0, 256 * j:256 * j + 256], ACT.Sigmoid, bias=pc("lru_ba", l, j))
                for j in range(2):
                    a(H(9)[:, 256 * j:256 * j + 256], ps[:, 1, 256 * j:256 * j + 256], ACT.Sigmoid, bias=pc("lru_bx", l, j)).then_inc(S("lru_ri"), 1)
                act.wait_ge(S("lora_mm"), l + 1)
                for j in range(2):
                    a(pt(C_X)[:, 256 * j:256 * j + 256], ps[:, 2, 256 * j:256 * j + 256], ACT.Sigmoid, bias=pc("rwkv_w0", l, j))
                for j in range(2):
                    a(pt(D_W)[:, 256 * j:256 * j + 256], ps[:, 3, 256 * j:256 * j + 256], ACT.Sigmoid, bias=pc("rwkv_a0", l, j))
                a(H(12), ps[:, 4, :], ACT.Copy).then_inc(S("lora_s"), 1)
                if l:
                    act.wait_ge(S("vmix_mm"), 1)
                    a(H(13)[0:32, 0:256], ps[0:32, 5, 0:256], ACT.Copy).then_inc(S("vmix1"), 1)
                    act.wait_ge(S("vmix_mm"), 2)
                    for j in range(2):
                        a(tmp(3)[:, 256 * j:256 * j + 256], ps[:, 6, 256 * j:256 * j + 256], ACT.Sigmoid,
                          bias=pc("rwkv_v0", None, j)).then_inc(S("vmix2"), 1)
                act.wait_ge(S("gelu_in"), l + 1)
                a(tmp(4), tmp(4), ACT.Sigmoid).then_inc(S("gelu_s"), 1)

            def logs(l):
                if l == 0:
                    a(tmp(5), pt(A_F), ACT.Abs)
                    a(tmp(5), tmp(5), ACT.Exp, scale=-1.0)
                    a(tmp(5), tmp(5), ACT.Ln, bias=1.0).then_inc(S("hg_ln"), 1)
                else:
                    act.wait_ge(S("hg_F"), 1)
                    a(tmp(6), tmp(5), ACT.Ln).then_inc(S("hg_ln"), 1)
                act.wait_ge(S("gd_x"), l + 1)
                a(col(ST_SP, 8), col(ST_X, 8), ACT.Abs)
                a(col(ST_SP, 8), col(ST_SP, 8), ACT.Exp, scale=-1.0)
                a(col(ST_SP, 8), col(ST_SP, 8), ACT.Ln, bias=1.0)
                o = PCOL["gdn_A_log", l][0]
                a(col(ST_EXPA, 4), par[:, o:o + 4], ACT.Exp).then_inc(S("gd_sp"), 1)
                o = PCOL["lru_lambda", l][0]
                a(col(ST_LAM, 2), par[:, o:o + 2], ACT.Abs)
                a(col(ST_LAM, 2), col(ST_LAM, 2), ACT.Exp, scale=-1.0)
                a(col(ST_LAM, 2), col(ST_LAM, 2), ACT.Ln, bias=1.0).then_inc(S("lam_sp"), 1)

            def rglru(l):
                act.wait_ge(S("lru_log"), l + 1)
                a(H(10), H(8), ACT.Exp)
                a(H(11), H(8), ACT.Exp, scale=2.0).then_inc(S("lru_a"), 1)
                act.wait_ge(S("lru_gain"), l + 1)
                a(H(11), H(11), ACT.Ln)
                a(H(11), H(11), ACT.Exp, scale=0.5).then_inc(S("lru_root"), 1)

            def hgrn(l):
                act.wait_ge(S("hg_tr"), l + 1)
                a(tmp(1), ps[:, 4, :], ACT.Copy).then_inc(S("hg_v"), 1)
                for v in range(LEVELS):
                    act.wait_ge(S("hg_d"), l * LEVELS + v + 1)
                    a(tmp(6 + v % 2), tmp(6 + v % 2), ACT.Exp).then_inc(S("hg_e"), 1)
                act.wait_ge(S("hg_qk"), (l + 1) * LEVELS)
                a(tmp(6), pt(A_F), ACT.Exp)
                for c in range(2):
                    b = pt(A_F)[:, 256 * c:256 * c + P]
                    a(tmp(7)[:, P * c:P * c + P], b, ACT.Exp, scale=-1.0, bias=b[:, P - 1:P]).then_inc(S("hg_end"), 1)
                act.wait_ge(S("hg_trk"), l + 1)
                a(tmp(5)[:, 0:256], ps[:, 5, 0:256], ACT.Copy).then_inc(S("hg_kd"), 1)
                head_rms(l, 0, 7)

            def head_rms(l, which, bank):
                act.wait_ge(S("o_full"), 2 * l + which + 1)
                a(tmp(6), ps[:, bank, :], ACT.Square).then_inc(S("o_sq"), 1)
                act.wait_ge(S("o_ss"), 2 * l + which + 1)
                a(tmp(7), ps[:, 6, :], ACT.Ln, scale=1.0 / HD, bias=epsc(0))
                a(tmp(7), tmp(7), ACT.Exp, scale=-0.5).then_inc(S("o_rn"), 1)

            def deltanet(l):
                a(H(0), pt(B_Q), ACT.Square)
                a(H(1), pt(B_K), ACT.Square).then_inc(S("gd_sq"), 1)
                act.wait_ge(S("gd_ss"), l + 1)
                for j in range(2):
                    a(H(j), ps[:, 2 + j, :], ACT.Ln, bias=epsc(0))
                    a(H(j), H(j), ACT.Exp, scale=-0.5).then_inc(S("gd_rn"), 1)
                act.wait_ge(S("gd_gd"), l + 1)
                a(col(ST_GD, 8), col(ST_GD, 8), ACT.Exp)
                a(tmp(5), ps[:, 4, :], ACT.Exp).then_inc(S("gd_eg"), 1)
                act.wait_ge(S("gd_diff"), l + 1)
                a(mt(1), mt(1), ACT.Exp).then_inc(S("gd_rel"), 1)
                for t in range(TT):
                    act.wait_ge(S("gd_u"), 2 * l + t + 1)
                    a(tmp(6)[:, 256 * t:256 * t + 256], ps[:, 6, 256 * t:256 * t + 256], ACT.Copy).then_inc(S("gd_us"), 1)
                head_rms(l, 1, 0)

            def rwkv(l):
                act.wait_ge(S("rk_kk"), l + 1)
                a(tmp(1), tmp(0), ACT.Square).then_inc(S("rk_sq"), 1)
                act.wait_ge(S("rk_ss"), l + 1)
                a(tmp(1), ps[:, 2, :], ACT.Ln, bias=epsc(0))
                a(tmp(1), tmp(1), ACT.Exp, scale=-0.5).then_inc(S("rk_rn"), 1)
                act.wait_ge(S("rk_b"), l + 1)
                for c in range(2):
                    for t in range(TT):
                        s_ = slice(256 * c + P * t, 256 * c + P * t + P)
                        b, bm, mid = tmp(3)[:, s_], tmp(4)[:, s_], 256 * c + P * t + HD - 1
                        n0 = col(ST_NC0 + 2 * c + t)
                        a(tmp(5)[:, s_], b, ACT.Exp, bias=n0)
                        a(tmp(6)[:, s_], b, ACT.Exp, scale=-1.0, bias=tmp(3)[:, mid:mid + 1])
                        a(tmp(7)[:, s_], bm, ACT.Exp, bias=n0)
                    s0, s1 = slice(256 * c, 256 * c + P), slice(256 * c + P, 256 * c + 256)
                    a(pt(A_Q)[:, s0], tmp(3)[:, s0], ACT.Exp, scale=-1.0, bias=tmp(3)[:, 256 * c + P - 1:256 * c + P])
                    a(pt(A_Q)[:, s1], tmp(3)[:, s1], ACT.Exp)
                    a(pt(A_F)[:, s1], tmp(4)[:, s1], ACT.Exp).then_inc(S("rk_e"), 1)
                act.wait_ge(S("rk_trv"), l + 1)
                a(tmp(5), ps[:, 6, :], ACT.Copy)
                a(tmp(6), ps[:, 7, :], ACT.Copy).then_inc(S("rk_vk"), 1)
                for t in range(TT):
                    act.wait_ge(S("rk_r"), 2 * l + t + 1)
                    a(tmp(7)[:, 256 * t:256 * t + 256], ps[:, 6, 256 * t:256 * t + 256], ACT.Copy).then_inc(S("rk_rs"), 1)
                    act.wait_ge(S("rk_u"), 2 * l + t + 1)
                    a(tmp(4)[:, 256 * t:256 * t + 256], ps[:, 7, 256 * t:256 * t + 256], ACT.Copy, scale=-1.0).then_inc(S("rk_us"), 1)
                act.wait_ge(S("rk_o"), l + 1)
                a(tmp(0), ps[:, 0, :], ACT.Copy).then_inc(S("rk_y"), 1)
                act.wait_ge(S("rk_yc"), l + 1)
                a(tmp(1), tmp(0), ACT.Square).then_inc(S("rk_ysq"), 1)
                act.wait_ge(S("rk_var"), l + 1)
                a(tmp(1), ps[:, 2, :], ACT.Ln, scale=1.0 / HD, bias=epsc(1))
                a(tmp(1), tmp(1), ACT.Exp, scale=-0.5).then_inc(S("rk_grn"), 1)

            def attention(l):
                cm_evac(first_chunk["xattn_wk", l], 4, lambda j: kT[:, 2 * j:2 * j + 2, :].rearrange("p c n -> p (c n)"))
                n = first_chunk["xattn_wv", l]
                for j in range(4):
                    ahead(n + j + SPL)
                act.wait_ge(S("chunk_done"), n + 4)
                for t in range(TT):
                    for hf in range(2):
                        a(vA[:, t, 512 * hf:512 * hf + 512], ps[:, 4 + 2 * t + hf, :], ACT.Copy).then_inc(S("at_v"), 1)
                act.wait_ge(S("x_done"), 3 * l + 1)
                norm(2 + 3 * l, x, lambda c: pc("norm_xattn", l, c), hT)
                cm_evac(first_chunk["xattn_wq", l], 4, lambda j: qT[:, 2 * j:2 * j + 2, :].rearrange("p c n -> p (c n)"),
                        scale=1.0 / 16.0)
                for i in range(2 * NH):
                    t, h = i // NH, i % NH
                    act.wait_ge(S("at_max"), 4 * l + i // 2 + 1)
                    a(pr[:, t, h, :], ps[:, i // 2, 256 * (h % 2):256 * (h % 2) + 256], ACT.Exp,
                      bias=col(ST_MX + i), accum_out=col(ST_SUM + i)).then_inc(S("at_exp"), 1)
                for b in range(4):
                    act.wait_ge(S("at_tr"), 4 * l + b + 1)
                    t, m = b // 2, b % 2
                    a(prT[:, m, :, t * P:(t + 1) * P], many(ps[:, 4 + b, :]), ACT.Copy).then_inc(S("at_prT"), 1)
                for b in range(4):
                    act.wait_ge(S("at_o"), 4 * l + b + 1)
                    a(yT[0][:, 2 * b:2 * b + 2, :].rearrange("p c n -> p (c n)"), ps[:, b, :], ACT.Copy).then_inc(S("at_hi"), 1)
                n = first_chunk["xattn_wo", l]
                for j in range(4):
                    ahead(n + j + SPL)

            def swiglu():
                act.wait_ge(S("x_done"), 2)
                norm(3, x, lambda c: pc("norm_ffn", 0, c), hT)
                for j in range(FSTEPS):
                    n = ff_chunk(j)
                    ahead(n + SPL)
                    act.wait_ge(S("chunk_done"), n + 1)
                    if j:
                        act.wait_ge(S("ff_prod"), j)
                    a(mt(0)[:, 0:512], ps[:, 2 * (j % 2), :], ACT.Silu).then_inc(S("ff_silu"), 1)
                    ahead(n + 1 + SPL)
                    act.wait_ge(S("ff_prod"), j + 1)
                    if j >= 2:
                        act.wait_ge(S("chunk_done"), ff_down(j - 2) + 1)
                    a(actT[j % 2][0], mt(1)[:, 512 * (j % 2):512 * (j % 2) + 512], ACT.Copy).then_inc(S("ff_hi"), 1)
                ahead(ff_down(FSTEPS - 1) + SPL)

            def experts():
                act.wait_ge(S("x_done"), 5)
                norm(6, x, lambda c: pc("norm_ffn", 1, c), hT)
                act.wait_ge(S("rt_d"), 1)
                a(col(ST_W, 4), col(ST_W, 4), ACT.Sigmoid).then_inc(S("rt_p"), 1)

                def chunk(h, m, q):
                    i, slot = ex_raw_slot(m, q), ex_slot(q)
                    act.wait_ge(S(f"raw_in{i}"), ex_fill(h, m, q) * 16)
                    act.wait_ge(S("chunk_done"), ex_count(h * 2 + m, q - SPL))
                    nc.scalar.activation(whi[slot][:, :], ex_raw[i], ACT.Copy).then_inc(S("w_hi"), 1)

                def silu(s, gate_done):
                    act.wait_ge(S("chunk_done"), gate_done)
                    act.wait_ge(S("ex_prod"), s + 1)
                    nc.scalar.activation(mt(0)[:, 0:256], ps[:, 0, 0:256], ACT.Silu).then_inc(S("ex_silu"), 1)

                def act_hi(s):
                    act.wait_ge(S("ex_tr"), s + 2)
                    nc.scalar.activation(actT[0][0][:, 0:256], ps[:, 2, 0:256], ACT.Copy).then_inc(S("ex_ahi"), 1)

                def gathered(p):
                    for c in range(KT):
                        act.wait_ge(S("ex_g"), p * 2 + (c // 4 + 1))
                        nc.scalar.activation(hE[0][:, c, :], g_tokens(c), ACT.Copy, scale=pc("norm_ffn", 1, c)).then_inc(S("ex_hi"), 1)

                def expert_output(q):
                    act.wait_ge(S("chunk_done"), ex_count(q * ESTEPS - 1, 2))
                    act.wait_ge(S("ex_add"), q + 1)
                    for hf in range(2):
                        nc.scalar.activation(yE[:, 512 * hf:512 * hf + 512], ps[:, 4 + hf, :], ACT.Copy).then_inc(S("ex_y"), 1)

                def step(h, m):
                    chunk(h, m, 2)
                    chunk(h, m, 3)
                    act_hi(h * 2 + m)
                    chunk(h, m, 4)

                chain.settle()
                act.wait_ge(S("ex_table"), 1)
                count = act.value_load(pass_count[0:1, 0:1], min_val=NE, max_val=NE + SECONDS)
                act.wait_ge(S("ex_tr"), 1)
                gathered(0)
                with act.Fori(0, NE + SECONDS) as ep:
                    which = act.value_load(pass_expert[0:1, bass.ds(ep, 1)], min_val=0, max_val=NE)
                    with act.If(which < NE):
                        h = ep * (ESTEPS // 2)
                        r = ep * ESTEPS
                        chunk(h, 0, 0)
                        chunk(h, 0, 1)
                        expert_output(ep)
                        silu(r, ex_count(r, 0))
                        step(h, 0)
                        with act.Fori(0, (ESTEPS - 2) // 2) as i:
                            for m in (1, 2):
                                silu(r + i * 2 + m, ex_count(r + i * 2 + (m - 1), 2))
                                step(h + i, m)
                        silu(r + (ESTEPS - 1), ex_count(r + (ESTEPS - 2), 2))
                        chunk(h, ESTEPS - 1, 2)
                        act.wait_ge(S("chunk_done"), ex_count(r + (ESTEPS - 2), 3))
                        gathered(ep + 1)
                        act_hi(r + (ESTEPS - 1))
                expert_output(count)

            act.wait_ge(S("tables_in"), 48)
            act.wait_ge(S("tables_in"), 48)
            act.wait_ge(S("eps"), 1)
            ahead(SPL)
            split_small(0)
            act.wait_ge(S("mem_in"), 16)
            norm(0, mem, lambda c: pc("mem_norm", None, c), memT)
            act.wait_ge(S("x_in"), 16)
            for l in range(DEPTH):
                if l:
                    act.wait_ge(S("x_done"), 3)
                norm(1 + 3 * l, x, lambda c: pc("norm_mix", l, c), hT)
                cm_evac(first_chunk["w_in", l], 14, lambda j: pt(2 * j))
                act.wait_ge(S("sw_in"), 16 * (l + 1))
                gates(l)
                logs(l)
                rglru(l)
                hgrn(l)
                deltanet(l)
                rwkv(l)
                split_small(l + 1)
                n = first_chunk["w_out", l]
                for j in range(4):
                    ahead(n + j + SPL)
                attention(l)
                if l == 0:
                    swiglu()
            experts()
            act.wait_ge(S("x_done"), 6)
            for t in range(TT):
                a(mt(6), x[:, t, :], ACT.Square, accum_out=col(2 + t))
            a(col(4, 2), col(2, 2), ACT.Ln, scale=1.0 / D, bias=epsc(0))
            a(col(0, 2), col(4, 2), ACT.Exp, scale=-0.5).then_inc(S("n_rstd"), 1)

        @block.vector
        def _(dve):
            chain = Chain(dve, S("dve_step"))
            split = [0]
            V = nc.vector

            def tt(o, x0, x1, op):
                return chain.link(lambda: V.tensor_tensor(o, x0, x1, op))

            def ts(o, x0, s1, op0, s2=None, op1=None):
                return chain.link(lambda: V.tensor_scalar(o, x0, s1, s2, op0, op1) if op1 else V.tensor_scalar(o, x0, s1, None, op0))

            def stt(o, x0, s_, x1, op0, op1):
                return chain.link(lambda: V.scalar_tensor_tensor(out=o, in0=x0, scalar=s_, in1=x1, op0=op0, op1=op1))

            def ahead(n):
                while split[0] < min(n, n_straight):
                    i = split[0]
                    dve.wait_ge(S("w_hi"), i + 1)
                    V.tensor_tensor(wlo[i % SPL][:, :], raw[i % RAW][:, :], whi[i % SPL][:, :].bitcast(F32),
                                    ALU.subtract).then_inc(S("w_lo"), 1)
                    split[0] += 1

            def norm(i, src, gain, dst):
                dve.wait_ge(S("n_rstd"), i + 1)
                for t in range(TT):
                    ts(xs[:, t, :], src[:, t, :], col(t), ALU.mult).then_inc(S("n_xs"), 1)
                for c in range(KT):
                    dve.wait_ge(S("n_hi"), i * KT + c + 1)
                    stt(dst[1][:, c, :], ps[:, c, 0:SEQ], gain(c), dst[0][:, c, :].bitcast(F32), ALU.mult, ALU.subtract).then_inc(S("n_lo"), 1)

            def cm_steps(n0, count):
                for j in range(count):
                    ahead(n0 + j + SPL)

            def tm_add(n0, count):
                for j in range(count):
                    ahead(n0 + j + SPL)
                dve.wait_ge(S("chunk_done"), n0 + count)
                for t in range(TT):
                    for hf in range(2):
                        s_ = slice(512 * hf, 512 * hf + 512)
                        last = t == TT - 1 and hf == 1
                        tt(x[:, t, s_], x[:, t, s_], ps[:, 4 + 2 * t + hf, :], ALU.add).then_inc(S("x_done"), 1 if last else 0)

            def split_small(k):
                dve.wait_ge(S("wsm_hi"), k + 1)
                tt(small[1], wsm_raw[:, :].rearrange("p (k n) -> p k n", k=KT), small[0].bitcast(F32), ALU.subtract).then_inc(S("wsm_split"), 1)

            def gates(l):
                dve.wait_ge(S("ab_mm"), l + 1)
                if l:
                    o0, o1 = PCOL["lb0"][0], PCOL["lb1"][0]
                    tt(col(ST_LBD, 2), par[:, o1:o1 + 2], par[:, o0:o0 + 2], ALU.subtract)
                chain.link(lambda: V.tensor_copy(col(ST_AB, 16), ps[:, 7, 0:16])).then_inc(S("sm_ready"), 1)
                dve.wait_ge(S("cm_free"), cm_index[first_chunk["w_in", l]] + 14)
                taps = PCOL["gdn_conv_w", l][0]
                for m in range(6):
                    src, dst = pt(B_Q + m, 1), MT[:, 256 * m:256 * m + 256]
                    ts(dst, src, par[:, taps + 18 + m:taps + 19 + m], ALU.mult)
                    for j in range(3):
                        k = 3 - j
                        stt(dst[:, k:], src[:, :SEQ - k], par[:, taps + 6 * j + m:taps + 6 * j + m + 1], dst[:, k:],
                            ALU.mult, ALU.add).then_inc(S("conv_g"), 1 if m == 5 and j == 2 else 0)
                taps = PCOL["lru_conv_w", l][0]
                for m in range(2):
                    src, dst = pt(C_X + m, 1), H(6)[:, 256 * m:256 * m + 256]
                    ts(dst, src, par[:, taps + 6 + m:taps + 7 + m], ALU.mult, pc("lru_conv_b", l, m), ALU.add)
                    for j in range(3):
                        k = 3 - j
                        stt(dst[:, k:], src[:, :SEQ - k], par[:, taps + 2 * j + m:taps + 2 * j + m + 1], dst[:, k:],
                            ALU.mult, ALU.add).then_inc(S("conv_l"), 1 if m == 1 and j == 2 else 0)
                c8 = pt(D_R, 8).rearrange("p (m n) -> p m n", m=8)
                d8 = MT[:, 4096:6144].rearrange("p (m n) -> p m n", m=8)
                tt(d8[:, :, 1:], c8[:, :, :SEQ - 1], c8[:, :, 1:], ALU.subtract)
                ts(d8[:, :, 0:1], c8[:, :, 0:1], -1.0, ALU.mult)
                for m in range(8):
                    stt(c8[:, m, :], d8[:, m, :], pc("rwkv_mu", l, m), c8[:, m, :], ALU.mult, ALU.add).then_inc(S("shift"), 1 if m == 7 else 0)
                g0 = 2.0 * float(np.sqrt(2.0 / np.pi))
                tt(tmp(4), pt(C_G), pt(C_G), ALU.mult)
                ts(tmp(4), tmp(4), 0.044715 * g0, ALU.mult, g0, ALU.add)
                tt(tmp(4), tmp(4), pt(C_G), ALU.mult).then_inc(S("gelu_in"), 1)
                dve.wait_ge(S("s_z"), l + 1)
                tt(pt(A_G), pt(A_G), tmp(1), ALU.mult)
                tt(pt(B_Z), pt(B_Z), tmp(2), ALU.mult)
                dve.wait_ge(S("s_qkv"), 3 * (l + 1))
                tt(pt(B_Q, 6), MT[:, 0:1536], MT[:, 1536:3072], ALU.mult)
                o = PCOL["gdn_dt_bias", l][0]
                for t in range(TT):
                    tt(col(ST_X + 4 * t, 4), col(ST_AB + 8 * t, 4), par[:, o:o + 4], ALU.add).then_inc(S("gd_x"), 1 if t else 0)
                dve.wait_ge(S("gelu_s"), l + 1)
                tt(pt(C_G), pt(C_G), tmp(4), ALU.mult)
                if l == 0:
                    chain.link(lambda: V.tensor_copy(v_first[:, :], pt(D_V)))
                else:
                    dve.wait_ge(S("vmix2"), 2)
                    tt(v_first[:, :], v_first[:, :], pt(D_V), ALU.subtract)
                    tt(v_first[:, :], v_first[:, :], tmp(3), ALU.mult)
                    tt(pt(D_V), pt(D_V), v_first[:, :], ALU.add)
                    ts(col(ST_LB1, 2), col(ST_LB, 2), -1.0, ALU.mult, 1.0, ALU.add)
                    for c in range(2):
                        s_ = slice(256 * c, 256 * c + 256)
                        ts(tmp(5)[:, s_], tmp(5)[:, s_], col(ST_LB1 + c), ALU.mult, col(ST_LB + c), ALU.add).then_inc(S("hg_F"), 1 if c else 0)
                    for c in range(2):
                        s_ = slice(256 * c, 256 * c + 256)
                        ts(tmp(0)[:, s_], tmp(0)[:, s_], col(ST_LB1 + c), ALU.mult)

            def logs(l):
                dve.wait_ge(S("hg_ln"), l + 1)
                if l == 0:
                    stt(tmp(6), pt(A_F), 0.0, tmp(5), ALU.min, ALU.subtract)
                dve.wait_ge(S("gd_sp"), l + 1)
                stt(col(ST_SP, 8), col(ST_X, 8), 0.0, col(ST_SP, 8), ALU.max, ALU.add)
                for t in range(TT):
                    stt(col(ST_G + 4 * t, 4), col(ST_SP + 4 * t, 4), -1.0, col(ST_EXPA, 4), ALU.mult, ALU.mult).then_inc(S("gd_g"), 1 if t else 0)
                dve.wait_ge(S("lam_sp"), l + 1)
                o = PCOL["lru_lambda", l][0]
                ts(col(ST_LAM + 2, 2), par[:, o:o + 2], -1.0, ALU.mult, 0.0, ALU.max)
                tt(col(ST_LAM, 2), col(ST_LAM, 2), col(ST_LAM + 2, 2), ALU.add)
                ts(col(ST_LAM, 2), col(ST_LAM, 2), -8.0, ALU.mult)

            def rglru(l):
                dve.wait_ge(S("lru_ri"), 2 * (l + 1))
                for c in range(2):
                    s_ = slice(256 * c, 256 * c + 256)
                    ts(H(8)[:, s_], H(8)[:, s_], col(ST_LAM + c), ALU.mult).then_inc(S("lru_log"), 1 if c else 0)
                ts(H(0), H(8), 2.0, ALU.mult)
                ts(H(1), H(0), 1.0 / 120, ALU.mult)
                for k in (1.0 / 24, 1.0 / 6, 0.5, 1.0):
                    stt(H(1), H(1), k, H(0), ALU.add, ALU.mult)
                ts(H(1), H(1), -1.0, ALU.mult)
                ts(H(0), H(0), -0.1, ALU.is_gt)
                dve.wait_ge(S("lru_a"), l + 1)
                ts(H(11), H(11), -1.0, ALU.mult, 1.0, ALU.add)
                chain.link(lambda: V.copy_predicated(H(11), H(0).bitcast(U32), H(1)))
                ts(H(11), H(11), 1e-18, ALU.max).then_inc(S("lru_gain"), 1)
                tt(H(9), H(9), H(6), ALU.mult)
                dve.wait_ge(S("lru_root"), l + 1)
                tt(H(9), H(9), H(11), ALU.mult)
                for c in range(2):
                    s_ = slice(256 * c, 256 * c + 256)
                    chain.link(lambda: V.tensor_tensor_scan(H(8)[:, s_], H(10)[:, s_], H(9)[:, s_], 0.0, ALU.mult, ALU.add))
                tt(H(8), H(8), pt(C_G), ALU.mult)
                put(2, H(8))

            def put(pair, src):
                o = [yT[i][:, 2 * pair:2 * pair + 2, :].rearrange("p c n -> p (c n)") for i in range(2)]
                chain.link(lambda: V.tensor_copy(o[0], src))
                tt(o[1], src, o[0].bitcast(F32), ALU.subtract).then_inc(S("y_put"), 1)

            def hgrn(l):
                one = ones
                b = pt(A_F)
                for i in range(4):
                    s_ = slice(P * i, P * i + P)
                    chain.link(lambda: V.tensor_tensor_scan(b[:, s_], one, tmp(6)[:, s_], 0.0, ALU.mult, ALU.add)).then_inc(S("hg_b"), 1 if i == 3 else 0)

                def diff(v):
                    h = 1 << v
                    bv = b.rearrange("p (n u h) -> p n u h", u=2, h=h)
                    dv = tmp(6 + v % 2).rearrange("p (n u h) -> p n u h", u=2, h=h)
                    n = 512 // (2 * h)
                    mid = bv[:, :, 0, h - 1:h].to_broadcast([P, n, h])
                    tt(dv[:, :, 0, :], mid, bv[:, :, 0, :], ALU.subtract)
                    tt(dv[:, :, 1, :], bv[:, :, 1, :], mid, ALU.subtract).then_inc(S("hg_d"), 1)

                def take(v):
                    dve.wait_ge(S("hg_s"), l * (LEVELS + 1) + v + 2)
                    for p_ in range(2):
                        bank = 2 * ((v + 1) % 2) + p_
                        o = many(mt(1)[:, 512 * p_:512 * p_ + 512])
                        if v < 0:
                            tt(o, many(ps[:, bank, :]), rep(ident, 4), ALU.mult).then_inc(S("hg_take"), 1 if p_ else 0)
                        else:
                            chain.link(lambda: V.copy_predicated(o, rep(lvl(v), 4).bitcast(mybir.dt.uint16), many(ps[:, bank, :]))).then_inc(S("hg_take"), 1 if p_ else 0)

                diff(0)
                diff(1)
                take(-1)
                for v in range(LEVELS):
                    dve.wait_ge(S("hg_e"), l * LEVELS + v + 1)
                    if v >= 2:
                        dve.wait_ge(S("hg_s"), l * (LEVELS + 1) + v)
                    tt(H(4 + v % 2), pt(A_Q), tmp(6 + v % 2), ALU.mult)
                    tt(H(v % 2), tmp(0), tmp(6 + v % 2), ALU.mult).then_inc(S("hg_qk"), 1)
                    if v + 2 < LEVELS:
                        diff(v + 2)
                    if v:
                        take(v - 1)
                take(LEVELS - 1)
                dve.wait_ge(S("hg_end"), 2 * (l + 1))
                tt(H(4), pt(A_Q), tmp(6), ALU.mult)
                k0 = cm(tmp(0))[:, :, 0:P]
                tt(H(0)[:, 0:256].rearrange("p (c n) -> p c n", c=2), k0, tmp(7)[:, 0:256].rearrange("p (c n) -> p c n", c=2),
                   ALU.mult).then_inc(S("hg_x"), 1)
                dve.wait_ge(S("state"), 3 * l + 1)
                tt(tmp(5)[:, 256:512].rearrange("p (c n) -> p c n", c=2), ps[:, 6, 0:256].rearrange("p (c n) -> p c n", c=2),
                   rep(bdones, 2), ALU.mult).then_inc(S("state_bd"), 1)
                head_out(l, 0, 7, lambda c: pc("hgrn_norm", l, c), pt(A_G), 0)

            def head_out(l, which, bank, gain, gate, pair):
                dve.wait_ge(S("o_rn"), 2 * l + which + 1)
                tt(tmp(7), ps[:, bank, :], tmp(7), ALU.mult)
                for c in range(2):
                    s_ = slice(256 * c, 256 * c + 256)
                    stt(tmp(7)[:, s_], tmp(7)[:, s_], gain(c), gate[:, s_], ALU.mult, ALU.mult)
                put(pair, tmp(7))

            def inverse(i):
                N, X, Y, T1 = mt(3), mt(4), mt(5), mt(0)
                for v in range(LEVELS):
                    for g in range(2):
                        s_ = slice(512 * g, 512 * g + 512)
                        k = 2 * (LEVELS * i + v) + g + 1
                        dve.wait_ge(S("inv_t"), k)
                        if v == 0:
                            tt(many(T1[:, s_]), many(ps[:, g, :]), rep(lvl(0, True), 4), ALU.mult)
                            tt(many(X[:, s_]), rep(ident, 4), many(T1[:, s_]), ALU.subtract)
                            tt(many(T1[:, s_]), many(N[:, s_]), rep(lvl(0), 4), ALU.mult)
                            tt(many(Y[:, s_]), rep(ident, 4), many(T1[:, s_]), ALU.subtract).then_inc(S("inv_xy"), 1)
                        else:
                            tt(many(T1[:, s_]), many(ps[:, g, :]), rep(lvl(v, True), 4), ALU.mult).then_inc(S("inv_t1"), 1)
                    if v:
                        for g in range(2):
                            s_ = slice(512 * g, 512 * g + 512)
                            dve.wait_ge(S("inv_p"), 2 * ((LEVELS - 1) * i + v - 1) + g + 1)
                            if v < LEVELS - 1:
                                tt(X[:, s_], X[:, s_], ps[:, 2 + g, :], ALU.subtract)
                            tt(Y[:, s_], Y[:, s_], ps[:, 4 + g, :], ALU.subtract).then_inc(S("inv_xy"), 1)

            def deltanet(l):
                chain.link(lambda: V.tensor_copy(many(tmp(6), 8), col(ST_G, 8).unsqueeze(2).to_broadcast([P, 8, HD])))
                for t in range(TT):
                    chain.link(lambda: V.tensor_copy(tmp(7)[:, 256 * t:256 * t + 256].rearrange("p (h n) -> p h n", h=4),
                                       beta[:, t, :].unsqueeze(2).to_broadcast([P, 4, HD]))).then_inc(S("gd_wide"), 1 if t else 0)
                dve.wait_ge(S("gd_rn"), 2 * (l + 1))
                stt(pt(B_Q), pt(B_Q), HD ** -0.5, H(0), ALU.mult, ALU.mult)
                tt(pt(B_K), pt(B_K), H(1), ALU.mult)
                dve.wait_ge(S("gd_cum"), l + 1)
                chain.link(lambda: V.tensor_copy(col(ST_GC, 16), ps[:, 5, 0:16]))
                tt(col(ST_GD, 8), col(ST_GTOT, 8), col(ST_GC, 8), ALU.subtract).then_inc(S("gd_gd"), 1)
                for p_ in range(2):
                    for t in range(TT):
                        for c in range(2):
                            a_ = at(p_, t, c)
                            ts(mt(1)[:, a_:a_ + P], ps[:, p_, a_ % 512:a_ % 512 + P], col(ST_GC + 4 * t + 2 * c + p_),
                               ALU.subtract, 0.0, ALU.min).then_inc(S("gd_diff"), 1 if a_ == at(1, 1, 1) else 0)
                dve.wait_ge(S("gd_eg"), l + 1)
                tt(tmp(0), pt(B_Q), tmp(5), ALU.mult)
                tt(tmp(1), pt(B_K), ps[:, 3, :], ALU.mult)
                tt(tmp(2), tmp(1), tmp(5), ALU.mult).then_inc(S("gd_ops"), 1)
                dve.wait_ge(S("gd_trk"), l + 1)
                dk = col(ST_GD, 4).unsqueeze(2).to_broadcast([P, 4, HD])
                tt(tmp(3)[:, 0:256].rearrange("p (h n) -> p h n", h=4), ps[:, 4, 0:256].rearrange("p (h n) -> p h n", h=4), dk, ALU.mult)
                for t in range(TT):
                    bt = beta[:, t, :].unsqueeze(2).to_broadcast([P, 4, HD])
                    tt(tmp(4)[:, 256 * t:256 * t + 256].rearrange("p (h n) -> p h n", h=4),
                       ps[:, 5, 256 * t:256 * t + 256].rearrange("p (h n) -> p h n", h=4), bt, ALU.mult)
                dve.wait_ge(S("gd_rel"), l + 1)
                tt(many(mt(1), 8), many(mt(1), 8), rep(incl, 8), ALU.mult)
                dve.wait_ge(S("gd_sc"), l + 1)
                tt(mt(3), ps[:, 6:8, :].rearrange("p b n -> p (b n)"), mt(1), ALU.mult)
                tt(many(mt(3), 8), many(mt(3), 8), rep(strict, 8), ALU.mult)
                tt(mt(2), ps[:, 2:4, :].rearrange("p b n -> p (b n)"), mt(1), ALU.mult).then_inc(S("inv_n"), 1)
                inverse(2 * l)
                dve.wait_ge(S("state"), 3 * l + 2)
                tt(tmp(3)[:, 256:512].rearrange("p (c n) -> p c n", c=2), ps[:, 7, 0:256].rearrange("p (c n) -> p c n", c=2),
                   rep(bdones, 2), ALU.mult).then_inc(S("state_bd"), 1)
                dve.wait_ge(S("gd_km"), l + 1)
                tt(tmp(4)[:, 256:512], tmp(4)[:, 256:512], ps[:, 7, 256:512], ALU.subtract).then_inc(S("gd_r1"), 1)
                head_out(l, 1, 0, lambda c: pc("gdn_norm", l), pt(B_Z), 1)

            def rwkv(l):
                for c in range(2):
                    s_ = slice(256 * c, 256 * c + 256)
                    ts(tmp(0)[:, s_], pt(D_K)[:, s_], pc("rwkv_k_k", l, c), ALU.mult).then_inc(S("rk_kk"), 1 if c else 0)
                for c in range(2):
                    s_ = slice(256 * c, 256 * c + 256)
                    ts(tmp(2)[:, s_], pt(D_W)[:, s_], -1.0, ALU.add, pc("rwkv_k_a", l, c), ALU.mult)
                stt(pt(D_K), tmp(2), 1.0, pt(D_K), ALU.add, ALU.mult)
                ts(pt(C_X), pt(C_X), -float(np.exp(-0.5)), ALU.mult)
                one = ones
                for i in range(4):
                    s_ = slice(P * i, P * i + P)
                    chain.link(lambda: V.tensor_tensor_scan(tmp(3)[:, s_], one, pt(C_X)[:, s_], 0.0, ALU.mult, ALU.add))
                ts(col(ST_NC0, 4).unsqueeze(2), many(tmp(3))[:, :, HD - 1:HD], -1.0, ALU.mult)
                tt(tmp(4), tmp(3), pt(C_X), ALU.subtract).then_inc(S("rk_b"), 1)
                dve.wait_ge(S("rk_rn"), l + 1)
                tt(tmp(0), tmp(0), tmp(1), ALU.mult)
                tt(tmp(2), tmp(0), pt(D_W), ALU.mult)
                dve.wait_ge(S("rk_e"), 2 * (l + 1))
                tt(pt(A_I), pt(D_R), tmp(5), ALU.mult)
                tt(pt(A_G), pt(D_K), tmp(6), ALU.mult)
                tt(pt(B_Q), tmp(2), tmp(6), ALU.mult)
                tt(pt(B_K), tmp(0), tmp(7), ALU.mult)
                for o, f0, f1, e1 in ((pt(B_V), pt(D_K), pt(D_R), pt(A_Q)), (pt(B_Z), tmp(2), tmp(0), pt(A_F))):
                    tt(cm(o)[:, :, 0:P], cm(f0)[:, :, 0:P], cm(pt(A_Q))[:, :, 0:P], ALU.mult)
                    tt(cm(o)[:, :, P:], cm(f1)[:, :, P:], cm(e1)[:, :, P:], ALU.mult)
                tt(tmp(2), pt(D_R), pt(D_K), ALU.mult)
                for c in range(2):
                    s_ = slice(256 * c, 256 * c + 256)
                    ts(tmp(2)[:, s_], tmp(2)[:, s_], pc("rwkv_r_k", l, c), ALU.mult).then_inc(S("rk_ops"), 1 if c else 0)
                dve.wait_ge(S("rk_sc"), l + 1)
                for bank, dst, mask in ((0, mt(3), strict), (2, mt(1), strict), (4, mt(2), incl), (6, PT[:, 0:1024], incl)):
                    stt(many(dst, 8), many(ps[:, bank:bank + 2, :].rearrange("p b n -> p (b n)"), 8), 1e30, rep(mask, 8),
                        ALU.min, ALU.mult).then_inc(S("inv_n"), 1 if bank == 6 else 0)
                inverse(2 * l + 1)
                dve.wait_ge(S("state"), 3 * l + 3)
                tt(tmp(3)[:, 0:256].rearrange("p (c n) -> p c n", c=2), ps[:, 5, 0:256].rearrange("p (c n) -> p c n", c=2),
                   rep(bdones, 2), ALU.mult).then_inc(S("state_bd"), 1)
                dve.wait_ge(S("rk_mean"), l + 1)
                stt(tmp(0), ps[:, 1, :], -1.0 / HD, tmp(0), ALU.mult, ALU.add).then_inc(S("rk_yc"), 1)
                dve.wait_ge(S("rk_bonus"), l + 1)
                tt(tmp(2), ps[:, 3, :], pt(D_V), ALU.mult)
                dve.wait_ge(S("rk_grn"), l + 1)
                tt(tmp(0), tmp(0), tmp(1), ALU.mult)
                for c in range(2):
                    s_ = slice(256 * c, 256 * c + 256)
                    ts(tmp(0)[:, s_], tmp(0)[:, s_], pc("rwkv_ln_w", l, c), ALU.mult, pc("rwkv_ln_b", l, c), ALU.add)
                tt(tmp(0), tmp(0), tmp(2), ALU.add)
                tt(tmp(0), tmp(0), H(12), ALU.mult).then_inc(S("mix_done"), 1)
                put(3, tmp(0))

            def attention(l):
                cm_steps(first_chunk["xattn_wk", l], 8)
                norm(2 + 3 * l, x, lambda c: pc("norm_xattn", l, c), hT)
                cm_steps(first_chunk["xattn_wq", l], 4)
                for b in range(4):
                    dve.wait_ge(S("at_s"), 4 * l + b + 1)
                    chain.link(lambda: V.tensor_reduce(col(ST_MX + 2 * b, 2), ps[:, b, :].rearrange("p (h n) -> p h n", h=2), AX, ALU.max))
                    ts(col(ST_MX + 2 * b, 2), col(ST_MX + 2 * b, 2), -1.0, ALU.mult).then_inc(S("at_max"), 1)
                dve.wait_ge(S("at_exp"), 8 * (l + 1))
                chain.link(lambda: V.reciprocal(col(ST_RS, 8), col(ST_SUM, 8)))
                for i in range(8):
                    ts(pr[:, i // NH, i % NH, :], pr[:, i // NH, i % NH, :], col(ST_RS + i), ALU.mult).then_inc(S("at_p"), 1)
                for b in range(4):
                    dve.wait_ge(S("at_hi"), 4 * l + b + 1)
                    o = [yT[i][:, 2 * b:2 * b + 2, :].rearrange("p c n -> p (c n)") for i in range(2)]
                    tt(o[1], ps[:, b, :], o[0].bitcast(F32), ALU.subtract).then_inc(S("at_lo"), 1)
                tm_add(first_chunk["xattn_wo", l], 4)

            def swiglu():
                norm(3, x, lambda c: pc("norm_ffn", 0, c), hT)
                for j in range(FSTEPS):
                    n = ff_chunk(j)
                    ahead(n + SPL)
                    dve.wait_ge(S("ff_silu"), j + 1)
                    dve.wait_ge(S("chunk_done"), n + 2)
                    m = mt(1)[:, 512 * (j % 2):512 * (j % 2) + 512]
                    tt(m, mt(0)[:, 0:512], ps[:, 2 * (j % 2) + 1, :], ALU.mult).then_inc(S("ff_prod"), 1)
                    ahead(n + 1 + SPL)
                    dve.wait_ge(S("ff_hi"), j + 1)
                    tt(actT[j % 2][1], m, actT[j % 2][0].bitcast(F32), ALU.subtract).then_inc(S("ff_lo"), 1)
                tm_add(ff_down(FSTEPS - 1), 1)

            def experts():
                norm(6, x, lambda c: pc("norm_ffn", 1, c), hT)
                dve.wait_ge(S("rt_mm"), 1)
                lg, sel, gate, rank = (col(a_, 16).rearrange("p (t n) -> p t n", t=2) for a_ in (ST_LG, ST_SEL, ST_GATE, ST_RANK))
                iota8 = con[:, C_IOTA:C_IOTA + 8]
                chain.link(lambda: V.tensor_copy(col(ST_LG, 16), ps[:, 0, 0:16]))
                for t in range(TT):
                    top, idx, idf = col(ST_TOP, 8), mt(5)[:, 8 * t:8 * t + 8].bitcast(U32), mt(5)[:, 16 + 8 * t:24 + 8 * t]
                    chain.link(lambda: V.max(top, lg[:, t, :]))
                    chain.link(lambda: V.max_index(idx, top, lg[:, t, :]))
                    chain.link(lambda: V.tensor_copy(idf, idx))
                    tt(col(ST_W + 2 * t), col(ST_TOP), col(ST_TOP + 1), ALU.subtract)
                    ts(col(ST_W + 2 * t + 1), col(ST_W + 2 * t), -1.0, ALU.mult).then_inc(S("rt_d"), 1 if t else 0)
                dve.wait_ge(S("rt_p"), 1)
                for t in range(TT):
                    idf = mt(5)[:, 16 + 8 * t:24 + 8 * t]
                    o = mt(5)[:, 32:48]
                    for k in range(2):
                        ts(o[:, 8 * k:8 * k + 8], iota8, idf[:, k:k + 1], ALU.is_equal)
                    tt(sel[:, t, :], o[:, 0:8], o[:, 8:16], ALU.add)
                    ts(o[:, 0:8], o[:, 0:8], col(ST_W + 2 * t), ALU.mult)
                    stt(gate[:, t, :], o[:, 8:16], col(ST_W + 2 * t + 1), o[:, 0:8], ALU.mult, ALU.add).then_inc(S("rt_d"), 1 if t else 0)
                dve.wait_ge(S("rt_mm"), 2)
                stt(col(ST_RANK, 16), ps[:, 1, 0:16], 1.0, col(ST_SEL, 16), ALU.add, ALU.mult)
                ts(col(ST_RANK, 16), col(ST_RANK, 16), -1.0, ALU.add)
                chain.link(lambda: V.tensor_copy(col(ST_TOTAL, NE), ps[:, 1, 16:16 + NE]))
                ts(col(ST_OVER, NE), iota8, -1.0, ALU.mult, float(NE), ALU.add)
                stt(col(ST_OVER, NE), col(ST_TOTAL, NE), float(P), col(ST_OVER, NE), ALU.is_gt, ALU.mult)
                chain.link(lambda: V.max(col(ST_TOTAL, NE), col(ST_OVER, NE)))
                ts(col(ST_OVER, NE), col(ST_TOTAL, NE), 0.0, ALU.is_gt)
                chain.link(lambda: V.tensor_reduce(col(ST_N1), col(ST_OVER, NE), AX, ALU.add))
                ts(col(ST_N1), col(ST_N1), float(NE), ALU.add)
                chain.link(lambda: V.tensor_copy(pass_count, col(ST_N1)))
                ts(col(ST_TOTAL, NE), col(ST_TOTAL, NE), -1.0, ALU.mult, float(NE), ALU.add)
                chain.link(lambda: V.memset(col(ST_BASE, NE), 0.0))
                chain.link(lambda: V.memset(col(ST_BASE + NE, NE), float(P)))
                chain.link(lambda: V.tensor_copy(pass_expert[:, 0:NE], iota8))
                chain.link(lambda: V.tensor_copy(pass_expert[:, NE:2 * NE], col(ST_TOTAL, NE)))
                ts(col(ST_TOTAL, NE), col(ST_TOTAL, NE), float(NE - 1), ALU.min)
                chain.link(lambda: V.tensor_copy(gather_expert[:, 0:NE], iota8))
                chain.link(lambda: V.tensor_copy(gather_expert[:, NE:2 * NE], col(ST_TOTAL, NE))).then_inc(S("ex_table"), 1)
                chain.link(lambda: V.memset(col(6), 0.0)).then_inc(S("ex_prod"), 1)
                chain.link(lambda: V.memset(col(6), 0.0)).then_inc(S("ex_alo"), 1)
                chain.link(lambda: V.memset(onehT, 0.0)).then_inc(S("ex_selT"), 1)
                chain.link(lambda: V.memset(yE, 0.0)).then_inc(S("ex_add"), 1)

                def chunk(h, m, q):
                    slot = ex_slot(q)
                    dve.wait_ge(S("w_hi"), ex_count(h * 2 + m, q))
                    V.tensor_tensor(wlo[slot][:, :], ex_raw[ex_raw_slot(m, q)], whi[slot][:, :].bitcast(F32),
                                    ALU.subtract).then_inc(S("w_lo"), 1)

                def prod(s, up_done):
                    dve.wait_ge(S("ex_silu"), s + 1)
                    dve.wait_ge(S("chunk_done"), up_done)
                    dve.wait_ge(S("ex_tr"), s + 1)
                    V.tensor_tensor(mt(1)[:, 0:256], mt(0)[:, 0:256], ps[:, 1, 0:256], ALU.mult).then_inc(S("ex_prod"), 1)

                def act_lo(s):
                    dve.wait_ge(S("ex_ahi"), s + 1)
                    V.tensor_tensor(actT[0][1][:, 0:256], ps[:, 2, 0:256], actT[0][0][:, 0:256].bitcast(F32),
                                    ALU.subtract).then_inc(S("ex_alo"), 1)

                def one_hots(p):
                    expert = dve.value_load(gather_expert[0:1, bass.ds(p, 1)], min_val=0, max_val=NE - 1)
                    for t in range(TT):
                        rk = col(ST_RANK + 8 * t, 8)[:, bass.ds(expert, 1)]
                        gt = col(ST_GATE + 8 * t, 8)[:, bass.ds(expert, 1)]
                        o, og = oneh[:, P * t:P * t + P], onehg[:, P * t:P * t + P]
                        V.tensor_scalar(o, con[:, C_IOTA:C_IOTA + P], col(ST_BASE, 16)[:, bass.ds(p, 1)], rk,
                                        ALU.add, ALU.is_equal).then_inc(S("ex_one"), 1)
                        dve.wait_ge(S("ex_one"), p * 2 + (t + 1))
                        V.tensor_scalar(og, o, gt, None, ALU.mult).then_inc(S("ex_sel"), 1)

                def gathered(p, cs):
                    for c in cs:
                        dve.wait_ge(S("ex_hi"), p * KT + (KT // 2 if c < KT // 2 else KT))
                        V.scalar_tensor_tensor(out=hE[1][:, c, :], in0=g_tokens(c), scalar=pc("norm_ffn", 1, c),
                                               in1=hE[0][:, c, :].bitcast(F32), op0=ALU.mult, op1=ALU.subtract).then_inc(S("ex_hlo"), 1)

                def scattered(q, hf):
                    for t in range(TT):
                        dve.wait_ge(S("ex_sc"), q * 4 + (2 * hf + t + 1))
                        s_ = slice(512 * hf, 512 * hf + 512)
                        V.tensor_tensor(x[:, t, s_], x[:, t, s_], ps[:, 6 + t, :], ALU.add).then_inc(S("ex_x"), 1)

                chain.settle()
                dve.wait_ge(S("ex_table"), 1)
                count = dve.value_load(pass_count[0:1, 0:1], min_val=NE, max_val=NE + SECONDS)
                one_hots(0)
                gathered(0, range(KT))
                with dve.Fori(0, NE + SECONDS) as ep:
                    which = dve.value_load(pass_expert[0:1, bass.ds(ep, 1)], min_val=0, max_val=NE)
                    with dve.If(which < NE):
                        h = ep * (ESTEPS // 2)
                        r = ep * ESTEPS
                        chunk(h, 0, 0)
                        chunk(h, 0, 1)
                        chunk(h, 0, 2)
                        prod(r, ex_count(r, 1))
                        scattered(ep, 0)
                        chunk(h, 0, 3)
                        act_lo(r)
                        scattered(ep, 1)
                        chunk(h, 0, 4)
                        dve.wait_ge(S("ex_x"), ep * 4 + 4)
                        V.memset(col(6), 0.0).then_inc(S("ex_add"), 1)
                        dve.wait_ge(S("ex_gt"), ep + 1)
                        V.tensor_copy(onehT, ps[:, 3, 0:256]).then_inc(S("ex_selT"), 1)
                        one_hots(ep + 1)
                        with dve.Fori(0, (ESTEPS - 2) // 2) as i:
                            for m in (1, 2):
                                chunk(h + i, m, 2)
                                prod(r + i * 2 + m, ex_count(r + i * 2 + (m - 1), 3))
                                chunk(h + i, m, 3)
                                act_lo(r + i * 2 + m)
                                chunk(h + i, m, 4)
                        chunk(h, ESTEPS - 1, 2)
                        prod(r + (ESTEPS - 1), ex_count(r + (ESTEPS - 2), 3))
                        gathered(ep + 1, range(KT // 2))
                        act_lo(r + (ESTEPS - 1))
                        gathered(ep + 1, range(KT // 2, KT))
                for hf in range(2):
                    scattered(count, hf)
                dve.wait_ge(S("ex_x"), count * 4 + 4)

            chain.link(lambda: V.memset(col(10), 1.0))
            chain.link(lambda: V.memset(col(8), EPS))
            chain.link(lambda: V.memset(col(9), GN_EPS)).then_inc(S("eps"), 1)
            ahead(SPL)
            dve.wait_ge(S("tables_in"), 48)
            dve.wait_ge(S("tables_in"), 48)
            split_small(0)
            dve.wait_ge(S("mem_in"), 16)
            norm(0, mem, lambda c: pc("mem_norm", None, c), memT)
            for l in range(DEPTH):
                norm(1 + 3 * l, x, lambda c: pc("norm_mix", l, c), hT)
                cm_steps(first_chunk["w_in", l], 14)
                gates(l)
                logs(l)
                rglru(l)
                hgrn(l)
                deltanet(l)
                rwkv(l)
                split_small(l + 1)
                tm_add(first_chunk["w_out", l], 4)
                attention(l)
                if l == 0:
                    swiglu()
            experts()
            chain.link(lambda: V.memset(col(7), 0.0)).then_inc(S("x_done"), 1)
            dve.wait_ge(S("n_rstd"), 8)
            for t in range(TT):
                ts(x[:, t, :], x[:, t, :], col(t), ALU.mult)
            dve.wait_ge(S("nf_in"), 16)
            for t in range(TT):
                tt(x[:, t, :], x[:, t, :], final_gain, ALU.mult).then_inc(S("x_done"), 1 if t else 0)

        @block.tensor
        def _(pe):
            cmi = [0]

            def mm(o, lhsT, rhs, start=True, stop=True):
                return Signalled(pe.matmul(o, lhsT, rhs, start=start, stop=stop, skip_group_check=True))

            def tr(o, i):
                return Signalled(pe.transpose(o, i, ident))

            PASSES = ((0, 0), (1, 0), (0, 1))

            def cm_product(n, src, bank):
                pe.wait_ge(S("w_lo"), n + 1)
                wp = [chunk_view(v[n % SPL][:, :], "cm") for v in (whi, wlo)]
                for m in range(2):
                    for i, (a_, b_) in enumerate(PASSES):
                        for k in range(KT):
                            last = i == 2 and k == KT - 1
                            ins = pe.matmul(ps[:, bank, SEQ * m:SEQ * m + SEQ], wp[a_][:, k, P * m:P * m + P], src[b_][:, k, :],
                                            start=i == 0 and k == 0, stop=last)
                ins.then_inc(S("chunk_done"), 1)

            def cm_phase(n0, count, src):
                for j in range(count):
                    if cmi[0] >= 4:
                        pe.wait_ge(S("cm_free"), cmi[0] - 3)
                    cm_product(n0 + j, src, cmi[0] % 4)
                    cmi[0] += 1

            def tm_product(n, src, first, last):
                pe.wait_ge(S("w_lo"), n + 1)
                wp = [chunk_view(v[n % SPL][:, :], "tm") for v in (whi, wlo)]
                for kk in range(TM_ROWS):
                    for t in range(TT):
                        for hf in range(2):
                            for i, (a_, b_) in enumerate(PASSES):
                                ins = pe.matmul(ps[:, 4 + 2 * t + hf, :], src(b_, kk, t), wp[a_][:, kk, 512 * hf:512 * hf + 512],
                                                start=first and kk == 0 and i == 0, stop=last and kk == TM_ROWS - 1 and i == 2)
                ins.then_inc(S("chunk_done"), 1)

            def tm_phase(n0, src):
                for j in range(4):
                    tm_product(n0 + j, lambda b_, kk, t: src[b_][:, TM_ROWS * j + kk, P * t:P * t + P], j == 0, j == 3)

            def norm(i):
                pe.wait_ge(S("n_xs"), 2 * (i + 1))
                for c in range(KT):
                    for t in range(TT):
                        tr(ps[:, c, P * t:P * t + P], xs[:, t, P * c:P * c + P]).then_inc(S("n_tr"), 1 if t else 0)
                pe.wait_ge(S("n_lo"), (i + 1) * KT)

            def small_product(bank, k):
                pe.wait_ge(S("wsm_split"), k + 1)
                for t in range(TT):
                    for i, (a_, b_) in enumerate(PASSES):
                        for kk in range(KT):
                            ins = pe.matmul(ps[:, bank, 8 * t:8 * t + 8], hT[b_][:, kk, P * t:P * t + P], small[a_][:, kk, :],
                                            start=i == 0 and kk == 0, stop=i == 2 and kk == KT - 1)
                return ins

            def gates(l):
                pe.wait_ge(S("conv_l"), l + 1)
                pe.wait_ge(S("cm_free"), cmi[0])
                for c in range(2):
                    for g in range(2):
                        mm(ps[:, g, 256 * c:256 * c + 256], sw[:, SW_LRU + P * (2 * g + c):SW_LRU + P * (2 * g + c + 1)],
                           H(6)[:, 256 * c:256 * c + 256]).then_inc(S("lru_mm"), 1 if c and g else 0)
                pe.wait_ge(S("lora_in"), l + 1)
                for c in range(2):
                    mm(ps[:, 2, 256 * c:256 * c + 256], sw[0:64, SW_WA + P * c:SW_WA + P * c + P], pt(D_W, 1)[0:64, :])
                for c in range(2):
                    mm(ps[:, 3, 256 * c:256 * c + 256], sw[64:128, SW_WA + P * c:SW_WA + P * c + P], pt(D_W, 1)[64:128, :])
                for c in range(2):
                    mm(ps[:, 4, 256 * c:256 * c + 256], sw[:, SW_G2 + P * c:SW_G2 + P * c + P], pt(D_G, 1)).then_inc(S("lora_mm"), 1 if c else 0)
                if l:
                    for c in range(2):
                        mm(ps[0:32, 5, 0:256], sw[:, SW_V1 + 32 * c:SW_V1 + 32 * c + 32], pt(D_V + c, 1), start=c == 0, stop=c == 1).then_inc(S("vmix_mm"), 1 if c else 0)
                    pe.wait_ge(S("vmix1"), 1)
                    for c in range(2):
                        mm(ps[:, 6, 256 * c:256 * c + 256], sw[0:32, SW_V2 + P * c:SW_V2 + P * c + P], H(13)[0:32, 0:256]).then_inc(S("vmix_mm"), 1 if c else 0)

            def scores(bank, k_, q_):
                for p_ in range(2):
                    for t in range(TT):
                        for c in range(2):
                            s_ = slice(256 * c + P * t, 256 * c + P * t + P)
                            a_ = at(0, t, c)
                            last = mm(ps[:, bank + p_, a_:a_ + P], k_[64 * p_:64 * p_ + 64, s_], q_[64 * p_:64 * p_ + 64, s_])
                return last

            def hgrn(l):
                pe.wait_ge(S("lora_s"), l + 1)
                if l:
                    pe.wait_ge(S("vmix2"), 2)
                for t in range(TT):
                    for c in range(2):
                        last = t == 1 and c == 1
                        tr(ps[:, 4, 256 * t + P * c:256 * t + P * c + P], pt(A_I + c, 1)[:, P * t:P * t + P]).then_inc(S("hg_tr"), 1 if last else 0)
                pe.wait_ge(S("s_kA"), l + 1)
                pe.wait_ge(S("hg_b"), l + 1)
                scores(0, tmp(0), pt(A_Q)).then_inc(S("hg_s"), 1)
                for v in range(LEVELS):
                    pe.wait_ge(S("hg_qk"), l * LEVELS + v + 1)
                    if v:
                        pe.wait_ge(S("hg_take"), l * (LEVELS + 1) + v)
                    scores(2 * ((v + 1) % 2), H(v % 2), H(4 + v % 2)).then_inc(S("hg_s"), 1)
                pe.wait_ge(S("hg_x"), l + 1)
                for c in range(2):
                    tr(ps[:, 5, P * c:P * c + P], H(0)[:, P * c:P * c + P]).then_inc(S("hg_trk"), 1 if c else 0)
                pe.wait_ge(S("hg_v"), l + 1)
                pe.wait_ge(S("hg_kd"), l + 1)
                for c in range(2):
                    mm(ps[:, 6, P * c:P * c + P], tmp(5)[:, P * c:P * c + P], tmp(1)[:, P * c:P * c + P]).then_inc(S("state"), 1 if c else 0)
                pe.wait_ge(S("state_bd"), 3 * l + 1)
                outputs(7, [(tmp(1), mt(1))], tmp(5)[:, 256:512], H(4)).then_inc(S("o_full"), 1)
                head_ss(l, 0)

            def outputs(bank, pairs, state, q_):
                for c in range(2):
                    for t in range(TT):
                        o_ = 256 * c + P * t
                        if t:
                            mm(ps[:, bank, o_:o_ + P], state[:, P * c:P * c + P], q_[:, 256 * c + P:256 * c + 256], stop=False)
                        for i, (v_, s_) in enumerate(pairs):
                            for p_ in range(2):
                                last = mm(ps[64 * p_:64 * p_ + 64, bank, o_:o_ + P],
                                   v_[:, 256 * t + P * c + 64 * p_:256 * t + P * c + 64 * p_ + 64],
                                   s_[:, at(p_, t, c):at(p_, t, c) + P], start=t == 0 and i == 0, stop=i == len(pairs) - 1)
                return last

            def head_ss(l, which):
                pe.wait_ge(S("o_sq"), 2 * l + which + 1)
                mm(ps[:, 6, :], bdones, tmp(6)).then_inc(S("o_ss"), 1)

            def inverse(i):
                N, X, Y, T1 = mt(3), mt(4), mt(5), mt(0)
                pe.wait_ge(S("inv_n"), i + 1)
                for v in range(LEVELS):
                    for g in range(2):
                        if v:
                            pe.wait_ge(S("inv_xy"), 2 * (LEVELS * i + v - 1) + g + 1)
                        for k in range(4):
                            s_ = slice(512 * g + P * k, 512 * g + P * k + P)
                            mm(ps[:, g, P * k:P * k + P], N[:, s_], X[:, s_] if v else ident).then_inc(S("inv_t"), 1 if k == 3 else 0)
                    if v:
                        for g in range(2):
                            pe.wait_ge(S("inv_t1"), 2 * ((LEVELS - 1) * i + v - 1) + g + 1)
                            for k in range(4):
                                s_ = slice(512 * g + P * k, 512 * g + P * k + P)
                                if v < LEVELS - 1:
                                    mm(ps[:, 2 + g, P * k:P * k + P], Y[:, s_], T1[:, s_])
                                mm(ps[:, 4 + g, P * k:P * k + P], T1[:, s_], Y[:, s_]).then_inc(S("inv_p"), 1 if k == 3 else 0)
                pe.wait_ge(S("inv_xy"), 2 * LEVELS * (i + 1))

            def solve(bank, t, r_):
                for h in range(NH):
                    a_ = at(h % 2, t, h // 2)
                    last = mm(ps[:, bank, 256 * t + HD * h:256 * t + HD * h + HD], mt(5)[:, a_:a_ + P], r_[:, 256 * t + HD * h:256 * t + HD * h + HD])
                return last

            def deltanet(l):
                pe.wait_ge(S("gd_sq"), l + 1)
                for j in range(2):
                    mm(ps[:, 2 + j, :], bdones, H(j)).then_inc(S("gd_ss"), 1 if j else 0)
                pe.wait_ge(S("gd_g"), l + 1)
                g8 = col(ST_G, 8)
                mm(ps[:, 5, 0:8], incl, g8)
                mm(ps[:, 5, 8:16], ones, g8)
                pe.wait_ge(S("gd_rn"), 2 * (l + 1))
                pe.wait_ge(S("gd_wide"), l + 1)
                for p_ in range(2):
                    for t in range(TT):
                        for c in range(2):
                            a_ = at(0, t, c)
                            k = ST_G + 4 * t + 2 * c + p_
                            mm(ps[:, p_, a_:a_ + P], col(k).to_broadcast([P, P]), incl)
                for c in range(2):
                    for t in range(TT):
                        o_ = 256 * c + P * t
                        w_ = 256 * t + P * c
                        mm(ps[:, 4, o_:o_ + P], tmp(6)[:, w_:w_ + P], incl)
                        mm(ps[:, 3, o_:o_ + P], tmp(7)[:, w_:w_ + P], ident).then_inc(S("gd_cum"), 1 if c and t else 0)
                pe.wait_ge(S("gd_gd"), l + 1)
                pe.wait_ge(S("gd_ops"), l + 1)
                for c in range(2):
                    tr(ps[:, 4, P * c:P * c + P], pt(B_K + c, 1)[:, 0:P])
                for t in range(TT):
                    for c in range(2):
                        tr(ps[:, 5, 256 * t + P * c:256 * t + P * c + P], pt(B_V + c, 1)[:, P * t:P * t + P]).then_inc(S("gd_trk"), 1 if t and c else 0)
                scores(2, pt(B_K), pt(B_Q))
                scores(6, pt(B_K), tmp(1)).then_inc(S("gd_sc"), 1)
                inverse(2 * l)
                solve(6, 0, tmp(4)).then_inc(S("gd_u"), 1)
                pe.wait_ge(S("gd_us"), 2 * l + 1)
                for c in range(2):
                    mm(ps[:, 7, P * c:P * c + P], tmp(3)[:, P * c:P * c + P], tmp(6)[:, P * c:P * c + P]).then_inc(S("state"), 1 if c else 0)
                pe.wait_ge(S("state_bd"), 3 * l + 2)
                for c in range(2):
                    mm(ps[:, 7, 256 + P * c:256 + P * c + P], tmp(2)[:, 256 * c + P:256 * c + 256], tmp(3)[:, 256 + P * c:256 + P * c + P]).then_inc(S("gd_km"), 1 if c else 0)
                pe.wait_ge(S("gd_r1"), l + 1)
                solve(6, 1, tmp(4)).then_inc(S("gd_u"), 1)
                pe.wait_ge(S("gd_us"), 2 * l + 2)
                outputs(0, [(tmp(6), mt(2))], tmp(3)[:, 256:512], tmp(0)).then_inc(S("o_full"), 1)
                head_ss(l, 1)

            def rwkv(l):
                pe.wait_ge(S("rk_sq"), l + 1)
                mm(ps[:, 2, :], bdones, tmp(1)).then_inc(S("rk_ss"), 1)
                pe.wait_ge(S("rk_ops"), l + 1)
                pe.wait_ge(S("y_put"), 4 * l + 3)
                scores(0, pt(B_Q), pt(B_K))
                scores(2, pt(A_G), pt(B_K))
                scores(4, pt(A_G), pt(A_I))
                scores(6, pt(B_Q), pt(A_I)).then_inc(S("rk_sc"), 1)
                pe.wait_ge(S("inv_n"), 2 * l + 2)
                for t in range(TT):
                    for c in range(2):
                        tr(ps[:, 6, 256 * t + P * c:256 * t + P * c + P], pt(D_V + c, 1)[:, P * t:P * t + P])
                for i, m_ in enumerate((B_V, B_Z)):
                    for c in range(2):
                        tr(ps[:, 7, 256 * i + P * c:256 * i + P * c + P], pt(m_ + c, 1)[:, 0:P]).then_inc(S("rk_trv"), 1 if i and c else 0)
                inverse(2 * l + 1)
                pe.wait_ge(S("rk_vk"), l + 1)

                def right_side(t):
                    for c in range(2):
                        o_ = 256 * t + P * c
                        if t:
                            mm(ps[:, 6, o_:o_ + P], pt(B_Z)[:, 256 * c + P:256 * c + 256], tmp(3)[:, P * c:P * c + P], stop=False)
                        for p_ in range(2):
                            mm(ps[:, 6, o_ + 64 * p_:o_ + 64 * p_ + 64], mt(1)[:, at(p_, t, c):at(p_, t, c) + P],
                               tmp(5)[:, o_ + 64 * p_:o_ + 64 * p_ + 64], start=t == 0).then_inc(S("rk_r"), 1 if c and p_ else 0)

                right_side(0)
                pe.wait_ge(S("rk_rs"), 2 * l + 1)
                solve(7, 0, tmp(7)).then_inc(S("rk_u"), 1)
                pe.wait_ge(S("rk_us"), 2 * l + 1)
                for c in range(2):
                    mm(ps[:, 5, P * c:P * c + P], tmp(6)[:, P * c:P * c + P], tmp(5)[:, P * c:P * c + P], stop=False)
                    mm(ps[:, 5, P * c:P * c + P], tmp(6)[:, 256 + P * c:256 + P * c + P], tmp(4)[:, P * c:P * c + P], start=False).then_inc(S("state"), 1 if c else 0)
                pe.wait_ge(S("state_bd"), 3 * l + 3)
                right_side(1)
                pe.wait_ge(S("rk_rs"), 2 * l + 2)
                solve(7, 1, tmp(7)).then_inc(S("rk_u"), 1)
                pe.wait_ge(S("rk_us"), 2 * l + 2)
                outputs(0, [(tmp(5), mt(2)), (tmp(4), PT[:, 0:1024])], tmp(3)[:, 0:256], pt(B_V)).then_inc(S("rk_o"), 1)
                pe.wait_ge(S("rk_y"), l + 1)
                mm(ps[:, 1, :], bdones, tmp(0)).then_inc(S("rk_mean"), 1)
                mm(ps[:, 3, :], bdones, tmp(2)).then_inc(S("rk_bonus"), 1)
                pe.wait_ge(S("rk_ysq"), l + 1)
                mm(ps[:, 2, :], bdones, tmp(1)).then_inc(S("rk_var"), 1)

            def attention(l):
                cm_phase(first_chunk["xattn_wk", l], 4, memT)
                pe.wait_ge(S("x_done"), 3 * l + 1)
                tm_phase(first_chunk["xattn_wv", l], memT)
                pe.wait_ge(S("at_v"), 4 * (l + 1))
                pe.wait_ge(S("cm_free"), cmi[0])
                norm(2 + 3 * l)
                cm_phase(first_chunk["xattn_wq", l], 4, hT)
                pe.wait_ge(S("cm_free"), cmi[0])
                for b in range(4):
                    for u in range(2):
                        t, h = b // 2, 2 * (b % 2) + u
                        for k in range(2):
                            mm(ps[:, b, 256 * u:256 * u + 256], qT[:, 2 * h + k, P * t:P * t + P], kT[:, 2 * h + k, :],
                               start=k == 0, stop=k == 1).then_inc(S("at_s"), 1 if u and k else 0)
                for b in range(4):
                    t, m = b // 2, b % 2
                    pe.wait_ge(S("at_p"), 8 * l + 4 * (t + 1))
                    for h in range(NH):
                        tr(ps[:, 4 + b, P * h:P * h + P], pr[:, t, h, P * m:P * m + P]).then_inc(S("at_tr"), 1 if h == 3 else 0)
                pe.wait_ge(S("at_prT"), 4 * (l + 1))
                for h in range(NH):
                    for k in range(2):
                        for m in range(2):
                            mm(ps[:, h, 256 * k:256 * k + 256], vA[:, m, 256 * h + P * k:256 * h + P * k + P], prT[:, m, h, :],
                               start=m == 0, stop=m == 1).then_inc(S("at_o"), 1 if k and m else 0)
                pe.wait_ge(S("at_lo"), 4 * (l + 1))
                tm_phase(first_chunk["xattn_wo", l], yT)

            def swiglu():
                pe.wait_ge(S("x_done"), 2)
                norm(3)
                for j in range(FSTEPS + 1):
                    if j < FSTEPS:
                        if j >= 2:
                            pe.wait_ge(S("ff_prod"), j - 1)
                        cm_product(ff_chunk(j), hT, 2 * (j % 2))
                        cm_product(ff_chunk(j) + 1, hT, 2 * (j % 2) + 1)
                    if j:
                        pe.wait_ge(S("ff_lo"), j)
                        av = [v.rearrange("p (k n) -> p k n", k=2) for v in actT[(j - 1) % 2]]
                        tm_product(ff_down(j - 1), lambda b_, kk, t: av[b_][:, kk, P * t:P * t + P], j == 1, j == FSTEPS)

            def experts():
                pe.wait_ge(S("x_done"), 5)
                norm(6)
                small_product(0, 2).then_inc(S("rt_mm"), 1)
                pe.wait_ge(S("rt_d"), 2)
                sel = col(ST_SEL, 16).rearrange("p (t n) -> p t n", t=2)
                mm(ps[:, 1, 0:8], strict, sel[:, 0, :])
                mm(ps[:, 1, 8:16], ones, sel[:, 0, :], stop=False)
                mm(ps[:, 1, 8:16], strict, sel[:, 1, :], start=False)
                mm(ps[:, 1, 16:24], ones, sel[:, 0, :], stop=False)
                mm(ps[:, 1, 16:24], ones, sel[:, 1, :], start=False).then_inc(S("rt_mm"), 1)
                pe.wait_ge(S("ex_add"), 1)
                for hf in range(2):
                    ins = mm(ps[:, 4 + hf, :], onehT[:, 0:P], yE[:, 512 * hf:512 * hf + 512])
                ins.then_inc(S("ex_tr"), 1)

                def product(s, q, bank):
                    pe.wait_ge(S("w_lo"), ex_count(s, q))
                    wp = [chunk_view(v[ex_slot(q)][:, :], "cm") for v in (whi, wlo)]
                    for i, (a_, b_) in enumerate(PASSES):
                        for k in range(KT):
                            ins = pe.matmul(ps[:, bank, 0:256], hE[b_][:, k, :], wp[a_][:, k, :], start=i == 0 and k == 0,
                                            stop=i == 2 and k == KT - 1)
                    ins.then_inc(S("chunk_done"), 1)

                def gate_up(s, s3, q):
                    pe.wait_ge(S("ex_prod"), s + 1)
                    product(s3, q, 0)
                    product(s3, q + 1, 1)

                def turn(s):
                    pe.wait_ge(S("ex_prod"), s + 2)
                    pe.wait_ge(S("ex_alo"), s + 1)
                    for k in range(2):
                        ins = pe.transpose(ps[:, 2, P * k:P * k + P], mt(1)[:, P * k:P * k + P], ident)
                    ins.then_inc(S("ex_tr"), 1)

                def down(s, s3, q, start):
                    pe.wait_ge(S("ex_alo"), s + 2)
                    pe.wait_ge(S("w_lo"), ex_count(s3, q))
                    wp = [chunk_view(v[ex_slot(q)][:, :], "tm") for v in (whi, wlo)]
                    for kk in range(TM_ROWS):
                        for hf in range(2):
                            for i, (a_, b_) in enumerate(PASSES):
                                ins = pe.matmul(ps[:, 4 + hf, :], actT[0][b_][:, P * kk:P * kk + P], wp[a_][:, kk, 512 * hf:512 * hf + 512],
                                                start=start and kk == 0 and i == 0, stop=True, skip_group_check=True)
                    ins.then_inc(S("chunk_done"), 1)

                def gather(p):
                    pe.wait_ge(S("ex_sel"), p * 2 + 2)
                    pe.wait_ge(S("ex_selT"), p + 1)
                    for t in range(TT):
                        ins = pe.transpose(ps[:, 3, P * t:P * t + P], onehg[:, P * t:P * t + P], ident)
                    ins.then_inc(S("ex_gt"), 1)
                    for c in range(KT):
                        for t in range(TT):
                            ins = pe.matmul(g_tokens(c), xs[:, t, P * c:P * c + P], oneh[:, P * t:P * t + P],
                                            start=t == 0, stop=t == 1)
                        if c % 4 == 3:
                            ins.then_inc(S("ex_g"), 1)

                def scatter(q, hf):
                    pe.wait_ge(S("ex_y"), q * 2 + (hf + 1))
                    if hf == 0:
                        pe.wait_ge(S("ex_selT"), q + 1)
                    for t in range(TT):
                        if hf:
                            pe.wait_ge(S("ex_x"), q * 4 + (t + 1))
                        pe.matmul(ps[:, 6 + t, :], onehT[:, P * t:P * t + P], yE[:, 512 * hf:512 * hf + 512],
                                  start=True, stop=True).then_inc(S("ex_sc"), 1)

                pe.wait_ge(S("ex_table"), 1)
                count = pe.value_load(pass_count[0:1, 0:1], min_val=NE, max_val=NE + SECONDS)
                gather(0)
                with pe.Fori(0, NE + SECONDS) as ep:
                    which = pe.value_load(pass_expert[0:1, bass.ds(ep, 1)], min_val=0, max_val=NE)
                    with pe.If(which < NE):
                        r = ep * ESTEPS
                        pe.wait_ge(S("ex_hlo"), ep * KT + KT)
                        gate_up(r, r, 0)
                        scatter(ep, 0)
                        turn(r)
                        scatter(ep, 1)
                        gate_up(r + 1, r, 2)
                        down(r, r, 4, True)
                        pe.wait_ge(S("ex_x"), ep * 4 + 4)
                        gather(ep + 1)
                        with pe.Fori(2, ESTEPS) as j:
                            turn(r + j - 1)
                            gate_up(r + j, r + j - 1, 2)
                            down(r + j - 1, r + j - 1, 4, False)
                        turn(r + (ESTEPS - 1))
                        down(r + (ESTEPS - 1), r + (ESTEPS - 1), 2, False)
                pe.wait_ge(S("ex_hlo"), count * KT + KT)
                for hf in range(2):
                    scatter(count, hf)

            pe.wait_ge(S("tables_in"), 48)
            norm(0)
            for l in range(DEPTH):
                norm(1 + 3 * l)
                cm_phase(first_chunk["w_in", l], 14, hT)
                small_product(7, l).then_inc(S("ab_mm"), 1)
                pe.wait_ge(S("sw_in"), 16 * (l + 1))
                gates(l)
                hgrn(l)
                deltanet(l)
                rwkv(l)
                pe.wait_ge(S("y_put"), 4 * (l + 1))
                tm_phase(first_chunk["w_out", l], yT)
                attention(l)
                if l == 0:
                    swiglu()
            experts()


BIG = ["x", "mem", "w_in", "w_out", "xattn_wq", "xattn_wk", "xattn_wv", "xattn_wo", "ffn_w_gate", "ffn_w_up",
       "ffn_w_down", "moe_router", "moe_w_gate", "moe_w_up", "moe_w_down"]


def lay_out_params(v):
    out = np.zeros((P, NPAR), np.float32)

    def put(key, a):
        at, n = PCOL[key]
        out[:, at:at + n] = a

    for layer in range(DEPTH):
        for name in ("norm_mix", "norm_xattn", "norm_ffn", "hgrn_norm", "lru_conv_b", "lru_ba", "lru_bx", "lru_lambda",
                     "rwkv_mu", "rwkv_w0", "rwkv_a0", "rwkv_k_k", "rwkv_k_a", "rwkv_r_k", "rwkv_ln_w", "rwkv_ln_b"):
            put((name, layer), v[name][layer].reshape(-1, P).T)
        for name in ("gdn_conv_w", "lru_conv_w"):
            put((name, layer), v[name][layer].reshape(-1, P).T)
        for name in ("gdn_A_log", "gdn_dt_bias"):
            put((name, layer), np.broadcast_to(v[name][layer], (P, NH)))
        put(("gdn_norm", layer), np.tile(v["gdn_norm"][layer], 2)[:, None])
        put(f"lb{layer}", v["hgrn_lb_logits"][layer].reshape(-1, P).T)
    put("rwkv_v0", v["rwkv_v0"][0].reshape(-1, P).T)
    put("mem_norm", v["mem_norm"].reshape(-1, P).T)
    return out


def lay_out_small(v):
    out = np.zeros((DEPTH, P, NSW), np.float32)
    for layer in range(DEPTH):
        for g, name in enumerate(("lru_wa", "lru_wx")):
            for n in range(4):
                a = SW_LRU + P * (2 * g + n // 2) + HD * (n % 2)
                out[layer, HD * (n % 2):HD * (n % 2) + HD, a:a + HD] = v[name][layer, n]
        out[layer, 0:64, SW_WA:SW_WA + GROUP] = v["rwkv_w2"][layer]
        out[layer, 64:128, SW_WA:SW_WA + GROUP] = v["rwkv_a2"][layer]
        out[layer, :, SW_G2:SW_G2 + GROUP] = v["rwkv_g2"][layer]
    out[1, :, SW_V1:SW_V1 + 64] = v["rwkv_v1"][0].reshape(2, P, 32).transpose(1, 0, 2).reshape(P, 64)
    out[1, 0:32, SW_V2:SW_V2 + GROUP] = v["rwkv_v2"][0]
    return out


def constant_tables():
    i = np.arange(P)
    out = np.zeros((P, NCON), np.float32)
    out[:, C_ID:C_ID + P] = np.eye(P)
    out[:, C_INCL:C_INCL + P] = i[:, None] <= i[None]
    out[:, C_STRICT:C_STRICT + P] = i[:, None] < i[None]
    out[:, C_BD:C_BD + P] = i[:, None] // HD == i[None] // HD
    out[:, C_IOTA:C_IOTA + P] = i[None]
    level = np.zeros((2, LEVELS, P, P), np.float32)
    for v in range(LEVELS):
        h = 1 << v
        left, right = (i // h) % 2 == 0, (i // h) % 2 == 1
        m = (i[:, None] // (2 * h) == i[None] // (2 * h)) & left[:, None] & right[None]
        level[0, v], level[1, v] = m, m.T
    return out, level.transpose(2, 0, 1, 3).reshape(P, 2 * LEVELS * P)


def kernel(**inputs):
    import concourse.bacc as bacc
    from concourse.bass_utils import run_bass_kernel_spmd

    v = {k: np.asarray(a) for k, a in inputs.items()}
    nc = bacc.Bacc("TRN2", target_bir_lowering=False, num_devices=1)
    con, level = constant_tables()
    arrays = {k: np.ascontiguousarray(v[k]) for k in BIG}
    arrays["params"] = lay_out_params(v)
    arrays["small_w"] = lay_out_small(v)
    arrays["norm_final"] = np.ascontiguousarray(np.broadcast_to(v["norm_final"], (P, D)))
    arrays["consts"] = con
    arrays["level_masks"] = level.astype(mybir.dt.np(mybir.dt.bfloat16))
    aps = {k: nc.dram_tensor(f"in_{k}", a.shape, mybir.dt.from_np(a.dtype), kind="ExternalInput").ap() for k, a in arrays.items()}
    out = nc.dram_tensor("out_0", (1, SEQ, D), F32, kind="ExternalOutput").ap()
    build(nc, aps, out)
    r = run_bass_kernel_spmd(nc, [{f"in_{k}": a for k, a in arrays.items()}], core_ids=[0])
    return r.results[0]["out_0"]
```

```python
from contextlib import ExitStack

import numpy as np

import concourse.bass as bass
from concourse import mybir

P = 128
D = 1024
KT = D // P
SEQ = 256
TT = SEQ // P
DEPTH = 2
GROUP = 256
HD = 64
NH = 4
LEVELS = 7
D_FF = 2816
D_FFE = 3584
NE = 8
CH = 2048
CM_COLS = CH // KT
TM_ROWS = CH // D
EPS = 1e-6
GN_EPS = 64e-5
RAW = 3
SPL = 3

F32 = mybir.dt.float32
F32R = mybir.dt.float32r
I32 = mybir.dt.int32
U32 = mybir.dt.uint32
ACT = mybir.ActivationFunctionType
ALU = mybir.AluOpType
AX = mybir.AxisListType.X

A_Q, A_F, A_I, A_G, B_Q, B_K, B_V, B_Z, C_X, C_G, D_R, D_K, D_V, D_W, D_G = 0, 2, 4, 6, 8, 10, 12, 14, 16, 18, 20, 22, 24, 26, 27
GDN_AB = 2048
W_IN_PARTS = [B_Q, B_K, B_V, C_X, D_R, D_K, D_V, D_W, C_G, A_F, A_G, B_Z, A_I, A_Q]
W_IN_COLS = [P * m + (8 if m >= C_X else 0) for m in W_IN_PARTS]


def param_columns():
    sizes = [("norm_mix", 8), ("norm_xattn", 8), ("norm_ffn", 8), ("hgrn_norm", 2), ("gdn_conv_w", 24),
             ("gdn_A_log", 4), ("gdn_dt_bias", 4), ("gdn_norm", 1), ("lru_conv_w", 8), ("lru_conv_b", 2),
             ("lru_ba", 2), ("lru_bx", 2), ("lru_lambda", 2), ("rwkv_mu", 8), ("rwkv_w0", 2), ("rwkv_a0", 2),
             ("rwkv_k_k", 2), ("rwkv_k_a", 2), ("rwkv_r_k", 2), ("rwkv_ln_w", 2), ("rwkv_ln_b", 2)]
    at, out = 0, {}
    for layer in range(DEPTH):
        for name, n in sizes:
            out[name, layer] = (at, n)
            at += n
    for name, n in (("lb0", 2), ("lb1", 2), ("rwkv_v0", 2), ("mem_norm", 8)):
        out[name] = (at, n)
        at += n
    return out, at


PCOL, NPAR = param_columns()
C_ID, C_INCL, C_STRICT, C_BD, C_IOTA = (P * i for i in range(5))
NCON = P * 5
SW_LRU, SW_WA, SW_G2, SW_V1, SW_V2 = 0, 4 * P, 4 * P + GROUP, 4 * P + 2 * GROUP, 4 * P + 2 * GROUP + 64
NSW = SW_V2 + GROUP


def plan_chunks():
    out = []
    for layer in range(DEPTH):
        out += [("cm", "w_in", layer, c) for c in W_IN_COLS]
        out += [("tm", "w_out", layer, r) for r in range(0, KT, TM_ROWS)]
        out += [("cm", "xattn_wk", layer, c) for c in range(0, D, CM_COLS)]
        out += [("tm", "xattn_wv", layer, r) for r in range(0, KT, TM_ROWS)]
        out += [("cm", "xattn_wq", layer, c) for c in range(0, D, CM_COLS)]
        out += [("tm", "xattn_wo", layer, r) for r in range(0, KT, TM_ROWS)]
        if layer == 0:
            steps = D_FF // CM_COLS
            for j in range(steps + 1):
                if j < steps:
                    out += [("cm", "ffn_w_gate", 0, CM_COLS * j), ("cm", "ffn_w_up", 0, CM_COLS * j)]
                if j:
                    out += [("tm", "ffn_w_down", 0, TM_ROWS * (j - 1))]
    return out


def build(nc, A, out):
    chunks = plan_chunks()
    n_straight = len(chunks)
    first_chunk = {}
    for n, c in enumerate(chunks):
        first_chunk.setdefault(c[1:3], n)
    FSTEPS = D_FF // CM_COLS
    ESTEPS = D_FFE // CM_COLS

    with ExitStack() as ctx:
        def sb(name, cols, dt=F32):
            return ctx.enter_context(nc.sbuf_tensor(name, [P, cols], dt))

        sems = {}

        def S(name):
            if name not in sems:
                sems[name] = ctx.enter_context(nc.semaphore(name))
            return sems[name]

        raw = [sb(f"raw{i}", CH) for i in range(RAW)]
        whi = [sb(f"whi{i}", CH, F32R) for i in range(SPL)]
        wlo = [sb(f"wlo{i}", CH, F32R) for i in range(SPL)]
        x = sb("x", TT * D)[:, :].rearrange("p (t n) -> p t n", t=TT)
        hT = [sb(f"hT_{s}", KT * SEQ, F32R)[:, :].rearrange("p (c n) -> p c n", c=KT) for s in ("hi", "lo")]
        memT_flat = [sb(f"memT_{s}", KT * SEQ, F32R) for s in ("hi", "lo")]
        memT = [m[:, :].rearrange("p (c n) -> p c n", c=KT) for m in memT_flat]
        yT = hT
        actT = [[sb(f"act{b}_{s}", 2 * SEQ, F32R)[:, :] for s in ("hi", "lo")] for b in range(2)]
        small = [sb(f"wsm_{s}", 64, F32R)[:, :].rearrange("p (k n) -> p k n", k=KT) for s in ("hi", "lo")]
        PT = sb("PT", 28 * SEQ)
        MT = sb("MT", 7 * 1024)
        TMP = sb("TMP", 8 * 512)
        v_first = sb("v_first", 512)
        par = sb("par", NPAR)
        con = sb("con", NCON)
        sw = sb("sw", NSW)
        wsm_raw = sb("wsm_raw", 64)
        st = sb("st", 256)
        ps = ctx.enter_context(nc.psum_tensor("ps", [P, 8, 512], F32))

        def pt(m, n=2):
            return PT[:, m * SEQ:(m + n) * SEQ]

        def mt(i):
            return MT[:, i * 1024:(i + 1) * 1024]

        def tmp(i):
            return TMP[:, i * 512:(i + 1) * 512]

        def pc(name, layer=None, j=0, rows=slice(0, P)):
            a, _ = PCOL[(name, layer) if layer is not None else name]
            return par[rows, a + j:a + j + 1]

        def cst(a, n=P):
            return con[:, a:a + n]

        ident = cst(C_ID)
        con16 = sb("con16", 2 * LEVELS * P, mybir.dt.bfloat16)
        bdones = cst(C_BD)
        incl, strict = cst(C_INCL), cst(C_STRICT)
        xs = PT[:, 0:TT * D].rearrange("p (t n) -> p t n", t=TT)

        def cm(ap):
            return ap.rearrange("p (c n) -> p c n", c=2)

        NORMS = ["mix0", "mem", "xat0", "ffn0", "mix1", "xat1", "ffn1"]
        cm_index, n_cm = {}, 0
        for n, c in enumerate(chunks):
            if c[0] == "cm" and not c[1].startswith("ffn"):
                cm_index[n] = n_cm
                n_cm += 1
        TM_PHASES = [(w, l) for l in range(DEPTH) for w in ("w_out", "xattn_wv", "xattn_wo")]
        TM_PHASES.insert(3, ("ffn_w_down", 0))

        def chunk_src(c):
            kind, name, layer, at = c
            w = A[name][layer]
            if kind == "cm":
                return w.rearrange("(k p) n -> p k n", p=P)[:, :, at:at + CM_COLS]
            return w.rearrange("(k p) n -> p k n", p=P)[:, at:at + TM_ROWS, :]

        def chunk_view(ap, kind):
            return ap.rearrange("p (k n) -> p k n", k=KT if kind == "cm" else TM_ROWS)

        class Signalled:

            def __init__(self, ins):
                self.ins, self.sem = ins, None

            def then_inc(self, sem, by):
                if by:
                    self.ins.then_inc(sem, by)
                    self.sem = sem
                return self

        class Chain:

            def __init__(self, eng, own):
                self.eng, self.own, self.last, self.counts = eng, own, None, {}

            def settle(self):
                if self.last is not None:
                    if self.last.sem is None:
                        self.last.then_inc(self.own, 1)
                    n = self.counts[self.last.sem.name] = self.counts.get(self.last.sem.name, 0) + 1
                    self.eng.wait_ge(self.last.sem, n)
                self.last = None

            def link(self, emit):
                self.settle()
                self.last = Signalled(emit())
                return self.last


        def H(i):
            return MT[:, i * 512:(i + 1) * 512]

        G_N = H(7), H(13)
        K_KK, K_KA, K_B, K_BM, K_E, K_EN, K_EM, K_RN = H(2), H(3), H(13), tmp(1), tmp(5), tmp(6), tmp(7), pt(A_I)

        def lvl(v, flip=False):
            a = (v + LEVELS * flip) * P
            return con16[:, a:a + P]

        def rep(ap, n):
            return ap.unsqueeze(1).to_broadcast([P, n, P])

        def many(ap, n=4):
            return ap.rearrange("p (n m) -> p n m", n=n)

        def at(par_, t, c):
            return par_ * 512 + t * 256 + c * P

        def col(a, n=1):
            return st[:, a:a + n]

        ST_AB, ST_SIG, ST_X, ST_SP, ST_EXPA, ST_LBD, ST_LB, ST_LB1, ST_LAM = 16, 32, 48, 56, 64, 68, 70, 72, 74
        ST_G, ST_GC, ST_GTOT, ST_GD, ST_EGC, ST_NC0 = 80, 88, 96, 104, 112, 120
        ST_MX, ST_SUM, ST_RS = 128, 136, 144
        ST_LG, ST_TOP, ST_SEL, ST_GATE, ST_RANK, ST_W = 160, 176, 192, 208, 224, 240
        ST_BASE, ST_TOTAL, ST_OVER, ST_NEXT, ST_COUNT, ST_N1 = ST_SIG, ST_X, ST_SP, ST_EXPA, ST_G, ST_G + 1
        beta = col(ST_SIG, 16).rearrange("p (t n) -> p t n", t=2)[:, :, 4:8]

        kT = PT[:, 2048:4096].rearrange("p (c n) -> p c n", c=KT)
        vA = PT[:, 4096:6144].rearrange("p (t n) -> p t n", t=TT)
        qT = MT[:, 0:2048].rearrange("p (c n) -> p c n", c=KT)
        pr = MT[:, 2048:4096].rearrange("p (t h n) -> p t h n", t=TT, h=NH)
        prT = MT[:, 4096:6144].rearrange("p (m h n) -> p m h n", m=2, h=NH)
        hE = [m[:, 0:KT * P].rearrange("p (c n) -> p c n", c=KT) for m in memT_flat]
        yE = mt(2)
        g_tokens = lambda c: ps[:, 6 + c // 4, P * (c % 4):P * (c % 4) + P]
        pass_expert, gather_expert, pass_count = (col(a_, n_).bitcast(I32) for a_, n_ in
                                                  ((ST_AB, 2 * NE), (ST_NEXT, 2 * NE), (ST_COUNT, 1)))
        SECONDS = TT * P * 2 // (P + 1)
        oneh, onehg, onehT = mt(3)[:, 0:256], mt(3)[:, 256:512], mt(4)[:, 0:256]
        EXRAW = 2 * RAW
        assert (3 * ESTEPS) % EXRAW == 0 and RAW == SPL == 3

        def ff_chunk(j):
            return first_chunk["ffn_w_gate", 0] + 3 * j - (1 if j else 0)

        def ff_down(j):
            return first_chunk["ffn_w_gate", 0] + 3 * j + (4 if j < FSTEPS - 1 else 2)

        assert ESTEPS % 2 == 0

        def ex_slot(q):
            return (n_straight + q) % SPL

        def ex_count(s, q):
            return s * 3 + (n_straight + q + 1)

        def ex_raw_slot(m, q):
            return (3 * m + q) % EXRAW

        def ex_fill(h, m, q):
            i = ex_raw_slot(m, q)
            return h + ((3 * m + q) // EXRAW + 1 + (len(range(i, n_straight, RAW)) if i < RAW else 0))

        epsc = lambda i: col(8 + i)
        ones = col(10).to_broadcast([P, P])
        mem = MT[:, 4096:6144].rearrange("p (t n) -> p t n", t=TT)
        MEM_NORM = 1
        norm_index = lambda l: 4 if l else 0
        AB_T = tmp(7)[0:8, 0:SEQ]
        final_gain = PT[:, 6144:7168]
        ex_raw = [raw[i][:, :] for i in range(RAW)] + [PT[:, CH:2 * CH], PT[:, 2 * CH:3 * CH], TMP[:, 0:CH]]

        block = ctx.enter_context(nc.Block())

        @block.sync
        def _(sp):
            sp.dma_start(x, A["x"][0].rearrange("(t p) n -> p t n", p=P)).then_inc(S("x_in"), 16)
            sp.dma_start(par[:, :], A["params"]).then_inc(S("tables_in"), 16)
            sp.dma_start(con[:, :], A["consts"]).then_inc(S("tables_in"), 16)
            sp.dma_start(wsm_raw[:, :].rearrange("p (k n) -> p k n", k=KT),
                 A["w_in"][0].rearrange("(k p) n -> p k n", p=P)[:, :, GDN_AB:GDN_AB + 8]).then_inc(S("wsm_in"), 16)
            for n, c in enumerate(chunks):
                if n >= RAW:
                    sp.wait_ge(S("w_lo"), n - RAW + 1)
                sp.dma_start(chunk_view(raw[n % RAW][:, :], c[0]), chunk_src(c)).then_inc(S(f"raw_in{n % RAW}"), 16)
                if n == RAW - 1:
                    sp.dma_start(mem, A["mem"][0].rearrange("(t p) n -> p t n", p=P)).then_inc(S("mem_in"), 16)
                    sp.dma_start(con16[:, :], A["level_masks"]).then_inc(S("mem_in"), 16)
                    sp.dma_start(sw[:, :], A["small_w"][0]).then_inc(S("sw_in"), 16)
                if n == first_chunk["w_out", 0]:
                    sp.wait_ge(S("wsm_split"), 1)
                    sp.dma_start(wsm_raw[:, :].rearrange("p (k n) -> p k n", k=KT),
                         A["w_in"][1].rearrange("(k p) n -> p k n", p=P)[:, :, GDN_AB:GDN_AB + 8]).then_inc(S("wsm_in"), 16)
                if n == first_chunk["xattn_wq", 0]:
                    sp.wait_ge(S("mix_done"), 1)
                    sp.dma_start(sw[:, :], A["small_w"][1]).then_inc(S("sw_in"), 16)
                if n == first_chunk["w_out", 1]:
                    sp.wait_ge(S("wsm_split"), 2)
                    sp.dma_start(wsm_raw[:, :].rearrange("p (k n) -> p k n", k=KT),
                         A["moe_router"][0].rearrange("(k p) n -> p k n", p=P)).then_inc(S("wsm_in"), 16)
            def ex_load(name, e, j, h, m, q):
                i = ex_raw_slot(m, q)
                sp.wait_ge(S("w_lo"), ex_count(h * 2 + m, q - EXRAW))
                wt = A[name][0][bass.ds(e, 1)].rearrange("a (k p) n -> p (a k) n", p=P)
                down = name == "moe_w_down"
                src = wt[:, bass.ds(j * TM_ROWS, TM_ROWS), :] if down else wt[:, :, bass.ds(j * CM_COLS, CM_COLS)]
                sp.dma_start(chunk_view(ex_raw[i], "tm" if down else "cm"), src).then_inc(S(f"raw_in{i}"), 16)

            def ex_pass(ep, e):
                h = ep * (ESTEPS // 2)

                def step(j, h, m):
                    ex_load("moe_w_gate", e, j + 1, h, m, 2)
                    if m == 0:
                        sp.wait_ge(S("x_done"), 10)
                    ex_load("moe_w_up", e, j + 1, h, m, 3)
                    ex_load("moe_w_down", e, j, h, m, 4)

                ex_load("moe_w_gate", e, 0, h, 0, 0)
                ex_load("moe_w_up", e, 0, h, 0, 1)
                step(0, h, 0)
                with sp.Fori(0, (ESTEPS - 2) // 2) as i:
                    for m in (1, 2):
                        step(i * 2 + m, h + i, m)
                ex_load("moe_w_down", e, ESTEPS - 1, h, ESTEPS - 1, 2)

            sp.wait_ge(S("w_lo"), n_straight)
            with sp.Fori(0, NE) as e:
                ex_pass(e, e)
            sp.dma_start(final_gain, A["norm_final"]).then_inc(S("nf_in"), 16)
            sp.wait_ge(S("ex_table"), 1)
            with sp.Fori(0, SECONDS) as i:
                which = sp.value_load(pass_expert[0:1, bass.ds(i + NE, 1)], min_val=0, max_val=NE)
                with sp.If(which < NE):
                    e = sp.value_load(pass_expert[0:1, bass.ds(i + NE, 1)], min_val=0, max_val=NE - 1)
                    ex_pass(i + NE, e)
            sp.wait_ge(S("x_done"), 12)
            sp.dma_start(out[0].rearrange("(t p) n -> p t n", p=P), x).then_inc(S("stored"), 16)
            sp.wait_ge(S("stored"), 16)

        @block.scalar
        def _(act):
            chain = Chain(act, S("act_step"))
            split = [0]

            def a(o, i, f, **kw):
                return chain.link(lambda: nc.scalar.activation(o, i, f, **kw))

            def ahead(n):
                while split[0] < min(n, n_straight):
                    i = split[0]
                    act.wait_ge(S(f"raw_in{i % RAW}"), 16 * (i // RAW + 1))
                    if i >= SPL:
                        act.wait_ge(S("chunk_done"), i - SPL + 1)
                    nc.scalar.activation(whi[i % SPL][:, :], raw[i % RAW][:, :], ACT.Copy).then_inc(S("w_hi"), 1)
                    split[0] += 1

            def stats(i, src, adds=0):
                for t in range(TT):
                    if adds:
                        act.wait_ge(S("x_done"), TT * (adds - 1) + t + 1)
                    a(mt(6), src[:, t, :], ACT.Square, accum_out=col(2 + t))
                    a(col(4 + t), col(2 + t), ACT.Sqrt, scale=1.0 / D, bias=epsc(0)).then_inc(S("n_rms"), 1)

            def norm(i, gain, dst):
                ahead(2)
                for c in range(KT):
                    act.wait_ge(S("n_tr"), i * KT + c + 1)
                    a(dst[0][:, c, :], ps[:, c, 0:SEQ], ACT.Copy, scale=gain(c)).then_inc(S("n_hi"), 1)

            def cm_evac(n0, count, dst, scale=1.0, after=None):
                for j in range(count):
                    if after:
                        after(j)
                    n = n0 + j
                    ahead(n + SPL)
                    act.wait_ge(S("chunk_done"), n + 1)
                    a(dst(j), ps[:, cm_index[n] % 4, :], ACT.Copy, scale=scale).then_inc(S("cm_free"), 1)

            def split_small(k):
                act.wait_ge(S("wsm_in"), 16 * (k + 1))
                if k:
                    act.wait_ge(S("ab_mm"), 2 * k - 1)
                a(small[0], wsm_raw[:, :].rearrange("p (k n) -> p k n", k=KT), ACT.Copy).then_inc(S("wsm_hi"), 1)

            def mem_norm(j):
                for c in (2 * j - 2, 2 * j - 1):
                    act.wait_ge(S("n_tr"), MEM_NORM * KT + c + 1)
                    a(memT[0][:, c, :], ps[:, 4 + c % 2, 0:SEQ], ACT.Copy, scale=pc("mem_norm", None, c)).then_inc(S("n_hi"), 1)

            def gates_ahead(l, j):
                if l == 0 and 1 <= j <= KT // 2:
                    mem_norm(j)
                if j == 6:
                    act.wait_ge(S("sm_ready"), 2 * (l + 1))
                    a(col(ST_SIG, 16), col(ST_AB, 16), ACT.Sigmoid)
                    if l:
                        a(col(ST_LB, 2), col(ST_LBD, 2), ACT.Sigmoid)
                    act.wait_ge(S("conv_g"), l + 1)
                    for i in range(3):
                        a(H(3 + i), H(i), ACT.Sigmoid).then_inc(S("s_qkv"), 1)
                if j == 8:
                    act.wait_ge(S("lru_mm"), l + 1)
                    for i in range(2):
                        a(H(8)[:, 256 * i:256 * i + 256], ps[:, 5, 256 * i:256 * i + 256], ACT.Sigmoid, bias=pc("lru_ba", l, i))
                    for i in range(2):
                        a(H(9)[:, 256 * i:256 * i + 256], ps[:, 6, 256 * i:256 * i + 256], ACT.Sigmoid, bias=pc("lru_bx", l, i)).then_inc(S("lru_ri"), 1)
                if j == 11:
                    act.wait_ge(S("shift"), l + 1)
                    a(PT[0:64, D_W * SEQ:(D_W + 1) * SEQ], PT[0:64, D_W * SEQ:(D_W + 1) * SEQ], ACT.Tanh)
                    a(pt(D_G, 1), pt(D_G, 1), ACT.Sigmoid).then_inc(S("lora_in"), 1)
                    a(tmp(0), pt(A_F), ACT.Sigmoid, scale=-1.0).then_inc(S("s_kA"), 1)
                    a(tmp(1), pt(A_G), ACT.Sigmoid)
                if j == 12:
                    a(tmp(2), pt(B_Z), ACT.Sigmoid).then_inc(S("s_z"), 1)
                    if l:
                        a(tmp(5), pt(A_F), ACT.Sigmoid)
                if j == 13:
                    act.wait_ge(S("gelu_in"), l + 1)
                    a(tmp(4), tmp(4), ACT.Sigmoid).then_inc(S("gelu_s"), 1)

            def gates(l):
                act.wait_ge(S("lora_mm"), l + 1)
                for j in range(2):
                    a(pt(C_X)[:, 256 * j:256 * j + 256], ps[:, 2, 256 * j:256 * j + 256], ACT.Sigmoid, bias=pc("rwkv_w0", l, j))
                for j in range(2):
                    a(pt(D_W)[:, 256 * j:256 * j + 256], ps[:, 3, 256 * j:256 * j + 256], ACT.Sigmoid, bias=pc("rwkv_a0", l, j))
                a(H(12), ps[:, 4, :], ACT.Copy).then_inc(S("lora_s"), 1)
                if l:
                    act.wait_ge(S("vmix_mm"), 1)
                    a(H(13)[0:32, 0:256], ps[0:32, 5, 0:256], ACT.Copy).then_inc(S("vmix1"), 1)
                    act.wait_ge(S("vmix_mm"), 2)
                    for j in range(2):
                        a(tmp(3)[:, 256 * j:256 * j + 256], ps[:, 6, 256 * j:256 * j + 256], ACT.Sigmoid,
                          bias=pc("rwkv_v0", None, j)).then_inc(S("vmix2"), 1)

            def logs(l):
                o, o2 = PCOL["gdn_A_log", l][0], PCOL["lru_lambda", l][0]
                act.wait_ge(S("gd_x"), l + 1)
                a(col(ST_SP, 8), col(ST_X, 8), ACT.Abs)
                a(col(ST_LAM, 2), par[:, o2:o2 + 2], ACT.Abs)
                if l == 0:
                    a(tmp(5), pt(A_F), ACT.Abs)
                    a(tmp(5), tmp(5), ACT.Exp, scale=-1.0)
                a(col(ST_SP, 8), col(ST_SP, 8), ACT.Exp, scale=-1.0)
                a(col(ST_EXPA, 4), par[:, o:o + 4], ACT.Exp)
                a(col(ST_LAM, 2), col(ST_LAM, 2), ACT.Exp, scale=-1.0)
                if l == 0:
                    a(tmp(5), tmp(5), ACT.Ln, bias=1.0).then_inc(S("hg_ln"), 1)
                else:
                    act.wait_ge(S("hg_F"), 1)
                    a(tmp(6), tmp(5), ACT.Ln).then_inc(S("hg_ln"), 1)
                a(col(ST_SP, 8), col(ST_SP, 8), ACT.Ln, bias=1.0).then_inc(S("gd_sp"), 1)
                a(col(ST_LAM, 2), col(ST_LAM, 2), ACT.Ln, bias=1.0).then_inc(S("lam_sp"), 1)

            def rglru(l, v):
                if v == 1:
                    act.wait_ge(S("lru_log"), l + 1)
                    a(H(10), H(8), ACT.Exp)
                    a(H(11), H(8), ACT.Exp, scale=2.0).then_inc(S("lru_a"), 1)
                if v == LEVELS - 1:
                    act.wait_ge(S("lru_gain"), l + 1)
                    a(H(11), H(11), ACT.Ln)
                    a(H(11), H(11), ACT.Exp, scale=0.5).then_inc(S("lru_root"), 1)
                    a(G_N[0], pt(B_Q), ACT.Square)
                    a(G_N[1], pt(B_K), ACT.Square).then_inc(S("gd_sq"), 1)

            def hgrn(l):
                for v in range(LEVELS):
                    act.wait_ge(S("hg_d"), l * LEVELS + v + 1)
                    a(tmp(6 + v % 2), tmp(6 + v % 2), ACT.Exp).then_inc(S("hg_e"), 1)
                    if v == 0:
                        act.wait_ge(S("hg_tr"), l + 1)
                        a(tmp(1), ps[:, 4, :], ACT.Copy).then_inc(S("hg_v"), 1)
                    rglru(l, v)
                act.wait_ge(S("hg_qk"), (l + 1) * LEVELS)
                a(tmp(6), pt(A_F), ACT.Exp)
                for c in range(2):
                    b = pt(A_F)[:, 256 * c:256 * c + P]
                    a(tmp(7)[:, P * c:P * c + P], b, ACT.Exp, scale=-1.0, bias=b[:, P - 1:P]).then_inc(S("hg_end"), 1)
                act.wait_ge(S("hg_trk"), l + 1)
                a(tmp(5)[:, 0:256], ps[:, 5, 0:256], ACT.Copy).then_inc(S("hg_kd"), 1)
                act.wait_ge(S("gd_ss"), l + 1)
                for j in range(2):
                    a(G_N[j], ps[:, j, :], ACT.Ln, bias=epsc(0))
                for j in range(2):
                    a(G_N[j], G_N[j], ACT.Exp, scale=-0.5).then_inc(S("gd_rn"), 1)
                head_rms(l, 0, 7)

            def head_rms(l, which, bank):
                act.wait_ge(S("o_full"), 2 * l + which + 1)
                a(tmp(6), ps[:, bank, :], ACT.Square).then_inc(S("o_sq"), 1)
                act.wait_ge(S("o_ss"), 2 * l + which + 1)
                a(tmp(7), ps[:, 6, :], ACT.Ln, scale=1.0 / HD, bias=epsc(0))
                a(tmp(7), tmp(7), ACT.Exp, scale=-0.5).then_inc(S("o_rn"), 1)

            def rwkv_ahead(l):
                act.wait_ge(S("rk_kk"), l + 1)
                a(K_RN, K_KK, ACT.Square).then_inc(S("rk_sq"), 1)
                act.wait_ge(S("rk_ss"), l + 1)
                a(K_RN, ps[:, 6, :], ACT.Ln, bias=epsc(0))
                a(K_RN, K_RN, ACT.Exp, scale=-0.5).then_inc(S("rk_rn"), 1)
                act.wait_ge(S("rk_b"), l + 1)
                for c in range(2):
                    for t in range(TT):
                        s_ = slice(256 * c + P * t, 256 * c + P * t + P)
                        b, bm, mid = K_B[:, s_], K_BM[:, s_], 256 * c + P * t + HD - 1
                        n0 = col(ST_NC0 + 2 * c + t)
                        a(K_E[:, s_], b, ACT.Exp, bias=n0)
                        a(K_EN[:, s_], b, ACT.Exp, scale=-1.0, bias=K_B[:, mid:mid + 1])
                        a(K_EM[:, s_], bm, ACT.Exp, bias=n0)
                    s0, s1 = slice(256 * c, 256 * c + P), slice(256 * c + P, 256 * c + 256)
                    a(pt(A_Q)[:, s0], K_B[:, s0], ACT.Exp, scale=-1.0, bias=K_B[:, 256 * c + P - 1:256 * c + P])
                    a(pt(A_Q)[:, s1], K_B[:, s1], ACT.Exp)
                    a(pt(A_F)[:, s1], K_BM[:, s1], ACT.Exp).then_inc(S("rk_e"), 1)
            def deltanet(l):
                act.wait_ge(S("gd_gd"), l + 1)
                a(col(ST_GD, 8), col(ST_GD, 8), ACT.Exp)
                a(tmp(5), ps[:, 4, :], ACT.Exp).then_inc(S("gd_eg"), 1)
                act.wait_ge(S("gd_diff"), l + 1)
                a(mt(1), mt(1), ACT.Exp).then_inc(S("gd_rel"), 1)
                rwkv_ahead(l)
                for t in range(TT):
                    act.wait_ge(S("gd_u"), 2 * l + t + 1)
                    a(tmp(6)[:, 256 * t:256 * t + 256], ps[:, 6, 256 * t:256 * t + 256], ACT.Copy).then_inc(S("gd_us"), 1)
                head_rms(l, 1, 0)

            def rwkv(l):
                act.wait_ge(S("rk_trv"), l + 1)
                a(tmp(5), ps[:, 6, :], ACT.Copy)
                a(tmp(6), ps[:, 7, :], ACT.Copy).then_inc(S("rk_vk"), 1)
                for t in range(TT):
                    act.wait_ge(S("rk_r"), 2 * l + t + 1)
                    a(tmp(7)[:, 256 * t:256 * t + 256], ps[:, 6, 256 * t:256 * t + 256], ACT.Copy).then_inc(S("rk_rs"), 1)
                    act.wait_ge(S("rk_u"), 2 * l + t + 1)
                    a(tmp(4)[:, 256 * t:256 * t + 256], ps[:, 7, 256 * t:256 * t + 256], ACT.Copy, scale=-1.0).then_inc(S("rk_us"), 1)
                act.wait_ge(S("rk_o"), l + 1)
                a(tmp(0), ps[:, 0, :], ACT.Copy).then_inc(S("rk_y"), 1)
                act.wait_ge(S("rk_yc"), l + 1)
                a(tmp(1), tmp(0), ACT.Square).then_inc(S("rk_ysq"), 1)
                act.wait_ge(S("rk_var"), l + 1)
                a(tmp(1), ps[:, 2, :], ACT.Ln, scale=1.0 / HD, bias=epsc(1))
                a(tmp(1), tmp(1), ACT.Exp, scale=-0.5).then_inc(S("rk_gn"), 1)

            def attention(l):
                stats(2 + 3 * l, x, 3 * l + 1)
                cm_evac(first_chunk["xattn_wk", l], 4, lambda j: kT[:, 2 * j:2 * j + 2, :].rearrange("p c n -> p (c n)"))
                norm(2 + 3 * l, lambda c: pc("norm_xattn", l, c), hT)
                n = first_chunk["xattn_wv", l]
                for j in range(4):
                    ahead(n + j + SPL)
                act.wait_ge(S("chunk_done"), n + 4)
                for t in range(TT):
                    for hf in range(2):
                        a(vA[:, t, 512 * hf:512 * hf + 512], ps[:, 4 + 2 * t + hf, :], ACT.Copy).then_inc(S("at_v"), 1)
                cm_evac(first_chunk["xattn_wq", l], 4, lambda j: qT[:, 2 * j:2 * j + 2, :].rearrange("p c n -> p (c n)"),
                        scale=1.0 / 16.0)
                for i in range(2 * NH):
                    t, h = i // NH, i % NH
                    act.wait_ge(S("at_max"), 4 * l + i // 2 + 1)
                    a(pr[:, t, h, :], ps[:, i // 2, 256 * (h % 2):256 * (h % 2) + 256], ACT.Exp,
                      bias=col(ST_MX + i), accum_out=col(ST_SUM + i)).then_inc(S("at_exp"), 1)
                for b in range(4):
                    act.wait_ge(S("at_tr"), 4 * l + b + 1)
                    t, m = b // 2, b % 2
                    a(prT[:, m, :, t * P:(t + 1) * P], many(ps[:, 4 + b, :]), ACT.Copy).then_inc(S("at_prT"), 1)
                for b in range(4):
                    act.wait_ge(S("at_o"), 4 * l + b + 1)
                    a(yT[0][:, 2 * b:2 * b + 2, :].rearrange("p c n -> p (c n)"), ps[:, b, :], ACT.Copy).then_inc(S("at_hi"), 1)
                n = first_chunk["xattn_wo", l]
                for j in range(4):
                    ahead(n + j + SPL)

            def swiglu():
                stats(3, x, 2)
                norm(3, lambda c: pc("norm_ffn", 0, c), hT)
                for j in range(FSTEPS):
                    n = ff_chunk(j)
                    ahead(n + SPL)
                    act.wait_ge(S("chunk_done"), n + 1)
                    if j:
                        act.wait_ge(S("ff_prod"), j)
                    a(mt(0)[:, 0:512], ps[:, 2 * (j % 2), :], ACT.Silu).then_inc(S("ff_silu"), 1)
                    ahead(n + 1 + SPL)
                    act.wait_ge(S("ff_prod"), j + 1)
                    if j >= 2:
                        act.wait_ge(S("chunk_done"), ff_down(j - 2) + 1)
                    a(actT[j % 2][0], mt(1)[:, 512 * (j % 2):512 * (j % 2) + 512], ACT.Copy).then_inc(S("ff_hi"), 1)
                ahead(ff_down(FSTEPS - 1) + SPL)

            def experts():
                stats(6, x, 5)
                norm(6, lambda c: pc("norm_ffn", 1, c), hT)
                act.wait_ge(S("rt_d"), 1)
                a(col(ST_W, 4), col(ST_W, 4), ACT.Sigmoid).then_inc(S("rt_p"), 1)

                def chunk(h, m, q):
                    i, slot = ex_raw_slot(m, q), ex_slot(q)
                    act.wait_ge(S(f"raw_in{i}"), ex_fill(h, m, q) * 16)
                    act.wait_ge(S("chunk_done"), ex_count(h * 2 + m, q - SPL))
                    nc.scalar.activation(whi[slot][:, :], ex_raw[i], ACT.Copy).then_inc(S("w_hi"), 1)

                def silu(s, gate_done):
                    act.wait_ge(S("chunk_done"), gate_done)
                    act.wait_ge(S("ex_prod"), s + 1)
                    nc.scalar.activation(mt(0)[:, 0:256], ps[:, 0, 0:256], ACT.Silu).then_inc(S("ex_silu"), 1)

                def act_hi(s):
                    act.wait_ge(S("ex_tr"), s + 2)
                    nc.scalar.activation(actT[0][0][:, 0:256], ps[:, 2, 0:256], ACT.Copy).then_inc(S("ex_ahi"), 1)

                def gathered(p):
                    for c in range(KT):
                        act.wait_ge(S("ex_g"), p * 2 + (c // 4 + 1))
                        nc.scalar.activation(hE[0][:, c, :], g_tokens(c), ACT.Copy, scale=pc("norm_ffn", 1, c)).then_inc(S("ex_hi"), 1)

                def expert_output(q):
                    act.wait_ge(S("chunk_done"), ex_count(q * ESTEPS - 1, 2))
                    act.wait_ge(S("ex_add"), q + 1)
                    for hf in range(2):
                        nc.scalar.activation(yE[:, 512 * hf:512 * hf + 512], ps[:, 4 + hf, :], ACT.Copy).then_inc(S("ex_y"), 1)

                def step(h, m):
                    chunk(h, m, 2)
                    chunk(h, m, 3)
                    act_hi(h * 2 + m)
                    chunk(h, m, 4)

                chain.settle()
                gathered(0)
                act.wait_ge(S("ex_table"), 1)
                count = act.value_load(pass_count[0:1, 0:1], min_val=NE, max_val=NE + SECONDS)
                act.wait_ge(S("ex_tr"), 1)
                with act.Fori(0, NE + SECONDS) as ep:
                    which = act.value_load(pass_expert[0:1, bass.ds(ep, 1)], min_val=0, max_val=NE)
                    with act.If(which < NE):
                        h = ep * (ESTEPS // 2)
                        r = ep * ESTEPS
                        chunk(h, 0, 0)
                        chunk(h, 0, 1)
                        expert_output(ep)
                        silu(r, ex_count(r, 0))
                        step(h, 0)
                        with act.Fori(0, (ESTEPS - 2) // 2) as i:
                            for m in (1, 2):
                                silu(r + i * 2 + m, ex_count(r + i * 2 + (m - 1), 2))
                                step(h + i, m)
                        silu(r + (ESTEPS - 1), ex_count(r + (ESTEPS - 2), 2))
                        chunk(h, ESTEPS - 1, 2)
                        act.wait_ge(S("chunk_done"), ex_count(r + (ESTEPS - 2), 3))
                        gathered(ep + 1)
                        act_hi(r + (ESTEPS - 1))
                expert_output(count)

            act.wait_ge(S("tables_in"), 32)
            act.wait_ge(S("eps"), 1)
            act.wait_ge(S("x_in"), 16)
            for l in range(DEPTH):
                stats(norm_index(l), x, 3 * l)
                norm(norm_index(l), lambda c: pc("norm_mix", l, c), hT)
                if l == 0:
                    ahead(SPL)
                    split_small(0)
                    act.wait_ge(S("mem_in"), 32)
                    stats(MEM_NORM, mem)
                cm_evac(first_chunk["w_in", l], 14, lambda j: pt(W_IN_PARTS[j]), after=lambda j: gates_ahead(l, j))
                act.wait_ge(S("sw_in"), 16 * (l + 1))
                gates(l)
                logs(l)
                hgrn(l)
                deltanet(l)
                rwkv(l)
                split_small(l + 1)
                n = first_chunk["w_out", l]
                for j in range(4):
                    ahead(n + j + SPL)
                attention(l)
                if l == 0:
                    swiglu()
            experts()
            act.wait_ge(S("x_done"), 11)
            stats(7, x)

        @block.vector
        def _(dve):
            chain = Chain(dve, S("dve_step"))
            split = [0]
            V = nc.vector

            def tt(o, x0, x1, op):
                return chain.link(lambda: V.tensor_tensor(o, x0, x1, op))

            def ts(o, x0, s1, op0, s2=None, op1=None):
                return chain.link(lambda: V.tensor_scalar(o, x0, s1, s2, op0, op1) if op1 else V.tensor_scalar(o, x0, s1, None, op0))

            def stt(o, x0, s_, x1, op0, op1):
                return chain.link(lambda: V.scalar_tensor_tensor(out=o, in0=x0, scalar=s_, in1=x1, op0=op0, op1=op1))

            def ahead(n):
                while split[0] < min(n, n_straight):
                    i = split[0]
                    dve.wait_ge(S("w_hi"), i + 1)
                    V.tensor_tensor(wlo[i % SPL][:, :], raw[i % RAW][:, :], whi[i % SPL][:, :].bitcast(F32),
                                    ALU.subtract).then_inc(S("w_lo"), 1)
                    split[0] += 1

            def stats(i, src, dst):
                for t in range(TT):
                    dve.wait_ge(S("n_rms"), TT * i + t + 1)
                    chain.link(lambda: V.reciprocal(col(t), col(4 + t)))
                    ts(col(6 + t), col(2 + t), 1.0 / D, ALU.mult, EPS, ALU.add)
                    stt(col(6 + t), col(6 + t), col(t), col(t), ALU.mult, ALU.mult)
                    ts(col(6 + t), col(6 + t), -0.5, ALU.mult, 1.5, ALU.add)
                    tt(col(t), col(t), col(6 + t), ALU.mult)
                    ts(dst[:, t, :], src[:, t, :], col(t), ALU.mult).then_inc(S("n_xs"), 1)

            def norm(i, gain, dst):
                ahead(2)
                for c in range(KT):
                    dve.wait_ge(S("n_hi"), i * KT + c + 1)
                    stt(dst[1][:, c, :], ps[:, c, 0:SEQ], gain(c), dst[0][:, c, :].bitcast(F32), ALU.mult, ALU.subtract).then_inc(S("n_lo"), 1)

            def cm_steps(n0, count, after=None):
                for j in range(count):
                    ahead(n0 + j + SPL)
                    if after:
                        after(j)

            def tm_add(n0, count):
                for j in range(count):
                    ahead(n0 + j + SPL)
                dve.wait_ge(S("chunk_done"), n0 + count)
                for t in range(TT):
                    for hf in range(2):
                        s_ = slice(512 * hf, 512 * hf + 512)
                        tt(x[:, t, s_], x[:, t, s_], ps[:, 4 + 2 * t + hf, :], ALU.add).then_inc(S("x_done"), hf)

            def split_small(k):
                dve.wait_ge(S("wsm_hi"), k + 1)
                tt(small[1], wsm_raw[:, :].rearrange("p (k n) -> p k n", k=KT), small[0].bitcast(F32), ALU.subtract).then_inc(S("wsm_split"), 1)

            def conv(taps, count, m, src, dst, bias=None):
                w = lambda j: par[:, taps + count * j + m:taps + count * j + m + 1]
                if bias is None:
                    ts(dst, src, w(3), ALU.mult)
                else:
                    ts(dst, src, w(3), ALU.mult, bias, ALU.add)
                for j in range(3):
                    k = 3 - j
                    last = stt(dst[:, k:], src[:, :SEQ - k], w(j), dst[:, k:], ALU.mult, ALU.add)
                return last

            def mem_norm(j):
                for c in (2 * j - 2, 2 * j - 1):
                    dve.wait_ge(S("n_hi"), MEM_NORM * KT + c + 1)
                    stt(memT[1][:, c, :], ps[:, 4 + c % 2, 0:SEQ], pc("mem_norm", None, c), memT[0][:, c, :].bitcast(F32),
                        ALU.mult, ALU.subtract).then_inc(S("n_lo"), 1)

            def gates_ahead(l, j):
                if l == 0 and 1 <= j <= KT // 2:
                    mem_norm(j)
                if j == 0:
                    return
                if j == 1:
                    dve.wait_ge(S("ab_mm"), 2 * l + 1)
                    chain.link(lambda: V.tensor_copy(AB_T, ps[0:8, 7, 0:SEQ])).then_inc(S("sm_ready"), 1)
                if j == 2:
                    dve.wait_ge(S("ab_mm"), 2 * l + 2)
                    if l:
                        o0, o1 = PCOL["lb0"][0], PCOL["lb1"][0]
                        tt(col(ST_LBD, 2), par[:, o1:o1 + 2], par[:, o0:o0 + 2], ALU.subtract)
                    chain.link(lambda: V.tensor_copy(col(ST_AB, 16), ps[:, 7, 0:16])).then_inc(S("sm_ready"), 1)
                    o = PCOL["gdn_dt_bias", l][0]
                    for t in range(TT):
                        tt(col(ST_X + 4 * t, 4), col(ST_AB + 8 * t, 4), par[:, o:o + 4], ALU.add).then_inc(S("gd_x"), 1 if t else 0)
                dve.wait_ge(S("cm_free"), cm_index[first_chunk["w_in", l]] + j)
                if j <= 3:
                    for m in (2 * j - 2, 2 * j - 1):
                        conv(PCOL["gdn_conv_w", l][0], 6, m, pt(B_Q + m, 1), MT[:, 256 * m:256 * m + 256]).then_inc(S("conv_g"), 1 if m == 5 else 0)
                if j == 4:
                    for m in range(2):
                        conv(PCOL["lru_conv_w", l][0], 2, m, pt(C_X + m, 1), H(6)[:, 256 * m:256 * m + 256],
                             pc("lru_conv_b", l, m)).then_inc(S("conv_l"), 1 if m else 0)
                c8 = pt(D_R, 8).rearrange("p (m n) -> p m n", m=8)
                d8 = TMP[:, 0:2048].rearrange("p (m n) -> p m n", m=8)
                if 5 <= j <= 8:
                    m = slice(2 * j - 10, 2 * j - 8)
                    tt(d8[:, m, 1:], c8[:, m, :SEQ - 1], c8[:, m, 1:], ALU.subtract)
                    ts(d8[:, m, 0:1], c8[:, m, 0:1], -1.0, ALU.mult)
                    for i in (m.start, m.start + 1):
                        stt(c8[:, i, :], d8[:, i, :], pc("rwkv_mu", l, i), c8[:, i, :], ALU.mult, ALU.add).then_inc(S("shift"), 1 if i == 7 else 0)
                if j == 9:
                    g0 = 2.0 * float(np.sqrt(2.0 / np.pi))
                    tt(tmp(4), pt(C_G), pt(C_G), ALU.mult)
                    ts(tmp(4), tmp(4), 0.044715 * g0, ALU.mult, g0, ALU.add)
                    tt(tmp(4), tmp(4), pt(C_G), ALU.mult).then_inc(S("gelu_in"), 1)
                if j == 10:
                    dve.wait_ge(S("s_qkv"), 3 * (l + 1))
                    tt(pt(B_Q, 6), MT[:, 0:1536], MT[:, 1536:3072], ALU.mult)
                if j == 11:
                    if l == 0:
                        chain.link(lambda: V.tensor_copy(v_first[:, :], pt(D_V)))
                    else:
                        tt(v_first[:, :], v_first[:, :], pt(D_V), ALU.subtract)
                if j == 13:
                    dve.wait_ge(S("s_z"), l + 1)
                    tt(pt(A_G), pt(A_G), tmp(1), ALU.mult)
                    tt(pt(B_Z), pt(B_Z), tmp(2), ALU.mult)

            def gates(l):
                dve.wait_ge(S("cm_free"), cm_index[first_chunk["w_in", l]] + 14)
                dve.wait_ge(S("gelu_s"), l + 1)
                tt(pt(C_G), pt(C_G), tmp(4), ALU.mult)
                if l:
                    ts(col(ST_LB1, 2), col(ST_LB, 2), -1.0, ALU.mult, 1.0, ALU.add)
                    for c in range(2):
                        s_ = slice(256 * c, 256 * c + 256)
                        ts(tmp(5)[:, s_], tmp(5)[:, s_], col(ST_LB1 + c), ALU.mult, col(ST_LB + c), ALU.add).then_inc(S("hg_F"), 1 if c else 0)
                    for c in range(2):
                        s_ = slice(256 * c, 256 * c + 256)
                        ts(tmp(0)[:, s_], tmp(0)[:, s_], col(ST_LB1 + c), ALU.mult)
                    dve.wait_ge(S("vmix2"), 2)
                    tt(v_first[:, :], v_first[:, :], tmp(3), ALU.mult)
                    tt(pt(D_V), pt(D_V), v_first[:, :], ALU.add)

            def logs(l):
                dve.wait_ge(S("hg_ln"), l + 1)
                if l == 0:
                    stt(tmp(6), pt(A_F), 0.0, tmp(5), ALU.min, ALU.subtract)
                dve.wait_ge(S("gd_sp"), l + 1)
                stt(col(ST_SP, 8), col(ST_X, 8), 0.0, col(ST_SP, 8), ALU.max, ALU.add)
                for t in range(TT):
                    stt(col(ST_G + 4 * t, 4), col(ST_SP + 4 * t, 4), -1.0, col(ST_EXPA, 4), ALU.mult, ALU.mult).then_inc(S("gd_g"), 1 if t else 0)
                dve.wait_ge(S("lam_sp"), l + 1)
                o = PCOL["lru_lambda", l][0]
                ts(col(ST_LAM + 2, 2), par[:, o:o + 2], -1.0, ALU.mult, 0.0, ALU.max)
                tt(col(ST_LAM, 2), col(ST_LAM, 2), col(ST_LAM + 2, 2), ALU.add)
                ts(col(ST_LAM, 2), col(ST_LAM, 2), -8.0, ALU.mult)

            def rglru(l, v):
                la, ex = H(7), H(13)
                if v == 0:
                    dve.wait_ge(S("lru_ri"), 2 * (l + 1))
                    for c in range(2):
                        s_ = slice(256 * c, 256 * c + 256)
                        ts(H(8)[:, s_], H(8)[:, s_], col(ST_LAM + c), ALU.mult).then_inc(S("lru_log"), 1 if c else 0)
                if v == 1:
                    ts(la, H(8), 2.0, ALU.mult)
                    ts(ex, la, 1.0 / 120, ALU.mult)
                    stt(ex, ex, 1.0 / 24, la, ALU.add, ALU.mult)
                if v == 2:
                    stt(ex, ex, 1.0 / 6, la, ALU.add, ALU.mult)
                    stt(ex, ex, 0.5, la, ALU.add, ALU.mult)
                if v == 3:
                    stt(ex, ex, 1.0, la, ALU.add, ALU.mult)
                    ts(ex, ex, -1.0, ALU.mult)
                    ts(la, la, -0.1, ALU.is_gt)
                if v == 4:
                    dve.wait_ge(S("lru_a"), l + 1)
                    ts(H(11), H(11), -1.0, ALU.mult, 1.0, ALU.add)
                    chain.link(lambda: V.copy_predicated(H(11), la.bitcast(U32), ex))
                    ts(H(11), H(11), 1e-18, ALU.max).then_inc(S("lru_gain"), 1)
                if v == 5:
                    tt(H(9), H(9), H(6), ALU.mult)
                if v == LEVELS:
                    dve.wait_ge(S("lru_root"), l + 1)
                    tt(H(9), H(9), H(11), ALU.mult)
                    for c in range(2):
                        s_ = slice(256 * c, 256 * c + 256)
                        chain.link(lambda: V.tensor_tensor_scan(H(8)[:, s_], H(10)[:, s_], H(9)[:, s_], 0.0, ALU.mult, ALU.add))
                    tt(H(8), H(8), pt(C_G), ALU.mult)
                    put(2, H(8))

            def put(pair, src):
                o = [yT[i][:, 2 * pair:2 * pair + 2, :].rearrange("p c n -> p (c n)") for i in range(2)]
                chain.link(lambda: V.tensor_copy(o[0], src))
                tt(o[1], src, o[0].bitcast(F32), ALU.subtract).then_inc(S("y_put"), 1)

            def hgrn(l):
                one = ones
                b = pt(A_F)
                for i in range(4):
                    s_ = slice(P * i, P * i + P)
                    chain.link(lambda: V.tensor_tensor_scan(b[:, s_], one, tmp(6)[:, s_], 0.0, ALU.mult, ALU.add)).then_inc(S("hg_b"), 1 if i == 3 else 0)

                def diff(v):
                    h = 1 << v
                    bv = b.rearrange("p (n u h) -> p n u h", u=2, h=h)
                    dv = tmp(6 + v % 2).rearrange("p (n u h) -> p n u h", u=2, h=h)
                    n = 512 // (2 * h)
                    mid = bv[:, :, 0, h - 1:h].to_broadcast([P, n, h])
                    tt(dv[:, :, 0, :], mid, bv[:, :, 0, :], ALU.subtract)
                    tt(dv[:, :, 1, :], bv[:, :, 1, :], mid, ALU.subtract).then_inc(S("hg_d"), 1)

                def take(v):
                    dve.wait_ge(S("hg_s"), l * (LEVELS + 1) + v + 2)
                    for p_ in range(2):
                        bank = 2 * ((v + 1) % 2) + p_
                        o = many(mt(1)[:, 512 * p_:512 * p_ + 512])
                        if v < 0:
                            tt(o, many(ps[:, bank, :]), rep(ident, 4), ALU.mult).then_inc(S("hg_take"), 1 if p_ else 0)
                        else:
                            chain.link(lambda: V.copy_predicated(o, rep(lvl(v), 4).bitcast(mybir.dt.uint16), many(ps[:, bank, :]))).then_inc(S("hg_take"), 1 if p_ else 0)

                diff(0)
                diff(1)
                take(-1)
                for v in range(LEVELS):
                    dve.wait_ge(S("hg_e"), l * LEVELS + v + 1)
                    if v >= 2:
                        dve.wait_ge(S("hg_s"), l * (LEVELS + 1) + v)
                    tt(H(4 + v % 2), pt(A_Q), tmp(6 + v % 2), ALU.mult)
                    tt(H(v % 2), tmp(0), tmp(6 + v % 2), ALU.mult).then_inc(S("hg_qk"), 1)
                    if v + 2 < LEVELS:
                        diff(v + 2)
                    if v:
                        take(v - 1)
                    rglru(l, v)
                take(LEVELS - 1)
                dve.wait_ge(S("hg_end"), 2 * (l + 1))
                tt(H(4), pt(A_Q), tmp(6), ALU.mult)
                k0 = cm(tmp(0))[:, :, 0:P]
                tt(H(0)[:, 0:256].rearrange("p (c n) -> p c n", c=2), k0, tmp(7)[:, 0:256].rearrange("p (c n) -> p c n", c=2),
                   ALU.mult).then_inc(S("hg_x"), 1)
                rglru(l, LEVELS)
                dve.wait_ge(S("state"), 3 * l + 1)
                tt(tmp(5)[:, 256:512].rearrange("p (c n) -> p c n", c=2), ps[:, 6, 0:256].rearrange("p (c n) -> p c n", c=2),
                   rep(bdones, 2), ALU.mult).then_inc(S("state_bd"), 1)
                head_out(l, 0, 7, lambda c: pc("hgrn_norm", l, c), pt(A_G), 0)

            def head_out(l, which, bank, gain, gate, pair):
                dve.wait_ge(S("o_rn"), 2 * l + which + 1)
                tt(tmp(7), ps[:, bank, :], tmp(7), ALU.mult)
                for c in range(2):
                    s_ = slice(256 * c, 256 * c + 256)
                    stt(tmp(7)[:, s_], tmp(7)[:, s_], gain(c), gate[:, s_], ALU.mult, ALU.mult)
                put(pair, tmp(7))

            def inverse(i, after=None):
                N, X, Y, T1 = mt(3), mt(4), mt(5), mt(0)
                for v in range(LEVELS):
                    for g in range(2):
                        s_ = slice(512 * g, 512 * g + 512)
                        k = 2 * (LEVELS * i + v) + g + 1
                        dve.wait_ge(S("inv_t"), k)
                        if v == 0:
                            tt(many(T1[:, s_]), many(ps[:, g, :]), rep(lvl(0, True), 4), ALU.mult)
                            tt(many(X[:, s_]), rep(ident, 4), many(T1[:, s_]), ALU.subtract)
                            tt(many(T1[:, s_]), many(N[:, s_]), rep(lvl(0), 4), ALU.mult)
                            tt(many(Y[:, s_]), rep(ident, 4), many(T1[:, s_]), ALU.subtract).then_inc(S("inv_xy"), 1)
                        else:
                            tt(many(T1[:, s_]), many(ps[:, g, :]), rep(lvl(v, True), 4), ALU.mult).then_inc(S("inv_t1"), 1)
                    if after:
                        after(v)
                    if v:
                        for g in range(2):
                            s_ = slice(512 * g, 512 * g + 512)
                            dve.wait_ge(S("inv_p"), 2 * ((LEVELS - 1) * i + v - 1) + g + 1)
                            if v < LEVELS - 1:
                                tt(X[:, s_], X[:, s_], ps[:, 2 + g, :], ALU.subtract)
                            tt(Y[:, s_], Y[:, s_], ps[:, 4 + g, :], ALU.subtract).then_inc(S("inv_xy"), 1)

            def rwkv_ahead(l, v):
                if v == 0:
                    for c in range(2):
                        s_ = slice(256 * c, 256 * c + 256)
                        ts(K_KK[:, s_], pt(D_K)[:, s_], pc("rwkv_k_k", l, c), ALU.mult).then_inc(S("rk_kk"), 1 if c else 0)
                    for c in range(2):
                        s_ = slice(256 * c, 256 * c + 256)
                        ts(K_KA[:, s_], pt(D_W)[:, s_], -1.0, ALU.add, pc("rwkv_k_a", l, c), ALU.mult)
                if v == 1:
                    stt(pt(D_K), K_KA, 1.0, pt(D_K), ALU.add, ALU.mult)
                    ts(pt(C_X), pt(C_X), -float(np.exp(-0.5)), ALU.mult)
                    for i in range(4):
                        s_ = slice(P * i, P * i + P)
                        chain.link(lambda: V.tensor_tensor_scan(K_B[:, s_], ones, pt(C_X)[:, s_], 0.0, ALU.mult, ALU.add))
                    ts(col(ST_NC0, 4).unsqueeze(2), many(K_B)[:, :, HD - 1:HD], -1.0, ALU.mult)
                    tt(K_BM, K_B, pt(C_X), ALU.subtract).then_inc(S("rk_b"), 1)
                if v == 3:
                    dve.wait_ge(S("rk_rn"), l + 1)
                    tt(K_KK, K_KK, K_RN, ALU.mult)
                    tt(K_KA, K_KK, pt(D_W), ALU.mult)
                if v == 5:
                    dve.wait_ge(S("rk_e"), 2 * (l + 1))
                    tt(pt(A_I), pt(D_R), K_E, ALU.mult)
                    tt(pt(A_G), pt(D_K), K_EN, ALU.mult)
                    tt(pt(B_Q), K_KA, K_EN, ALU.mult)
                if v == 6:
                    tt(pt(B_K), K_KK, K_EM, ALU.mult)
                    tt(cm(pt(B_V))[:, :, 0:P], cm(pt(D_K))[:, :, 0:P], cm(pt(A_Q))[:, :, 0:P], ALU.mult)
                    tt(cm(pt(B_V))[:, :, P:], cm(pt(D_R))[:, :, P:], cm(pt(A_Q))[:, :, P:], ALU.mult)
                    tt(cm(pt(C_X))[:, :, 0:P], cm(K_KA)[:, :, 0:P], cm(pt(A_Q))[:, :, 0:P], ALU.mult)
                    tt(cm(pt(C_X))[:, :, P:], cm(K_KK)[:, :, P:], cm(pt(A_F))[:, :, P:], ALU.mult)
                    tt(K_B, pt(D_R), pt(D_K), ALU.mult)
                    for c in range(2):
                        s_ = slice(256 * c, 256 * c + 256)
                        ts(K_B[:, s_], K_B[:, s_], pc("rwkv_r_k", l, c), ALU.mult).then_inc(S("rk_ops"), 1 if c else 0)

            def deltanet(l):
                chain.link(lambda: V.tensor_copy(many(tmp(6), 8), col(ST_G, 8).unsqueeze(2).to_broadcast([P, 8, HD])))
                for t in range(TT):
                    chain.link(lambda: V.tensor_copy(tmp(7)[:, 256 * t:256 * t + 256].rearrange("p (h n) -> p h n", h=4),
                                       beta[:, t, :].unsqueeze(2).to_broadcast([P, 4, HD]))).then_inc(S("gd_wide"), 1 if t else 0)
                dve.wait_ge(S("gd_rn"), 2 * (l + 1))
                stt(pt(B_Q), pt(B_Q), HD ** -0.5, G_N[0], ALU.mult, ALU.mult)
                tt(pt(B_K), pt(B_K), G_N[1], ALU.mult)
                dve.wait_ge(S("gd_cum"), l + 1)
                chain.link(lambda: V.tensor_copy(col(ST_GC, 16), ps[:, 5, 0:16]))
                tt(col(ST_GD, 8), col(ST_GTOT, 8), col(ST_GC, 8), ALU.subtract).then_inc(S("gd_gd"), 1)
                for p_ in range(2):
                    for t in range(TT):
                        for c in range(2):
                            a_ = at(p_, t, c)
                            ts(mt(1)[:, a_:a_ + P], ps[:, p_, a_ % 512:a_ % 512 + P], col(ST_GC + 4 * t + 2 * c + p_),
                               ALU.subtract, 0.0, ALU.min).then_inc(S("gd_diff"), 1 if a_ == at(1, 1, 1) else 0)
                dve.wait_ge(S("gd_eg"), l + 1)
                tt(tmp(0), pt(B_Q), tmp(5), ALU.mult)
                tt(tmp(1), pt(B_K), ps[:, 3, :], ALU.mult)
                tt(tmp(2), tmp(1), tmp(5), ALU.mult).then_inc(S("gd_ops"), 1)
                dve.wait_ge(S("gd_trk"), l + 1)
                dk = col(ST_GD, 4).unsqueeze(2).to_broadcast([P, 4, HD])
                tt(tmp(3)[:, 0:256].rearrange("p (h n) -> p h n", h=4), ps[:, 4, 0:256].rearrange("p (h n) -> p h n", h=4), dk, ALU.mult)
                for t in range(TT):
                    bt = beta[:, t, :].unsqueeze(2).to_broadcast([P, 4, HD])
                    tt(tmp(4)[:, 256 * t:256 * t + 256].rearrange("p (h n) -> p h n", h=4),
                       ps[:, 5, 256 * t:256 * t + 256].rearrange("p (h n) -> p h n", h=4), bt, ALU.mult)
                dve.wait_ge(S("gd_rel"), l + 1)
                tt(many(mt(1), 8), many(mt(1), 8), rep(incl, 8), ALU.mult)
                dve.wait_ge(S("gd_sc"), 2 * l + 1)
                tt(mt(3), ps[:, 6:8, :].rearrange("p b n -> p (b n)"), mt(1), ALU.mult)
                tt(many(mt(3), 8), many(mt(3), 8), rep(strict, 8), ALU.mult)
                dve.wait_ge(S("gd_sc"), 2 * l + 2)
                tt(mt(2), ps[:, 2:4, :].rearrange("p b n -> p (b n)"), mt(1), ALU.mult).then_inc(S("inv_n"), 1)
                inverse(2 * l, after=lambda v: rwkv_ahead(l, v))
                dve.wait_ge(S("state"), 3 * l + 2)
                tt(tmp(3)[:, 256:512].rearrange("p (c n) -> p c n", c=2), ps[:, 7, 0:256].rearrange("p (c n) -> p c n", c=2),
                   rep(bdones, 2), ALU.mult).then_inc(S("state_bd"), 1)
                dve.wait_ge(S("gd_km"), l + 1)
                tt(tmp(4)[:, 256:512], tmp(4)[:, 256:512], ps[:, 7, 256:512], ALU.subtract).then_inc(S("gd_r1"), 1)
                head_out(l, 1, 0, lambda c: pc("gdn_norm", l), pt(B_Z), 1)

            def rwkv(l):
                for i, (bank, dst, mask) in enumerate(((2, mt(1), strict), (4, mt(2), incl), (0, mt(3), strict), (6, PT[:, 0:1024], incl))):
                    dve.wait_ge(S("rk_sc"), 4 * l + i + 1)
                    last = stt(many(dst, 8), many(ps[:, bank:bank + 2, :].rearrange("p b n -> p (b n)"), 8), 1e30, rep(mask, 8),
                               ALU.min, ALU.mult)
                    if bank == 0:
                        last.then_inc(S("inv_n"), 1)
                last.then_inc(S("rk_m"), 1)
                inverse(2 * l + 1)
                dve.wait_ge(S("state"), 3 * l + 3)
                tt(tmp(3)[:, 0:256].rearrange("p (c n) -> p c n", c=2), ps[:, 5, 0:256].rearrange("p (c n) -> p c n", c=2),
                   rep(bdones, 2), ALU.mult).then_inc(S("state_bd"), 1)
                dve.wait_ge(S("rk_mean"), l + 1)
                stt(tmp(0), ps[:, 1, :], -1.0 / HD, tmp(0), ALU.mult, ALU.add).then_inc(S("rk_yc"), 1)
                dve.wait_ge(S("rk_bonus"), l + 1)
                tt(tmp(2), ps[:, 3, :], pt(D_V), ALU.mult)
                dve.wait_ge(S("rk_gn"), l + 1)
                tt(tmp(0), tmp(0), tmp(1), ALU.mult)
                for c in range(2):
                    s_ = slice(256 * c, 256 * c + 256)
                    ts(tmp(0)[:, s_], tmp(0)[:, s_], pc("rwkv_ln_w", l, c), ALU.mult, pc("rwkv_ln_b", l, c), ALU.add)
                tt(tmp(0), tmp(0), tmp(2), ALU.add)
                tt(tmp(0), tmp(0), H(12), ALU.mult).then_inc(S("mix_done"), 1)
                put(3, tmp(0))

            def attention(l):
                stats(2 + 3 * l, x, xs)
                cm_steps(first_chunk["xattn_wk", l], 4)
                norm(2 + 3 * l, lambda c: pc("norm_xattn", l, c), hT)
                cm_steps(first_chunk["xattn_wv", l], 4)
                cm_steps(first_chunk["xattn_wq", l], 4)
                for b in range(4):
                    dve.wait_ge(S("at_s"), 4 * l + b + 1)
                    chain.link(lambda: V.tensor_reduce(col(ST_MX + 2 * b, 2), ps[:, b, :].rearrange("p (h n) -> p h n", h=2), AX, ALU.max))
                    ts(col(ST_MX + 2 * b, 2), col(ST_MX + 2 * b, 2), -1.0, ALU.mult).then_inc(S("at_max"), 1)
                dve.wait_ge(S("at_exp"), 8 * (l + 1))
                chain.link(lambda: V.reciprocal(col(ST_RS, 8), col(ST_SUM, 8)))
                for i in range(8):
                    ts(pr[:, i // NH, i % NH, :], pr[:, i // NH, i % NH, :], col(ST_RS + i), ALU.mult).then_inc(S("at_p"), 1)
                for b in range(4):
                    dve.wait_ge(S("at_hi"), 4 * l + b + 1)
                    o = [yT[i][:, 2 * b:2 * b + 2, :].rearrange("p c n -> p (c n)") for i in range(2)]
                    tt(o[1], ps[:, b, :], o[0].bitcast(F32), ALU.subtract).then_inc(S("at_lo"), 1)
                tm_add(first_chunk["xattn_wo", l], 4)

            def swiglu():
                stats(3, x, xs)
                norm(3, lambda c: pc("norm_ffn", 0, c), hT)
                for j in range(FSTEPS):
                    n = ff_chunk(j)
                    ahead(n + SPL)
                    dve.wait_ge(S("ff_silu"), j + 1)
                    dve.wait_ge(S("chunk_done"), n + 2)
                    m = mt(1)[:, 512 * (j % 2):512 * (j % 2) + 512]
                    tt(m, mt(0)[:, 0:512], ps[:, 2 * (j % 2) + 1, :], ALU.mult).then_inc(S("ff_prod"), 1)
                    ahead(n + 1 + SPL)
                    dve.wait_ge(S("ff_hi"), j + 1)
                    tt(actT[j % 2][1], m, actT[j % 2][0].bitcast(F32), ALU.subtract).then_inc(S("ff_lo"), 1)
                tm_add(ff_down(FSTEPS - 1), 1)

            def experts():
                stats(6, x, xs)
                norm(6, lambda c: pc("norm_ffn", 1, c), hT)
                chain.link(lambda: V.memset(col(6), 0.0)).then_inc(S("ex_prod"), 1)
                chain.link(lambda: V.memset(col(6), 0.0)).then_inc(S("ex_alo"), 1)
                chain.link(lambda: V.memset(onehT, 0.0)).then_inc(S("ex_selT"), 1)
                chain.link(lambda: V.memset(yE, 0.0)).then_inc(S("ex_add"), 1)
                chain.link(lambda: V.memset(col(ST_BASE, NE), 0.0))
                chain.link(lambda: V.memset(col(ST_BASE + NE, NE), float(P)))
                dve.wait_ge(S("rt_mm"), 1)
                chain.link(lambda: V.tensor_copy(AB_T, ps[0:8, 0, 0:SEQ])).then_inc(S("sm_ready"), 1)
                dve.wait_ge(S("rt_mm"), 2)
                lg, sel, gate, rank = (col(a_, 16).rearrange("p (t n) -> p t n", t=2) for a_ in (ST_LG, ST_SEL, ST_GATE, ST_RANK))
                iota8 = con[:, C_IOTA:C_IOTA + 8]
                chain.link(lambda: V.tensor_copy(col(ST_LG, 16), ps[:, 1, 0:16]))
                for t in range(TT):
                    top, idx, idf = col(ST_TOP, 8), mt(5)[:, 8 * t:8 * t + 8].bitcast(U32), mt(5)[:, 16 + 8 * t:24 + 8 * t]
                    chain.link(lambda: V.max(top, lg[:, t, :]))
                    chain.link(lambda: V.max_index(idx, top, lg[:, t, :]))
                    chain.link(lambda: V.tensor_copy(idf, idx))
                    tt(col(ST_W + 2 * t), col(ST_TOP), col(ST_TOP + 1), ALU.subtract)
                    ts(col(ST_W + 2 * t + 1), col(ST_W + 2 * t), -1.0, ALU.mult).then_inc(S("rt_d"), 1 if t else 0)
                dve.wait_ge(S("rt_p"), 1)
                for t in range(TT):
                    idf = mt(5)[:, 16 + 8 * t:24 + 8 * t]
                    o = mt(5)[:, 32:48]
                    for k in range(2):
                        ts(o[:, 8 * k:8 * k + 8], iota8, idf[:, k:k + 1], ALU.is_equal)
                    tt(sel[:, t, :], o[:, 0:8], o[:, 8:16], ALU.add)
                    ts(o[:, 0:8], o[:, 0:8], col(ST_W + 2 * t), ALU.mult)
                    stt(gate[:, t, :], o[:, 8:16], col(ST_W + 2 * t + 1), o[:, 0:8], ALU.mult, ALU.add).then_inc(S("rt_d"), 1 if t else 0)
                dve.wait_ge(S("rt_mm"), 3)
                stt(col(ST_RANK, 16), ps[:, 1, 0:16], 1.0, col(ST_SEL, 16), ALU.add, ALU.mult)
                ts(col(ST_RANK, 16), col(ST_RANK, 16), -1.0, ALU.add)

                def chunk(h, m, q):
                    slot = ex_slot(q)
                    dve.wait_ge(S("w_hi"), ex_count(h * 2 + m, q))
                    V.tensor_tensor(wlo[slot][:, :], ex_raw[ex_raw_slot(m, q)], whi[slot][:, :].bitcast(F32),
                                    ALU.subtract).then_inc(S("w_lo"), 1)

                def prod(s, up_done):
                    dve.wait_ge(S("ex_silu"), s + 1)
                    dve.wait_ge(S("chunk_done"), up_done)
                    dve.wait_ge(S("ex_tr"), s + 1)
                    V.tensor_tensor(mt(1)[:, 0:256], mt(0)[:, 0:256], ps[:, 1, 0:256], ALU.mult).then_inc(S("ex_prod"), 1)

                def act_lo(s):
                    dve.wait_ge(S("ex_ahi"), s + 1)
                    V.tensor_tensor(actT[0][1][:, 0:256], ps[:, 2, 0:256], actT[0][0][:, 0:256].bitcast(F32),
                                    ALU.subtract).then_inc(S("ex_alo"), 1)

                def one_hots(p, first=False):
                    expert = 0 if first else dve.value_load(gather_expert[0:1, bass.ds(p, 1)], min_val=0, max_val=NE - 1)
                    for t in range(TT):
                        rk = col(ST_RANK + 8 * t, 8)[:, bass.ds(expert, 1)]
                        gt = col(ST_GATE + 8 * t, 8)[:, bass.ds(expert, 1)]
                        o, og = oneh[:, P * t:P * t + P], onehg[:, P * t:P * t + P]
                        V.tensor_scalar(o, con[:, C_IOTA:C_IOTA + P], col(ST_BASE, 16)[:, bass.ds(p, 1)], rk,
                                        ALU.add, ALU.is_equal).then_inc(S("ex_one"), 1)
                        dve.wait_ge(S("ex_one"), p * 2 + (t + 1))
                        V.tensor_scalar(og, o, gt, None, ALU.mult).then_inc(S("ex_sel"), 1)

                def gathered(p, cs):
                    for c in cs:
                        dve.wait_ge(S("ex_hi"), p * KT + (KT // 2 if c < KT // 2 else KT))
                        V.scalar_tensor_tensor(out=hE[1][:, c, :], in0=g_tokens(c), scalar=pc("norm_ffn", 1, c),
                                               in1=hE[0][:, c, :].bitcast(F32), op0=ALU.mult, op1=ALU.subtract).then_inc(S("ex_hlo"), 1)

                def scattered(q, hf):
                    for t in range(TT):
                        dve.wait_ge(S("ex_sc"), q * 4 + (2 * hf + t + 1))
                        s_ = slice(512 * hf, 512 * hf + 512)
                        V.tensor_tensor(x[:, t, s_], x[:, t, s_], ps[:, 6 + t, :], ALU.add).then_inc(S("ex_x"), 1)

                chain.settle()
                one_hots(0, first=True)
                chain.link(lambda: V.tensor_copy(col(ST_TOTAL, NE), ps[:, 1, 16:16 + NE]))
                ts(col(ST_OVER, NE), iota8, -1.0, ALU.mult, float(NE), ALU.add)
                stt(col(ST_OVER, NE), col(ST_TOTAL, NE), float(P), col(ST_OVER, NE), ALU.is_gt, ALU.mult)
                chain.link(lambda: V.max(col(ST_TOTAL, NE), col(ST_OVER, NE)))
                ts(col(ST_OVER, NE), col(ST_TOTAL, NE), 0.0, ALU.is_gt)
                chain.link(lambda: V.tensor_reduce(col(ST_N1), col(ST_OVER, NE), AX, ALU.add))
                ts(col(ST_N1), col(ST_N1), float(NE), ALU.add)
                chain.link(lambda: V.tensor_copy(pass_count, col(ST_N1)))
                ts(col(ST_TOTAL, NE), col(ST_TOTAL, NE), -1.0, ALU.mult, float(NE), ALU.add)
                chain.link(lambda: V.tensor_copy(pass_expert[:, 0:NE], iota8))
                chain.link(lambda: V.tensor_copy(pass_expert[:, NE:2 * NE], col(ST_TOTAL, NE)))
                ts(col(ST_TOTAL, NE), col(ST_TOTAL, NE), float(NE - 1), ALU.min)
                chain.link(lambda: V.tensor_copy(gather_expert[:, 0:NE], iota8))
                chain.link(lambda: V.tensor_copy(gather_expert[:, NE:2 * NE], col(ST_TOTAL, NE))).then_inc(S("ex_table"), 1)
                chain.settle()
                dve.wait_ge(S("ex_table"), 1)
                count = dve.value_load(pass_count[0:1, 0:1], min_val=NE, max_val=NE + SECONDS)
                gathered(0, range(KT))
                with dve.Fori(0, NE + SECONDS) as ep:
                    which = dve.value_load(pass_expert[0:1, bass.ds(ep, 1)], min_val=0, max_val=NE)
                    with dve.If(which < NE):
                        h = ep * (ESTEPS // 2)
                        r = ep * ESTEPS
                        chunk(h, 0, 0)
                        chunk(h, 0, 1)
                        chunk(h, 0, 2)
                        prod(r, ex_count(r, 1))
                        scattered(ep, 0)
                        chunk(h, 0, 3)
                        act_lo(r)
                        scattered(ep, 1)
                        chunk(h, 0, 4)
                        dve.wait_ge(S("ex_x"), ep * 4 + 4)
                        V.memset(col(6), 0.0).then_inc(S("ex_add"), 1)
                        dve.wait_ge(S("ex_gt"), ep + 1)
                        V.tensor_copy(onehT, ps[:, 3, 0:256]).then_inc(S("ex_selT"), 1)
                        one_hots(ep + 1)
                        with dve.Fori(0, (ESTEPS - 2) // 2) as i:
                            for m in (1, 2):
                                chunk(h + i, m, 2)
                                prod(r + i * 2 + m, ex_count(r + i * 2 + (m - 1), 3))
                                chunk(h + i, m, 3)
                                act_lo(r + i * 2 + m)
                                chunk(h + i, m, 4)
                        chunk(h, ESTEPS - 1, 2)
                        prod(r + (ESTEPS - 1), ex_count(r + (ESTEPS - 2), 3))
                        gathered(ep + 1, range(KT // 2))
                        act_lo(r + (ESTEPS - 1))
                        gathered(ep + 1, range(KT // 2, KT))
                for hf in range(2):
                    scattered(count, hf)
                dve.wait_ge(S("ex_x"), count * 4 + 4)

            chain.link(lambda: V.memset(col(10), 1.0))
            chain.link(lambda: V.memset(col(8), EPS))
            chain.link(lambda: V.memset(col(9), GN_EPS)).then_inc(S("eps"), 1)
            dve.wait_ge(S("tables_in"), 32)
            for l in range(DEPTH):
                stats(norm_index(l), x, xs)
                norm(norm_index(l), lambda c: pc("norm_mix", l, c), hT)
                if l == 0:
                    ahead(SPL)
                    split_small(0)
                    dve.wait_ge(S("mem_in"), 32)
                    stats(MEM_NORM, mem, mem)
                cm_steps(first_chunk["w_in", l], 14, after=lambda j: gates_ahead(l, j))
                gates(l)
                logs(l)
                hgrn(l)
                deltanet(l)
                rwkv(l)
                split_small(l + 1)
                tm_add(first_chunk["w_out", l], 4)
                attention(l)
                if l == 0:
                    swiglu()
            experts()
            chain.link(lambda: V.memset(col(7), 0.0)).then_inc(S("x_done"), 1)
            stats(7, x, x)
            dve.wait_ge(S("nf_in"), 16)
            for t in range(TT):
                tt(x[:, t, :], x[:, t, :], final_gain, ALU.mult).then_inc(S("x_done"), 1 if t else 0)

        @block.tensor
        def _(pe):
            cmi = [0]

            def mm(o, lhsT, rhs, start=True, stop=True):
                return Signalled(pe.matmul(o, lhsT, rhs, start=start, stop=stop, skip_group_check=True))

            def tr(o, i):
                return Signalled(pe.transpose(o, i, ident))

            PASSES = ((0, 0), (1, 0), (0, 1))

            def cm_product(n, src, bank):
                pe.wait_ge(S("w_lo"), n + 1)
                wp = [chunk_view(v[n % SPL][:, :], "cm") for v in (whi, wlo)]
                for m in range(2):
                    for i, (a_, b_) in enumerate(PASSES):
                        for k in range(KT):
                            last = i == 2 and k == KT - 1
                            ins = pe.matmul(ps[:, bank, SEQ * m:SEQ * m + SEQ], wp[a_][:, k, P * m:P * m + P], src[b_][:, k, :],
                                            start=i == 0 and k == 0, stop=last)
                ins.then_inc(S("chunk_done"), 1)

            def cm_phase(n0, count, src, after=None):
                for j in range(count):
                    if after:
                        after(j)
                    if cmi[0] >= 4:
                        pe.wait_ge(S("cm_free"), cmi[0] - 3)
                    cm_product(n0 + j, src, cmi[0] % 4)
                    cmi[0] += 1

            def tm_product(n, src, first, last):
                pe.wait_ge(S("w_lo"), n + 1)
                wp = [chunk_view(v[n % SPL][:, :], "tm") for v in (whi, wlo)]
                for kk in range(TM_ROWS):
                    for t in range(TT):
                        for hf in range(2):
                            for i, (a_, b_) in enumerate(PASSES):
                                ins = pe.matmul(ps[:, 4 + 2 * t + hf, :], src(b_, kk, t), wp[a_][:, kk, 512 * hf:512 * hf + 512],
                                                start=first and kk == 0 and i == 0, stop=last and kk == TM_ROWS - 1 and i == 2)
                ins.then_inc(S("chunk_done"), 1)

            def tm_phase(n0, src):
                for j in range(4):
                    tm_product(n0 + j, lambda b_, kk, t: src[b_][:, TM_ROWS * j + kk, P * t:P * t + P], j == 0, j == 3)

            def norm(i):
                for t in range(TT):
                    pe.wait_ge(S("n_xs"), TT * i + t + 1)
                    for c in range(KT):
                        tr(ps[:, c, P * t:P * t + P], xs[:, t, P * c:P * c + P]).then_inc(S("n_tr"), 1 if t else 0)
                pe.wait_ge(S("n_lo"), (i + 1) * KT)

            def small_product(bank, k):
                pe.wait_ge(S("wsm_split"), k + 1)
                for i, (a_, b_) in enumerate(PASSES):
                    for kk in range(KT):
                        ins = pe.matmul(ps[0:8, bank, 0:SEQ], small[a_][:, kk, :], hT[b_][:, kk, :],
                                        start=i == 0 and kk == 0, stop=i == 2 and kk == KT - 1)
                return ins

            def small_turn(bank, k):
                pe.wait_ge(S("sm_ready"), 2 * k + 1)
                for t in range(TT):
                    last = Signalled(pe.transpose(ps[:, bank, 8 * t:8 * t + 8], AB_T[:, P * t:P * t + P], ident[0:8, 0:8]))
                return last

            def gates_ahead(l, j):
                if j == 1:
                    small_product(7, l).then_inc(S("ab_mm"), 1)
                if j == 2:
                    small_turn(7, l).then_inc(S("ab_mm"), 1)
                if l == 0 and 1 <= j <= KT // 2:
                    pe.wait_ge(S("n_xs"), 2 * (MEM_NORM + 1))
                    pe.wait_ge(S("n_lo"), MEM_NORM * KT + 2 * j - 2)
                    for c in (2 * j - 2, 2 * j - 1):
                        for t in range(TT):
                            tr(ps[:, 4 + c % 2, P * t:P * t + P], mem[:, t, P * c:P * c + P]).then_inc(S("n_tr"), 1 if t else 0)
                if j != 7:
                    return
                pe.wait_ge(S("n_lo"), (MEM_NORM + 1) * KT)
                pe.wait_ge(S("sw_in"), 16 * (l + 1))
                pe.wait_ge(S("conv_l"), l + 1)
                for c in range(2):
                    for g in range(2):
                        mm(ps[:, 5 + g, 256 * c:256 * c + 256], sw[:, SW_LRU + P * (2 * g + c):SW_LRU + P * (2 * g + c + 1)],
                           H(6)[:, 256 * c:256 * c + 256]).then_inc(S("lru_mm"), 1 if c and g else 0)

            def gates(l):
                pe.wait_ge(S("cm_free"), cmi[0])
                pe.wait_ge(S("lora_in"), l + 1)
                for c in range(2):
                    mm(ps[:, 2, 256 * c:256 * c + 256], sw[0:64, SW_WA + P * c:SW_WA + P * c + P], pt(D_W, 1)[0:64, :])
                for c in range(2):
                    mm(ps[:, 3, 256 * c:256 * c + 256], sw[64:128, SW_WA + P * c:SW_WA + P * c + P], pt(D_W, 1)[64:128, :])
                for c in range(2):
                    mm(ps[:, 4, 256 * c:256 * c + 256], sw[:, SW_G2 + P * c:SW_G2 + P * c + P], pt(D_G, 1)).then_inc(S("lora_mm"), 1 if c else 0)
                if l:
                    pe.wait_ge(S("lru_ri"), 2 * (l + 1))
                    for c in range(2):
                        mm(ps[0:32, 5, 0:256], sw[:, SW_V1 + 32 * c:SW_V1 + 32 * c + 32], pt(D_V + c, 1), start=c == 0, stop=c == 1).then_inc(S("vmix_mm"), 1 if c else 0)
                    pe.wait_ge(S("vmix1"), 1)
                    for c in range(2):
                        mm(ps[:, 6, 256 * c:256 * c + 256], sw[0:32, SW_V2 + P * c:SW_V2 + P * c + P], H(13)[0:32, 0:256]).then_inc(S("vmix_mm"), 1 if c else 0)

            def scores(bank, k_, q_):
                for p_ in range(2):
                    for t in range(TT):
                        for c in range(2):
                            s_ = slice(256 * c + P * t, 256 * c + P * t + P)
                            a_ = at(0, t, c)
                            last = mm(ps[:, bank + p_, a_:a_ + P], k_[64 * p_:64 * p_ + 64, s_], q_[64 * p_:64 * p_ + 64, s_])
                return last

            def hgrn(l):
                pe.wait_ge(S("lora_s"), l + 1)
                if l:
                    pe.wait_ge(S("vmix2"), 2)
                for t in range(TT):
                    for c in range(2):
                        last = t == 1 and c == 1
                        tr(ps[:, 4, 256 * t + P * c:256 * t + P * c + P], pt(A_I + c, 1)[:, P * t:P * t + P]).then_inc(S("hg_tr"), 1 if last else 0)
                pe.wait_ge(S("s_kA"), l + 1)
                pe.wait_ge(S("hg_b"), l + 1)
                scores(0, tmp(0), pt(A_Q)).then_inc(S("hg_s"), 1)
                for v in range(LEVELS):
                    pe.wait_ge(S("hg_qk"), l * LEVELS + v + 1)
                    if v:
                        pe.wait_ge(S("hg_take"), l * (LEVELS + 1) + v)
                    scores(2 * ((v + 1) % 2), H(v % 2), H(4 + v % 2)).then_inc(S("hg_s"), 1)
                pe.wait_ge(S("hg_take"), l * (LEVELS + 1) + LEVELS)
                pe.wait_ge(S("gd_sq"), l + 1)
                for j in range(2):
                    mm(ps[:, j, :], bdones, G_N[j]).then_inc(S("gd_ss"), 1 if j else 0)
                pe.wait_ge(S("hg_x"), l + 1)
                for c in range(2):
                    tr(ps[:, 5, P * c:P * c + P], H(0)[:, P * c:P * c + P]).then_inc(S("hg_trk"), 1 if c else 0)
                pe.wait_ge(S("hg_v"), l + 1)
                pe.wait_ge(S("hg_kd"), l + 1)
                for c in range(2):
                    mm(ps[:, 6, P * c:P * c + P], tmp(5)[:, P * c:P * c + P], tmp(1)[:, P * c:P * c + P]).then_inc(S("state"), 1 if c else 0)
                pe.wait_ge(S("state_bd"), 3 * l + 1)
                outputs(7, [(tmp(1), mt(1))], tmp(5)[:, 256:512], H(4)).then_inc(S("o_full"), 1)
                head_ss(l, 0)

            def outputs(bank, pairs, state, q_):
                for c in range(2):
                    for t in range(TT):
                        o_ = 256 * c + P * t
                        if t:
                            mm(ps[:, bank, o_:o_ + P], state[:, P * c:P * c + P], q_[:, 256 * c + P:256 * c + 256], stop=False)
                        for i, (v_, s_) in enumerate(pairs):
                            for p_ in range(2):
                                last = mm(ps[64 * p_:64 * p_ + 64, bank, o_:o_ + P],
                                   v_[:, 256 * t + P * c + 64 * p_:256 * t + P * c + 64 * p_ + 64],
                                   s_[:, at(p_, t, c):at(p_, t, c) + P], start=t == 0 and i == 0, stop=i == len(pairs) - 1)
                return last

            def head_ss(l, which):
                pe.wait_ge(S("o_sq"), 2 * l + which + 1)
                mm(ps[:, 6, :], bdones, tmp(6)).then_inc(S("o_ss"), 1)

            def inverse(i, after=None):
                N, X, Y, T1 = mt(3), mt(4), mt(5), mt(0)
                pe.wait_ge(S("inv_n"), i + 1)
                for v in range(LEVELS):
                    for g in range(2):
                        if v:
                            pe.wait_ge(S("inv_xy"), 2 * (LEVELS * i + v - 1) + g + 1)
                        for k in range(4):
                            s_ = slice(512 * g + P * k, 512 * g + P * k + P)
                            mm(ps[:, g, P * k:P * k + P], N[:, s_], X[:, s_] if v else ident).then_inc(S("inv_t"), 1 if k == 3 else 0)
                    if v:
                        for g in range(2):
                            pe.wait_ge(S("inv_t1"), 2 * ((LEVELS - 1) * i + v - 1) + g + 1)
                            for k in range(4):
                                s_ = slice(512 * g + P * k, 512 * g + P * k + P)
                                if v < LEVELS - 1:
                                    mm(ps[:, 2 + g, P * k:P * k + P], Y[:, s_], T1[:, s_])
                                mm(ps[:, 4 + g, P * k:P * k + P], T1[:, s_], Y[:, s_]).then_inc(S("inv_p"), 1 if k == 3 else 0)
                    if after:
                        after(v)
                pe.wait_ge(S("inv_xy"), 2 * LEVELS * (i + 1))

            def solve(bank, t, r_):
                for h in range(NH):
                    a_ = at(h % 2, t, h // 2)
                    last = mm(ps[:, bank, 256 * t + HD * h:256 * t + HD * h + HD], mt(5)[:, a_:a_ + P], r_[:, 256 * t + HD * h:256 * t + HD * h + HD])
                return last

            def deltanet(l):
                pe.wait_ge(S("gd_g"), l + 1)
                g8 = col(ST_G, 8)
                mm(ps[:, 5, 0:8], incl, g8)
                mm(ps[:, 5, 8:16], ones, g8)
                pe.wait_ge(S("gd_rn"), 2 * (l + 1))
                pe.wait_ge(S("gd_wide"), l + 1)
                for p_ in range(2):
                    for t in range(TT):
                        for c in range(2):
                            a_ = at(0, t, c)
                            k = ST_G + 4 * t + 2 * c + p_
                            mm(ps[:, p_, a_:a_ + P], col(k).to_broadcast([P, P]), incl)
                for c in range(2):
                    for t in range(TT):
                        o_ = 256 * c + P * t
                        w_ = 256 * t + P * c
                        mm(ps[:, 4, o_:o_ + P], tmp(6)[:, w_:w_ + P], incl)
                        mm(ps[:, 3, o_:o_ + P], tmp(7)[:, w_:w_ + P], ident).then_inc(S("gd_cum"), 1 if c and t else 0)
                pe.wait_ge(S("gd_gd"), l + 1)
                pe.wait_ge(S("gd_ops"), l + 1)
                for c in range(2):
                    tr(ps[:, 4, P * c:P * c + P], pt(B_K + c, 1)[:, 0:P])
                for t in range(TT):
                    for c in range(2):
                        tr(ps[:, 5, 256 * t + P * c:256 * t + P * c + P], pt(B_V + c, 1)[:, P * t:P * t + P]).then_inc(S("gd_trk"), 1 if t and c else 0)
                scores(6, pt(B_K), tmp(1)).then_inc(S("gd_sc"), 1)
                scores(2, pt(B_K), pt(B_Q)).then_inc(S("gd_sc"), 1)
                def rwkv_ahead(v):
                    if v == 1:
                        pe.wait_ge(S("rk_sq"), l + 1)
                        mm(ps[:, 6, :], bdones, K_RN).then_inc(S("rk_ss"), 1)

                inverse(2 * l, after=rwkv_ahead)
                pe.wait_ge(S("rk_rn"), l + 1)
                solve(6, 0, tmp(4)).then_inc(S("gd_u"), 1)
                pe.wait_ge(S("gd_us"), 2 * l + 1)
                for c in range(2):
                    mm(ps[:, 7, P * c:P * c + P], tmp(3)[:, P * c:P * c + P], tmp(6)[:, P * c:P * c + P]).then_inc(S("state"), 1 if c else 0)
                pe.wait_ge(S("state_bd"), 3 * l + 2)
                for c in range(2):
                    mm(ps[:, 7, 256 + P * c:256 + P * c + P], tmp(2)[:, 256 * c + P:256 * c + 256], tmp(3)[:, 256 + P * c:256 + P * c + P]).then_inc(S("gd_km"), 1 if c else 0)
                pe.wait_ge(S("gd_r1"), l + 1)
                solve(6, 1, tmp(4)).then_inc(S("gd_u"), 1)
                pe.wait_ge(S("gd_us"), 2 * l + 2)
                outputs(0, [(tmp(6), mt(2))], tmp(3)[:, 256:512], tmp(0)).then_inc(S("o_full"), 1)
                head_ss(l, 1)

            def rwkv(l):
                pe.wait_ge(S("rk_ops"), l + 1)
                scores(2, pt(A_G), pt(B_K)).then_inc(S("rk_sc"), 1)
                scores(4, pt(A_G), pt(A_I)).then_inc(S("rk_sc"), 1)
                pe.wait_ge(S("y_put"), 4 * l + 3)
                scores(0, pt(B_Q), pt(B_K)).then_inc(S("rk_sc"), 1)
                scores(6, pt(B_Q), pt(A_I)).then_inc(S("rk_sc"), 1)

                def turn_operands(v):
                    if v != 1:
                        return
                    pe.wait_ge(S("rk_m"), l + 1)
                    for t in range(TT):
                        for c in range(2):
                            tr(ps[:, 6, 256 * t + P * c:256 * t + P * c + P], pt(D_V + c, 1)[:, P * t:P * t + P])
                    for i, m_ in enumerate((B_V, C_X)):
                        for c in range(2):
                            tr(ps[:, 7, 256 * i + P * c:256 * i + P * c + P], pt(m_ + c, 1)[:, 0:P]).then_inc(S("rk_trv"), 1 if i and c else 0)

                inverse(2 * l + 1, after=turn_operands)
                pe.wait_ge(S("rk_vk"), l + 1)

                def right_side(t):
                    for c in range(2):
                        o_ = 256 * t + P * c
                        if t:
                            mm(ps[:, 6, o_:o_ + P], pt(C_X)[:, 256 * c + P:256 * c + 256], tmp(3)[:, P * c:P * c + P], stop=False)
                        for p_ in range(2):
                            mm(ps[:, 6, o_ + 64 * p_:o_ + 64 * p_ + 64], mt(1)[:, at(p_, t, c):at(p_, t, c) + P],
                               tmp(5)[:, o_ + 64 * p_:o_ + 64 * p_ + 64], start=t == 0).then_inc(S("rk_r"), 1 if c and p_ else 0)

                right_side(0)
                pe.wait_ge(S("rk_rs"), 2 * l + 1)
                solve(7, 0, tmp(7)).then_inc(S("rk_u"), 1)
                pe.wait_ge(S("rk_us"), 2 * l + 1)
                for c in range(2):
                    mm(ps[:, 5, P * c:P * c + P], tmp(6)[:, P * c:P * c + P], tmp(5)[:, P * c:P * c + P], stop=False)
                    mm(ps[:, 5, P * c:P * c + P], tmp(6)[:, 256 + P * c:256 + P * c + P], tmp(4)[:, P * c:P * c + P], start=False).then_inc(S("state"), 1 if c else 0)
                pe.wait_ge(S("state_bd"), 3 * l + 3)
                right_side(1)
                pe.wait_ge(S("rk_rs"), 2 * l + 2)
                solve(7, 1, tmp(7)).then_inc(S("rk_u"), 1)
                pe.wait_ge(S("rk_us"), 2 * l + 2)
                outputs(0, [(tmp(5), mt(2)), (tmp(4), PT[:, 0:1024])], tmp(3)[:, 0:256], pt(B_V)).then_inc(S("rk_o"), 1)
                pe.wait_ge(S("rk_y"), l + 1)
                mm(ps[:, 1, :], bdones, tmp(0)).then_inc(S("rk_mean"), 1)
                mm(ps[:, 3, :], bdones, K_B).then_inc(S("rk_bonus"), 1)
                pe.wait_ge(S("rk_ysq"), l + 1)
                mm(ps[:, 2, :], bdones, tmp(1)).then_inc(S("rk_var"), 1)

            def attention(l):
                cm_phase(first_chunk["xattn_wk", l], 4, memT)
                pe.wait_ge(S("x_done"), 6 * l + 2)
                pe.wait_ge(S("cm_free"), cmi[0])
                norm(2 + 3 * l)
                tm_phase(first_chunk["xattn_wv", l], memT)
                cm_phase(first_chunk["xattn_wq", l], 4, hT)
                pe.wait_ge(S("at_v"), 4 * (l + 1))
                pe.wait_ge(S("cm_free"), cmi[0])
                for b in range(4):
                    for u in range(2):
                        t, h = b // 2, 2 * (b % 2) + u
                        for k in range(2):
                            mm(ps[:, b, 256 * u:256 * u + 256], qT[:, 2 * h + k, P * t:P * t + P], kT[:, 2 * h + k, :],
                               start=k == 0, stop=k == 1).then_inc(S("at_s"), 1 if u and k else 0)
                for b in range(4):
                    t, m = b // 2, b % 2
                    pe.wait_ge(S("at_p"), 8 * l + 4 * (t + 1))
                    for h in range(NH):
                        tr(ps[:, 4 + b, P * h:P * h + P], pr[:, t, h, P * m:P * m + P]).then_inc(S("at_tr"), 1 if h == 3 else 0)
                pe.wait_ge(S("at_prT"), 4 * (l + 1))
                for h in range(NH):
                    for k in range(2):
                        for m in range(2):
                            mm(ps[:, h, 256 * k:256 * k + 256], vA[:, m, 256 * h + P * k:256 * h + P * k + P], prT[:, m, h, :],
                               start=m == 0, stop=m == 1).then_inc(S("at_o"), 1 if k and m else 0)
                pe.wait_ge(S("at_lo"), 4 * (l + 1))
                tm_phase(first_chunk["xattn_wo", l], yT)

            def swiglu():
                pe.wait_ge(S("x_done"), 4)
                norm(3)
                for j in range(FSTEPS + 1):
                    if j < FSTEPS:
                        if j >= 2:
                            pe.wait_ge(S("ff_prod"), j - 1)
                        cm_product(ff_chunk(j), hT, 2 * (j % 2))
                        cm_product(ff_chunk(j) + 1, hT, 2 * (j % 2) + 1)
                    if j:
                        pe.wait_ge(S("ff_lo"), j)
                        av = [v.rearrange("p (k n) -> p k n", k=2) for v in actT[(j - 1) % 2]]
                        tm_product(ff_down(j - 1), lambda b_, kk, t: av[b_][:, kk, P * t:P * t + P], j == 1, j == FSTEPS)

            def experts():
                pe.wait_ge(S("x_done"), 10)
                norm(6)
                small_product(0, 2).then_inc(S("rt_mm"), 1)
                small_turn(1, 2).then_inc(S("rt_mm"), 1)
                pe.wait_ge(S("rt_d"), 2)
                sel = col(ST_SEL, 16).rearrange("p (t n) -> p t n", t=2)
                mm(ps[:, 1, 0:8], strict, sel[:, 0, :])
                mm(ps[:, 1, 8:16], ones, sel[:, 0, :], stop=False)
                mm(ps[:, 1, 8:16], strict, sel[:, 1, :], start=False)
                mm(ps[:, 1, 16:24], ones, sel[:, 0, :], stop=False)
                mm(ps[:, 1, 16:24], ones, sel[:, 1, :], start=False).then_inc(S("rt_mm"), 1)

                def prime():
                    pe.wait_ge(S("ex_add"), 1)
                    for hf in range(2):
                        ins = mm(ps[:, 4 + hf, :], onehT[:, 0:P], yE[:, 512 * hf:512 * hf + 512])
                    ins.then_inc(S("ex_tr"), 1)

                def product(s, q, bank):
                    pe.wait_ge(S("w_lo"), ex_count(s, q))
                    wp = [chunk_view(v[ex_slot(q)][:, :], "cm") for v in (whi, wlo)]
                    for i, (a_, b_) in enumerate(PASSES):
                        for k in range(KT):
                            ins = pe.matmul(ps[:, bank, 0:256], hE[b_][:, k, :], wp[a_][:, k, :], start=i == 0 and k == 0,
                                            stop=i == 2 and k == KT - 1)
                    ins.then_inc(S("chunk_done"), 1)

                def gate_up(s, s3, q):
                    pe.wait_ge(S("ex_prod"), s + 1)
                    product(s3, q, 0)
                    product(s3, q + 1, 1)

                def turn(s):
                    pe.wait_ge(S("ex_prod"), s + 2)
                    pe.wait_ge(S("ex_alo"), s + 1)
                    for k in range(2):
                        ins = pe.transpose(ps[:, 2, P * k:P * k + P], mt(1)[:, P * k:P * k + P], ident)
                    ins.then_inc(S("ex_tr"), 1)

                def down(s, s3, q, start):
                    pe.wait_ge(S("ex_alo"), s + 2)
                    pe.wait_ge(S("w_lo"), ex_count(s3, q))
                    wp = [chunk_view(v[ex_slot(q)][:, :], "tm") for v in (whi, wlo)]
                    for kk in range(TM_ROWS):
                        for hf in range(2):
                            for i, (a_, b_) in enumerate(PASSES):
                                ins = pe.matmul(ps[:, 4 + hf, :], actT[0][b_][:, P * kk:P * kk + P], wp[a_][:, kk, 512 * hf:512 * hf + 512],
                                                start=start and kk == 0 and i == 0, stop=True, skip_group_check=True)
                    ins.then_inc(S("chunk_done"), 1)

                def gather(p):
                    pe.wait_ge(S("ex_sel"), p * 2 + 2)
                    pe.wait_ge(S("ex_selT"), p + 1)
                    for t in range(TT):
                        ins = pe.transpose(ps[:, 3, P * t:P * t + P], onehg[:, P * t:P * t + P], ident)
                    ins.then_inc(S("ex_gt"), 1)
                    for c in range(KT):
                        for t in range(TT):
                            ins = pe.matmul(g_tokens(c), xs[:, t, P * c:P * c + P], oneh[:, P * t:P * t + P],
                                            start=t == 0, stop=t == 1)
                        if c % 4 == 3:
                            ins.then_inc(S("ex_g"), 1)

                def scatter(q, hf):
                    pe.wait_ge(S("ex_y"), q * 2 + (hf + 1))
                    if hf == 0:
                        pe.wait_ge(S("ex_selT"), q + 1)
                    for t in range(TT):
                        if hf:
                            pe.wait_ge(S("ex_x"), q * 4 + (t + 1))
                        pe.matmul(ps[:, 6 + t, :], onehT[:, P * t:P * t + P], yE[:, 512 * hf:512 * hf + 512],
                                  start=True, stop=True).then_inc(S("ex_sc"), 1)

                gather(0)
                prime()
                pe.wait_ge(S("ex_table"), 1)
                count = pe.value_load(pass_count[0:1, 0:1], min_val=NE, max_val=NE + SECONDS)
                with pe.Fori(0, NE + SECONDS) as ep:
                    which = pe.value_load(pass_expert[0:1, bass.ds(ep, 1)], min_val=0, max_val=NE)
                    with pe.If(which < NE):
                        r = ep * ESTEPS
                        pe.wait_ge(S("ex_hlo"), ep * KT + KT)
                        gate_up(r, r, 0)
                        scatter(ep, 0)
                        turn(r)
                        scatter(ep, 1)
                        gate_up(r + 1, r, 2)
                        down(r, r, 4, True)
                        pe.wait_ge(S("ex_x"), ep * 4 + 4)
                        gather(ep + 1)
                        with pe.Fori(2, ESTEPS) as j:
                            turn(r + j - 1)
                            gate_up(r + j, r + j - 1, 2)
                            down(r + j - 1, r + j - 1, 4, False)
                        turn(r + (ESTEPS - 1))
                        down(r + (ESTEPS - 1), r + (ESTEPS - 1), 2, False)
                pe.wait_ge(S("ex_hlo"), count * KT + KT)
                for hf in range(2):
                    scatter(count, hf)

            pe.wait_ge(S("tables_in"), 32)
            for l in range(DEPTH):
                norm(norm_index(l))
                cm_phase(first_chunk["w_in", l], 14, hT, after=lambda j: gates_ahead(l, j))
                gates(l)
                hgrn(l)
                deltanet(l)
                rwkv(l)
                pe.wait_ge(S("y_put"), 4 * (l + 1))
                tm_phase(first_chunk["w_out", l], yT)
                attention(l)
                if l == 0:
                    swiglu()
            experts()


BIG = ["x", "mem", "w_in", "w_out", "xattn_wq", "xattn_wk", "xattn_wv", "xattn_wo", "ffn_w_gate", "ffn_w_up",
       "ffn_w_down", "moe_router", "moe_w_gate", "moe_w_up", "moe_w_down"]


def lay_out_params(v):
    out = np.zeros((P, NPAR), np.float32)

    def put(key, a):
        at, n = PCOL[key]
        out[:, at:at + n] = a

    for layer in range(DEPTH):
        for name in ("norm_mix", "norm_xattn", "norm_ffn", "hgrn_norm", "lru_conv_b", "lru_ba", "lru_bx", "lru_lambda",
                     "rwkv_mu", "rwkv_w0", "rwkv_a0", "rwkv_k_k", "rwkv_k_a", "rwkv_r_k", "rwkv_ln_w", "rwkv_ln_b"):
            put((name, layer), v[name][layer].reshape(-1, P).T)
        for name in ("gdn_conv_w", "lru_conv_w"):
            put((name, layer), v[name][layer].reshape(-1, P).T)
        for name in ("gdn_A_log", "gdn_dt_bias"):
            put((name, layer), np.broadcast_to(v[name][layer], (P, NH)))
        put(("gdn_norm", layer), np.tile(v["gdn_norm"][layer], 2)[:, None])
        put(f"lb{layer}", v["hgrn_lb_logits"][layer].reshape(-1, P).T)
    put("rwkv_v0", v["rwkv_v0"][0].reshape(-1, P).T)
    put("mem_norm", v["mem_norm"].reshape(-1, P).T)
    return out


def lay_out_small(v):
    out = np.zeros((DEPTH, P, NSW), np.float32)
    for layer in range(DEPTH):
        for g, name in enumerate(("lru_wa", "lru_wx")):
            for n in range(4):
                a = SW_LRU + P * (2 * g + n // 2) + HD * (n % 2)
                out[layer, HD * (n % 2):HD * (n % 2) + HD, a:a + HD] = v[name][layer, n]
        out[layer, 0:64, SW_WA:SW_WA + GROUP] = v["rwkv_w2"][layer]
        out[layer, 64:128, SW_WA:SW_WA + GROUP] = v["rwkv_a2"][layer]
        out[layer, :, SW_G2:SW_G2 + GROUP] = v["rwkv_g2"][layer]
    out[1, :, SW_V1:SW_V1 + 64] = v["rwkv_v1"][0].reshape(2, P, 32).transpose(1, 0, 2).reshape(P, 64)
    out[1, 0:32, SW_V2:SW_V2 + GROUP] = v["rwkv_v2"][0]
    return out


def constant_tables():
    i = np.arange(P)
    out = np.zeros((P, NCON), np.float32)
    out[:, C_ID:C_ID + P] = np.eye(P)
    out[:, C_INCL:C_INCL + P] = i[:, None] <= i[None]
    out[:, C_STRICT:C_STRICT + P] = i[:, None] < i[None]
    out[:, C_BD:C_BD + P] = i[:, None] // HD == i[None] // HD
    out[:, C_IOTA:C_IOTA + P] = i[None]
    level = np.zeros((2, LEVELS, P, P), np.float32)
    for v in range(LEVELS):
        h = 1 << v
        left, right = (i // h) % 2 == 0, (i // h) % 2 == 1
        m = (i[:, None] // (2 * h) == i[None] // (2 * h)) & left[:, None] & right[None]
        level[0, v], level[1, v] = m, m.T
    return out, level.transpose(2, 0, 1, 3).reshape(P, 2 * LEVELS * P)


def kernel(**inputs):
    import concourse.bacc as bacc
    from concourse.bass_utils import run_bass_kernel_spmd

    v = {k: np.asarray(a) for k, a in inputs.items()}
    nc = bacc.Bacc("TRN2", target_bir_lowering=False, num_devices=1)
    con, level = constant_tables()
    arrays = {k: np.ascontiguousarray(v[k]) for k in BIG}
    arrays["params"] = lay_out_params(v)
    arrays["small_w"] = lay_out_small(v)
    arrays["norm_final"] = np.ascontiguousarray(np.broadcast_to(v["norm_final"], (P, D)))
    arrays["consts"] = con
    arrays["level_masks"] = level.astype(mybir.dt.np(mybir.dt.bfloat16))
    aps = {k: nc.dram_tensor(f"in_{k}", a.shape, mybir.dt.from_np(a.dtype), kind="ExternalInput").ap() for k, a in arrays.items()}
    out = nc.dram_tensor("out_0", (1, SEQ, D), F32, kind="ExternalOutput").ap()
    build(nc, aps, out)
    r = run_bass_kernel_spmd(nc, [{f"in_{k}": a for k, a in arrays.items()}], core_ids=[0])
    return r.results[0]["out_0"]
```
